# Optimizing a Trainium2 kernel written in Bass

```python
import jax, jax.numpy as jnp
from jax import lax
import numpy as np

D_MODEL = 1024
BATCH = 1
SEQ = 512
DEPTH = 1

EPS = 1e-6
N_MOD = 6
CONV_WIDTH = D_MODEL
CONV_KERNEL = 31
MLSTM_HEADS = 4
MLSTM_HEAD_DIM = D_MODEL // MLSTM_HEADS
MLSTM_WIDTH = MLSTM_HEADS * MLSTM_HEAD_DIM
QK_CONV = 4
CHUNK = 64
D_FF = ((8 * D_MODEL + 3 * 256 - 1) // (3 * 256)) * 256

N_GLU = 2 * CONV_WIDTH
N_QK = 2 * MLSTM_WIDTH
N_V = MLSTM_WIDTH
N_O = MLSTM_WIDTH
N_IF = 2 * MLSTM_HEADS
N_MERGE = 2 * D_MODEL
N_IN = N_GLU + N_QK + N_V + N_O + N_IF + N_MERGE
IN_SPLITS = (N_GLU, N_GLU + N_QK, N_GLU + N_QK + N_V, N_GLU + N_QK + N_V + N_O,
             N_GLU + N_QK + N_V + N_O + N_IF)
F_BIAS_OFFSET = N_GLU + N_QK + N_V + N_O + MLSTM_HEADS


def rms_norm(x, g):
    xf = x.astype(jnp.float32)
    y = xf * lax.rsqrt(jnp.mean(xf * xf, axis=-1, keepdims=True) + EPS)
    return (y * g.astype(jnp.float32)).astype(x.dtype)

def layer_norm(x, g, b):
    xf = x.astype(jnp.float32)
    mu = jnp.mean(xf, axis=-1, keepdims=True)
    var = jnp.mean(jnp.square(xf - mu), axis=-1, keepdims=True)
    y = (xf - mu) * lax.rsqrt(var + EPS)
    return (y * g.astype(jnp.float32) + b.astype(jnp.float32)).astype(x.dtype)

def causal_depthwise_conv(x, w, b):
    k = w.shape[0]
    y = lax.conv_general_dilated(
        x, w[:, None, :].astype(x.dtype), window_strides=(1,), padding=((k - 1, 0),),
        dimension_numbers=("NWC", "WIO", "NWC"), feature_group_count=x.shape[-1])
    return y + b

def mlstm_chunkwise(q, k, v, i_pre, f_pre):
    bsz, nh, s, dh = q.shape
    nc = s // CHUNK

    def to_chunks(t):
        return jnp.moveaxis(t.reshape(t.shape[:2] + (nc, CHUNK) + t.shape[3:]), 2, 0)

    log_f = jax.nn.log_sigmoid(f_pre)
    xs = (to_chunks(q), to_chunks(k), to_chunks(v), to_chunks(i_pre), to_chunks(log_f))
    causal = jnp.tril(jnp.ones((CHUNK, CHUNK), dtype=bool))

    def step(carry, inp):
        c_st, n_st, m_st = carry
        qc, kc, vc, ic, lfc = inp
        b = jnp.cumsum(lfc, axis=-1)
        d_log = jnp.where(causal, b[..., :, None] - b[..., None, :] + ic[..., None, :], -jnp.inf)
        inter_log = b + m_st[..., None]
        m_t = jnp.maximum(inter_log, jnp.max(d_log, axis=-1))
        dmat = jnp.exp(d_log - m_t[..., None])
        inter_w = jnp.exp(inter_log - m_t)
        sc = jnp.einsum("bhtd,bhsd->bhts", qc, kc) * dmat
        num = (jnp.einsum("bhts,bhse->bhte", sc, vc)
               + inter_w[..., None] * jnp.einsum("bhtd,bhde->bhte", qc, c_st))
        qn = jnp.sum(sc, axis=-1) + inter_w * jnp.einsum("bhtd,bhd->bht", qc, n_st)
        h = num / jnp.maximum(jnp.abs(qn), jnp.exp(-m_t))[..., None]
        b_last = b[..., -1]
        a = b_last[..., None] - b + ic
        m_new = jnp.maximum(b_last + m_st, jnp.max(a, axis=-1))
        decay = jnp.exp(b_last + m_st - m_new)
        w = jnp.exp(a - m_new[..., None])
        c_new = decay[..., None, None] * c_st + jnp.einsum("bhs,bhsd,bhse->bhde", w, kc, vc)
        n_new = decay[..., None] * n_st + jnp.einsum("bhs,bhsd->bhd", w, kc)
        return (c_new, n_new, m_new), h

    init = (jnp.zeros((bsz, nh, dh, dh), jnp.float32),
            jnp.zeros((bsz, nh, dh), jnp.float32),
            jnp.zeros((bsz, nh), jnp.float32))
    _, h = lax.scan(step, init, xs)
    return jnp.moveaxis(h, 0, 2).reshape(bsz, nh, s, dh)

def first_inputs(seed: int = 0) -> dict:
    key = jax.random.key(seed)
    ks = jax.random.split(key, 24)
    f32 = jnp.float32

    def nrm(k, shape, scale):
        return jax.random.normal(k, shape, f32) * scale

    x = jax.random.normal(ks[0], (BATCH, SEQ, D_MODEL), f32)
    c = jax.random.normal(ks[1], (BATCH, D_MODEL), f32)
    w_ada = nrm(ks[2], (DEPTH, D_MODEL, N_MOD * D_MODEL), 0.5 * D_MODEL ** -0.5)
    b_ada = nrm(ks[3], (DEPTH, N_MOD * D_MODEL), 0.02)
    norm_mix_g = 1.0 + nrm(ks[4], (DEPTH, D_MODEL), 0.1)
    w_in = nrm(ks[5], (DEPTH, D_MODEL, N_IN), D_MODEL ** -0.5)
    f_bias = jnp.linspace(3.0, 6.0, MLSTM_HEADS, dtype=f32)
    b_in = nrm(ks[6], (DEPTH, N_IN), 0.02)
    b_in = b_in.at[:, F_BIAS_OFFSET:F_BIAS_OFFSET + MLSTM_HEADS].add(f_bias)
    conv_dw_w = nrm(ks[7], (DEPTH, CONV_KERNEL, CONV_WIDTH), CONV_KERNEL ** -0.5)
    conv_dw_b = nrm(ks[8], (DEPTH, CONV_WIDTH), 0.02)
    conv_ln_g = 1.0 + nrm(ks[9], (DEPTH, CONV_WIDTH), 0.1)
    conv_ln_b = nrm(ks[10], (DEPTH, CONV_WIDTH), 0.02)
    w_conv_pw = nrm(ks[11], (DEPTH, CONV_WIDTH, D_MODEL), CONV_WIDTH ** -0.5)
    b_conv_pw = nrm(ks[12], (DEPTH, D_MODEL), 0.02)
    qk_conv_w = nrm(ks[13], (DEPTH, QK_CONV, N_QK), QK_CONV ** -0.5)
    qk_conv_b = nrm(ks[14], (DEPTH, N_QK), 0.02)
    mlstm_norm_g = 1.0 + nrm(ks[15], (DEPTH, MLSTM_WIDTH), 0.1)
    w_out = nrm(ks[16], (DEPTH, D_MODEL, D_MODEL), D_MODEL ** -0.5)
    norm_ffn_g = 1.0 + nrm(ks[17], (DEPTH, D_MODEL), 0.1)
    w_ffn_up = nrm(ks[18], (DEPTH, D_MODEL, 2 * D_FF), D_MODEL ** -0.5)
    w_ffn_down = nrm(ks[19], (DEPTH, D_FF, D_MODEL), D_FF ** -0.5)
    final_norm_g = 1.0 + nrm(ks[20], (D_MODEL,), 0.1)
    return {"x": x, "c": c, "w_ada": w_ada, "b_ada": b_ada, "norm_mix_g": norm_mix_g,
            "w_in": w_in, "b_in": b_in, "conv_dw_w": conv_dw_w, "conv_dw_b": conv_dw_b,
            "conv_ln_g": conv_ln_g, "conv_ln_b": conv_ln_b, "w_conv_pw": w_conv_pw,
            "b_conv_pw": b_conv_pw, "qk_conv_w": qk_conv_w, "qk_conv_b": qk_conv_b,
            "mlstm_norm_g": mlstm_norm_g, "w_out": w_out, "norm_ffn_g": norm_ffn_g,
            "w_ffn_up": w_ffn_up, "w_ffn_down": w_ffn_down, "final_norm_g": final_norm_g}

def first_block(x, c, w_ada, b_ada, norm_mix_g, w_in, b_in, conv_dw_w, conv_dw_b,
              conv_ln_g, conv_ln_b, w_conv_pw, b_conv_pw, qk_conv_w, qk_conv_b,
              mlstm_norm_g, w_out, norm_ffn_g, w_ffn_up, w_ffn_down, final_norm_g):
    bsz, s, _ = x.shape
    for l in range(DEPTH):
        mod = jnp.einsum("bd,de->be", jax.nn.silu(c), w_ada[l]) + b_ada[l]
        sh1, sc1, g1, sh2, sc2, g2 = jnp.split(mod[:, None, :], N_MOD, axis=-1)

        h = rms_norm(x, norm_mix_g[l]) * (1.0 + sc1) + sh1
        proj = jnp.einsum("bsd,de->bse", h, w_in[l]) + b_in[l]
        glu_in, qk_in, v, o_pre, if_pre, merge_pre = jnp.split(proj, IN_SPLITS, axis=-1)

        a = glu_in[..., :CONV_WIDTH] * jax.nn.sigmoid(glu_in[..., CONV_WIDTH:])
        a = causal_depthwise_conv(a, conv_dw_w[l], conv_dw_b[l])
        a = jax.nn.silu(layer_norm(a, conv_ln_g[l], conv_ln_b[l]))
        y_conv = jnp.einsum("bsc,cd->bsd", a, w_conv_pw[l]) + b_conv_pw[l]

        qk = jax.nn.silu(causal_depthwise_conv(qk_in, qk_conv_w[l], qk_conv_b[l]))
        q, k = jnp.split(qk, 2, axis=-1)

        def heads(t):
            return t.reshape(bsz, s, MLSTM_HEADS, MLSTM_HEAD_DIM).transpose(0, 2, 1, 3).astype(jnp.float32)

        gates = jnp.moveaxis(if_pre, -1, 1).astype(jnp.float32)
        hm = mlstm_chunkwise(heads(q), heads(k) * (MLSTM_HEAD_DIM ** -0.5), heads(v),
                             gates[:, :MLSTM_HEADS], gates[:, MLSTM_HEADS:])
        mu = jnp.mean(hm, axis=-1, keepdims=True)
        var = jnp.mean(jnp.square(hm - mu), axis=-1, keepdims=True)
        hm = ((hm - mu) * lax.rsqrt(var + EPS)).transpose(0, 2, 1, 3).reshape(bsz, s, MLSTM_WIDTH)
        hm = (hm * mlstm_norm_g[l].astype(jnp.float32)).astype(x.dtype)
        y_mlstm = jax.nn.sigmoid(o_pre) * hm

        g_conv, g_mlstm = jnp.split(jax.nn.sigmoid(merge_pre), 2, axis=-1)
        y = jnp.einsum("bsd,de->bse", g_conv * y_conv + g_mlstm * y_mlstm, w_out[l])
        x = x + g1 * y

        h = rms_norm(x, norm_ffn_g[l]) * (1.0 + sc2) + sh2
        gt, up = jnp.split(jnp.einsum("bsd,df->bsf", h, w_ffn_up[l]), 2, axis=-1)
        x = x + g2 * jnp.einsum("bsf,fd->bsd", jax.nn.silu(gt) * up, w_ffn_down[l])
    return rms_norm(x, final_norm_g)


DEPTH_2 = 2

N_MIXERS = 3
BLOCK = 128
ROPE_THETA = 500000.0
ROPE_FRAC = 4
NEG_INF = -1e30

A_HEADS = 8
A_QK_DIM = 128
A_ROPE_DIM = A_QK_DIM // ROPE_FRAC
A_NOPE_DIM = A_QK_DIM - A_ROPE_DIM
A_V_DIM = 128
A_KV_RANK = 256
IDX_HEADS = 16
IDX_DIM = 64
TOPK_MAX = 256

B_HEADS = 16
B_KV_HEADS = 4
B_HEAD_DIM = 64
B_WINDOW = 128

C_HEADS = 8
C_HEAD_DIM = 128
C_BRANCHES = ((128, 1), (512, 4), (2048, 16))

MEM_LEN = 256
MEM_HEADS = 4
MEM_HEAD_DIM = 64
MEM_WIDTH = MEM_HEADS * MEM_HEAD_DIM

D_FF_2 = 2816
CONV_WIDTH_2 = 3

MIX_WIDTH = 1024
OUT_IN = MIX_WIDTH + MEM_WIDTH
A_SPLITS = (A_HEADS * A_QK_DIM, A_KV_RANK, A_ROPE_DIM, IDX_HEADS * IDX_DIM, IDX_DIM, IDX_HEADS, MEM_WIDTH)
B_SPLITS = (B_HEADS * B_HEAD_DIM, B_KV_HEADS * B_HEAD_DIM, B_KV_HEADS * B_HEAD_DIM, MEM_WIDTH)
C_SPLITS = (C_HEADS * C_HEAD_DIM, C_HEADS * C_HEAD_DIM, C_HEADS * C_HEAD_DIM, MEM_WIDTH)
N_A = len(range(0, DEPTH_2, N_MIXERS))
N_B = len(range(1, DEPTH_2, N_MIXERS))
N_C = len(range(2, DEPTH_2, N_MIXERS))


def rmsnorm(x, g):
    xf = x.astype(jnp.float32)
    y = xf * lax.rsqrt(jnp.mean(xf * xf, axis=-1, keepdims=True) + EPS)
    return (y * g.astype(jnp.float32)).astype(x.dtype)

def split_cols(t, sizes):
    return jnp.split(t, np.cumsum(sizes)[:-1].tolist(), axis=-1)

def rope_tables(positions, rot_dim):
    inv = ROPE_THETA ** (-jnp.arange(0, rot_dim, 2, dtype=jnp.float32) / rot_dim)
    ang = positions.astype(jnp.float32)[..., None] * inv
    return jnp.cos(ang), jnp.sin(ang)

def apply_partial_rope(x, cos, sin):
    half = cos.shape[-1]
    rot = 2 * half
    xf = x[..., :rot].astype(jnp.float32)
    x1, x2 = xf[..., :half], xf[..., half:]
    c, s = cos[:, :, None, :], sin[:, :, None, :]
    xr = jnp.concatenate([x1 * c - x2 * s, x2 * c + x1 * s], axis=-1).astype(x.dtype)
    return jnp.concatenate([xr, x[..., rot:]], axis=-1)

def banded_window_attention(q, k, v, max_dist, scale, sink=None):
    B, n = q.shape[0], q.shape[1]
    nb = -(-n // BLOCK)
    pad = nb * BLOCK - n
    if pad:
        q = jnp.pad(q, ((0, 0), (0, pad), (0, 0), (0, 0), (0, 0)))
        k = jnp.pad(k, ((0, 0), (0, pad), (0, 0), (0, 0)))
        v = jnp.pad(v, ((0, 0), (0, pad), (0, 0), (0, 0)))
    qb = q.reshape(B, nb, BLOCK, *q.shape[2:])
    kb = k.reshape(B, nb, BLOCK, *k.shape[2:])
    vb = v.reshape(B, nb, BLOCK, *v.shape[2:])
    prev = ((0, 0), (1, 0), (0, 0), (0, 0), (0, 0))
    kk = jnp.concatenate([jnp.pad(kb[:, :-1], prev), kb], axis=2)
    vv = jnp.concatenate([jnp.pad(vb[:, :-1], prev), vb], axis=2)
    s = jnp.einsum('bnqhgd,bnkhd->bnhgqk', qb, kk).astype(jnp.float32) * scale
    qi = jnp.arange(BLOCK)[:, None]
    kj = jnp.arange(2 * BLOCK)[None, :]
    dist = BLOCK + qi - kj
    band = (dist >= 0) & (dist <= max_dist)
    blk = jnp.arange(nb)[:, None, None]
    mask = band[None] & ((blk > 0) | (kj >= BLOCK)[None])
    s = jnp.where(mask[None, :, None, None], s, NEG_INF)
    m = jnp.max(s, axis=-1)
    if sink is not None:
        sk = sink.astype(jnp.float32)[None, None, :, :, None]
        m = jnp.maximum(m, sk)
    p = jnp.exp(s - m[..., None])
    l = jnp.sum(p, axis=-1)
    if sink is not None:
        l = l + jnp.exp(sk - m)
    p = p / l[..., None]
    o = jnp.einsum('bnhgqk,bnkhd->bnqhgd', p, vv.astype(jnp.float32))
    o = o.reshape(B, nb * BLOCK, *o.shape[3:])[:, :n].astype(q.dtype)
    lse = (m + jnp.log(l)).transpose(0, 1, 4, 2, 3)
    lse = lse.reshape(B, nb * BLOCK, *lse.shape[3:])[:, :n]
    return o, lse

def dsa_attention(q_nope, q_rope, c_kv, k_rope, q_idx, k_idx, w_idx, w_uk, w_uv):
    B, S = q_nope.shape[0], q_nope.shape[1]
    topk = min(TOPK_MAX, S // 4)
    nb = S // BLOCK
    scale = A_QK_DIM ** -0.5
    q_lat = jnp.einsum('bshn,rhn->bshr', q_nope, w_uk)
    key_pos = jnp.arange(S)

    def to_blocks(t):
        return t.reshape(B, nb, BLOCK, *t.shape[2:]).swapaxes(0, 1)

    def one_block(args):
        ql, qr, qi, wi, t = args
        dots = jnp.einsum('bqhd,bsd->bqhs', qi, k_idx).astype(jnp.float32)
        score = jnp.einsum('bqhs,bqh->bqs', jax.nn.relu(dots), wi.astype(jnp.float32))
        causal = key_pos[None, :] <= t[:, None]
        score = jnp.where(causal[None], score, -jnp.inf)
        _, idx = lax.top_k(score, topk)
        c_sel = jax.vmap(lambda c, i: c[i])(c_kv, idx)
        kr_sel = jax.vmap(lambda c, i: c[i])(k_rope, idx)
        s = (jnp.einsum('bqhr,bqkr->bqhk', ql, c_sel)
             + jnp.einsum('bqhe,bqke->bqhk', qr, kr_sel)).astype(jnp.float32) * scale
        valid = idx <= t[None, :, None]
        s = jnp.where(valid[:, :, None, :], s, NEG_INF)
        p = jax.nn.softmax(s, axis=-1)
        return jnp.einsum('bqhk,bqkr->bqhr', p, c_sel.astype(jnp.float32)).astype(ql.dtype)

    t_ids = jnp.arange(S).reshape(nb, BLOCK)
    o_lat = lax.map(one_block, (to_blocks(q_lat), to_blocks(q_rope), to_blocks(q_idx), to_blocks(w_idx), t_ids))
    o_lat = o_lat.swapaxes(0, 1).reshape(B, S, A_HEADS, A_KV_RANK)
    return jnp.einsum('bshr,rhv->bshv', o_lat, w_uv)

def mixer_a(h, cos32, sin32, cos16, sin16, w_in, kv_norm, w_uk, w_uv):
    B, S, _ = h.shape
    q, c_kv, k_rope, q_idx, k_idx, w_idx, q_mem = split_cols(h @ w_in, A_SPLITS)
    q = apply_partial_rope(q.reshape(B, S, A_HEADS, A_QK_DIM), cos32, sin32)
    q_rope, q_nope = q[..., :A_ROPE_DIM], q[..., A_ROPE_DIM:]
    k_rope = apply_partial_rope(k_rope[:, :, None, :], cos32, sin32)[:, :, 0]
    c_kv = rmsnorm(c_kv, kv_norm)
    q_idx = apply_partial_rope(q_idx.reshape(B, S, IDX_HEADS, IDX_DIM), cos16, sin16)
    k_idx = apply_partial_rope(k_idx[:, :, None, :], cos16, sin16)[:, :, 0]
    w_idx = w_idx * (IDX_HEADS * IDX_DIM) ** -0.5
    o = dsa_attention(q_nope, q_rope, c_kv, k_rope, q_idx, k_idx, w_idx, w_uk, w_uv)
    return o.reshape(B, S, A_HEADS * A_V_DIM), q_mem

def mixer_b(h, cos16, sin16, w_in, sinks):
    B, S, _ = h.shape
    q, k, v, q_mem = split_cols(h @ w_in, B_SPLITS)
    group = B_HEADS // B_KV_HEADS
    q = apply_partial_rope(q.reshape(B, S, B_HEADS, B_HEAD_DIM), cos16, sin16)
    k = apply_partial_rope(k.reshape(B, S, B_KV_HEADS, B_HEAD_DIM), cos16, sin16)
    v = v.reshape(B, S, B_KV_HEADS, B_HEAD_DIM)
    q = q.reshape(B, S, B_KV_HEADS, group, B_HEAD_DIM)
    o, _ = banded_window_attention(q, k, v, B_WINDOW - 1, B_HEAD_DIM ** -0.5,
                                   sink=sinks.reshape(B_KV_HEADS, group))
    return o.reshape(B, S, B_HEADS * B_HEAD_DIM), q_mem

def dilate(t, d):
    B, S = t.shape[0], t.shape[1]
    return t.reshape(B, S // d, d, *t.shape[2:]).swapaxes(1, 2).reshape(B * d, S // d, *t.shape[2:])

def undilate(t, d, B):
    n = t.shape[1]
    return t.reshape(B, d, n, *t.shape[2:]).swapaxes(1, 2).reshape(B, n * d, *t.shape[2:])

def mixer_c(h, cos32, sin32, w_in):
    B, S, _ = h.shape
    q, k, v, q_mem = split_cols(h @ w_in, C_SPLITS)
    q = apply_partial_rope(q.reshape(B, S, C_HEADS, C_HEAD_DIM), cos32, sin32)
    k = apply_partial_rope(k.reshape(B, S, C_HEADS, C_HEAD_DIM), cos32, sin32)
    v = v.reshape(B, S, C_HEADS, C_HEAD_DIM)
    outs, lses = [], []
    for window, d in C_BRANCHES:
        o_g, lse_g = banded_window_attention(dilate(q, d)[:, :, :, None], dilate(k, d), dilate(v, d),
                                             window // d, C_HEAD_DIM ** -0.5)
        outs.append(undilate(o_g[:, :, :, 0], d, B))
        lses.append(undilate(lse_g[..., 0], d, B))
    alpha = jax.nn.softmax(jnp.stack(lses), axis=0)
    o = jnp.sum(alpha[..., None] * jnp.stack(outs).astype(jnp.float32), axis=0).astype(h.dtype)
    return o.reshape(B, S, C_HEADS * C_HEAD_DIM), q_mem

def memory_cross_attention(q_mem, mem_n, w_mem_kv):
    B, S, _ = q_mem.shape
    k, v = jnp.split(mem_n @ w_mem_kv, 2, axis=-1)
    k = k.reshape(B, -1, MEM_HEADS, MEM_HEAD_DIM)
    v = v.reshape(B, -1, MEM_HEADS, MEM_HEAD_DIM)
    q = q_mem.reshape(B, S, MEM_HEADS, MEM_HEAD_DIM)
    s = jnp.einsum('bshd,bmhd->bhsm', q, k).astype(jnp.float32) * MEM_HEAD_DIM ** -0.5
    p = jax.nn.softmax(s, axis=-1)
    o = jnp.einsum('bhsm,bmhd->bshd', p, v.astype(jnp.float32)).astype(q_mem.dtype)
    return o.reshape(B, S, MEM_WIDTH)

def conv_glu_ffn(h, w_up, conv_w, conv_b, w_down):
    S = h.shape[1]
    a, b = jnp.split(h @ w_up, 2, axis=-1)
    a_pad = jnp.pad(a, ((0, 0), (CONV_WIDTH_2 - 1, 0), (0, 0)))
    a = sum(conv_w[j] * a_pad[:, j:j + S] for j in range(CONV_WIDTH_2)) + conv_b
    return (jax.nn.silu(a) * b) @ w_down

def second_inputs(seed: int = 0) -> dict:
    key = jax.random.key(seed)
    ks = iter(jax.random.split(key, 40))

    def w(shape, fan_in):
        return jax.random.normal(next(ks), shape, jnp.float32) * fan_in ** -0.5

    def gain(shape):
        return 1.0 + 0.02 * jax.random.normal(next(ks), shape, jnp.float32)

    x = jax.random.normal(next(ks), (BATCH, SEQ, D_MODEL), jnp.float32)
    mem = jax.random.normal(next(ks), (BATCH, MEM_LEN, D_MODEL), jnp.float32)
    offset = jax.random.randint(next(ks), (BATCH, 1), 0, 4096, dtype=jnp.int32)
    positions = offset + jnp.arange(SEQ, dtype=jnp.int32)[None, :]
    return {
        'x': x, 'mem': mem, 'positions': positions,
        'g_mix': gain((DEPTH_2, D_MODEL)), 'g_ffn': gain((DEPTH_2, D_MODEL)),
        'g_mem': gain((D_MODEL,)), 'g_final': gain((D_MODEL,)),
        'w_mem_kv': w((DEPTH_2, D_MODEL, 2 * MEM_WIDTH), D_MODEL),
        'a_w_in': w((N_A, D_MODEL, sum(A_SPLITS)), D_MODEL),
        'a_kv_norm': gain((N_A, A_KV_RANK)),
        'a_w_uk': w((N_A, A_KV_RANK, A_HEADS, A_NOPE_DIM), A_KV_RANK),
        'a_w_uv': w((N_A, A_KV_RANK, A_HEADS, A_V_DIM), A_KV_RANK),
        'a_w_out': w((N_A, OUT_IN, D_MODEL), OUT_IN),
        'b_w_in': w((N_B, D_MODEL, sum(B_SPLITS)), D_MODEL),
        'b_sinks': 0.5 * jax.random.normal(next(ks), (N_B, B_HEADS), jnp.float32),
        'b_w_out': w((N_B, OUT_IN, D_MODEL), OUT_IN),
        'c_w_in': w((N_C, D_MODEL, sum(C_SPLITS)), D_MODEL),
        'c_w_out': w((N_C, OUT_IN, D_MODEL), OUT_IN),
        'f_w_up': w((DEPTH_2, D_MODEL, 2 * D_FF_2), D_MODEL),
        'f_conv_w': w((DEPTH_2, CONV_WIDTH_2, D_FF_2), CONV_WIDTH_2),
        'f_conv_b': 0.02 * jax.random.normal(next(ks), (DEPTH_2, D_FF_2), jnp.float32),
        'f_w_down': w((DEPTH_2, D_FF_2, D_MODEL), D_FF_2),
    }

def second_block(x, mem, positions, g_mix, g_ffn, g_mem, g_final, w_mem_kv,
              a_w_in, a_kv_norm, a_w_uk, a_w_uv, a_w_out,
              b_w_in, b_sinks, b_w_out, c_w_in, c_w_out,
              f_w_up, f_conv_w, f_conv_b, f_w_down):
    cos32, sin32 = rope_tables(positions, A_QK_DIM // ROPE_FRAC)
    cos16, sin16 = rope_tables(positions, B_HEAD_DIM // ROPE_FRAC)
    mem_n = rmsnorm(mem, g_mem)
    for i in range(DEPTH_2):
        kind, j = i % N_MIXERS, i // N_MIXERS
        h = rmsnorm(x, g_mix[i])
        if kind == 0:
            mix, q_mem = mixer_a(h, cos32, sin32, cos16, sin16, a_w_in[j], a_kv_norm[j], a_w_uk[j], a_w_uv[j])
            w_out = a_w_out[j]
        elif kind == 1:
            mix, q_mem = mixer_b(h, cos16, sin16, b_w_in[j], b_sinks[j])
            w_out = b_w_out[j]
        else:
            mix, q_mem = mixer_c(h, cos32, sin32, c_w_in[j])
            w_out = c_w_out[j]
        mem_o = memory_cross_attention(q_mem, mem_n, w_mem_kv[i])
        x = x + jnp.concatenate([mix, mem_o], axis=-1) @ w_out
        x = x + conv_glu_ffn(rmsnorm(x, g_ffn[i]), f_w_up[i], f_conv_w[i], f_conv_b[i], f_w_down[i])
    return rmsnorm(x, g_final)


def setup_inputs(seed=0):
    out = dict(first_inputs(seed))
    for name, value in second_inputs(seed + 1).items():
        if name != "x":
            out[name + "_2"] = value
    return out


def reference(
    x, c, w_ada, b_ada, norm_mix_g, w_in, b_in, conv_dw_w, conv_dw_b, conv_ln_g, conv_ln_b,
    w_conv_pw, b_conv_pw, qk_conv_w, qk_conv_b, mlstm_norm_g, w_out, norm_ffn_g, w_ffn_up,
    w_ffn_down, final_norm_g, mem_2, positions_2, g_mix_2, g_ffn_2, g_mem_2, g_final_2,
    w_mem_kv_2, a_w_in_2, a_kv_norm_2, a_w_uk_2, a_w_uv_2, a_w_out_2, b_w_in_2, b_sinks_2,
    b_w_out_2, c_w_in_2, c_w_out_2, f_w_up_2, f_conv_w_2, f_conv_b_2, f_w_down_2,
):
    x = first_block(
        x, c, w_ada, b_ada, norm_mix_g, w_in, b_in, conv_dw_w, conv_dw_b, conv_ln_g, conv_ln_b,
        w_conv_pw, b_conv_pw, qk_conv_w, qk_conv_b, mlstm_norm_g, w_out, norm_ffn_g, w_ffn_up,
        w_ffn_down, final_norm_g,
    )
    return second_block(
        x, mem_2, positions_2, g_mix_2, g_ffn_2, g_mem_2, g_final_2, w_mem_kv_2, a_w_in_2,
        a_kv_norm_2, a_w_uk_2, a_w_uv_2, a_w_out_2, b_w_in_2, b_sinks_2, b_w_out_2, c_w_in_2,
        c_w_out_2, f_w_up_2, f_conv_w_2, f_conv_b_2, f_w_down_2,
    )


_drawn_inputs = setup_inputs


def setup_inputs(seed=0):
    import zlib

    import numpy as np

    out = dict(_drawn_inputs(seed))
    spreads = {}
    factors = {'conv_dw_b': 5.385,
     'conv_ln_b': 8.0,
     'b_conv_pw': 5.262,
     'qk_conv_b': 8.0,
     'mlstm_norm_g': 3.018,
     'g_mem_2': 8.0,
     'g_final_2': 8.7,
     'a_kv_norm_2': 8.0,
     'b_sinks_2': 30.759,
     'f_conv_b_2': 17.639,
     'g_ffn_2': 8.0}
    for name, (base, spread) in spreads.items():
        noise = np.random.default_rng([zlib.crc32(name.encode()), seed]).standard_normal(out[name].shape)
        drawn = base * np.exp(spread * noise) if base else spread * noise
        out[name] = __import__('jax').numpy.asarray(drawn.astype(out[name].dtype))
    for name, factor in factors.items():
        out[name] = (out[name] * factor).astype(out[name].dtype)
    return out
```

```python
from contextlib import ExitStack

import concourse.bass as bass
import concourse.mybir as mybir
import numpy as np

F32 = mybir.dt.float32
I32 = mybir.dt.int32
ACT = mybir.ActivationFunctionType
ALU = mybir.AluOpType
AX = mybir.AxisListType.X

P = 128
T = 512
TB = T // P
D = 1024
DT = D // P
HEADS = 4
KW = 31
QW = 4
FF = 2816
FT = FF // P
MEM = 256
R = 256
A_HEADS = 8
IDX_HEADS = 16
TOPK = 128
B_HEADS = 16
EPS = 1e-6
NEG = -1e30
OUTSIDE = -3.0e38
CHOSEN = -3.2e38
SLOT = FT * P
OUT_K = 10

STAGES = [
    ("ada_first", 8), ("glu", 8), ("qk", 8), ("gates", 2), ("v", 4), ("o", 4), ("ada_rest", 16),
    ("merge_mlstm", 4), ("conv_pw", 4), ("merge_conv", 4), ("mix_out", 4), ("ffn0_up", 22), ("ffn0_down", 8),
    ("a_mem", 2), ("a_q", 4), ("a_idx", 4), ("a_keys", 2), ("a_qmem", 1), ("a_uk", 1), ("a_uv", 1),
    ("a_out", 4), ("ffn1_up", 22), ("ffn1_down", 8),
    ("b_mem", 2), ("b_q", 4), ("b_k", 1), ("b_v", 1), ("b_qmem", 1), ("b_out", 4), ("ffn2_up", 22), ("ffn2_down", 8),
]
PIECES = {"a_uk": 2, "glu": 2, "ffn0_up": 2, "ffn1_up": 2, "ffn2_up": 2}


def job_table():
    first, loaded, n, count = {}, {}, 0, [0, 0]
    for name, jobs in STAGES:
        first[name] = n
        for j in range(jobs):
            pieces = 4 if (name, j) == ("a_keys", 0) else PIECES.get(name, 1)
            count[n % 2] += 16 * pieces
            loaded[n] = count[n % 2]
            n += 1
    return first, loaded


FIRST, LOADED = job_table()

COLUMNS = [("b_ada", 48), ("c", 8), ("norm_mix_g", 8), ("b_glu", 16), ("b_qk", 16), ("b_o", 8), ("b_merge", 16),
           ("dw_w", DT * KW), ("dw_b", 8), ("ln_g", 8), ("ln_b", 8), ("b_pw", 8), ("qk_w", 16 * QW), ("qk_b", 16),
           ("mlstm_g", 8), ("norm_ffn_g", 8), ("final_g", 8), ("g_mix", 16), ("g_ffn", 16), ("g_mem", 8),
           ("g_last", 8), ("kv_g", 2), ("fconv_w", 2 * FT * 3), ("fconv_b", 2 * FT), ("sinks", B_HEADS),
           ("b_i", 1), ("b_f", 1)]
COL, NCOL = {}, 0
for _name, _n in COLUMNS:
    COL[_name] = NCOL
    NCOL += _n

CONSTS = [("ident", P), ("rot32", P), ("rot64", P), ("dup_lo", P), ("dup_hi", P), ("one", P), ("mean_d", P), ("mean_r", P),
          ("head_row", HEADS * P), ("causal", P), ("causal_bias", P), ("after_fill", P), ("causal_t", P), ("band", 2 * P),
          ("inv32", 1), ("inv64", 1), ("eps", 1), ("zero", 1)]
CON, NCON = {}, 0
for _name, _n in CONSTS:
    CON[_name] = NCON
    NCON += _n


def constants():
    k = np.zeros((P, NCON), np.float32)
    put = lambda name, a: k[:, CON[name]:CON[name] + a.shape[1]].__setitem__(slice(0, a.shape[0]), a)
    put("ident", np.eye(P))
    for name, half, heads in (("rot32", 16, 1), ("rot64", 8, 2)):
        m = np.zeros((P, P))
        for h in range(heads):
            for j in range(half):
                m[64 * h + half + j, 64 * h + j] = -1.0
                m[64 * h + j, 64 * h + half + j] = 1.0
        put(name, m)
    for name, low in (("dup_lo", 0), ("dup_hi", 64)):
        m = np.zeros((P, P))
        m[low + np.arange(P) % 64, np.arange(P)] = 1.0
        put(name, m)
    put("one", np.ones((P, P)))
    put("mean_d", np.full((P, P), 1.0 / D))
    put("mean_r", np.full((P, P), 1.0 / R))
    put("head_row", np.repeat(np.eye(HEADS), P, axis=1))
    q, s = np.arange(P)[:, None], np.arange(P)[None, :]
    put("causal", (s <= q).astype(np.float32))
    put("causal_bias", np.where(s <= q, 0.0, NEG))
    put("after_fill", np.where(s <= q, 0.0, OUTSIDE))
    put("causal_t", (s >= q).astype(np.float32))
    band = np.concatenate([np.where(s > q, 0.0, NEG), np.where(s <= q, 0.0, NEG)], axis=1)
    put("band", band)
    for name, rot, period in (("inv32", 32, P), ("inv64", 16, 64)):
        inv = np.float32(500000.0) ** (-np.arange(0, rot, 2, dtype=np.float32) / np.float32(rot))
        col = np.zeros((P, 1), np.float32)
        for p in range(P):
            if p % period < rot:
                col[p] = inv[p % period % (rot // 2)]
        put(name, col)
    put("eps", np.full((P, 1), EPS))
    return k


TWO_PI_HI = 6.28125
TWO_PI_MID = 4058 / 2 ** 21
TWO_PI_LO = float(2 * np.pi - TWO_PI_HI - TWO_PI_MID)
ROUND = 1.5 * 2 ** 23
PI_IN = 3.1415925


class Steps:

    def __init__(self, eng, sem):
        self.eng, self.sem, self.base, self.n = eng, sem, 0, 0

    def did(self, ins):
        ins.then_inc(self.sem, 1)
        self.n += 1

    def settle(self):
        if not isinstance(self.base, int) or self.n:
            self.eng.wait_ge(self.sem, self.base + self.n)

    def loop(self, turn, per_turn):
        self.start, self.per_turn = self.n, per_turn
        self.base, self.n = turn * per_turn + self.start, 0

    def end_loop(self, turns):
        assert self.n == self.per_turn, (self.n, self.per_turn)
        self.base, self.n = 0, self.start + turns * self.per_turn


def build(nc, io):
    ctx = ExitStack()
    with ctx:
        def sb(name, shape, dt=F32):
            return ctx.enter_context(nc.sbuf_tensor(name, shape, dt))

        def sem(name):
            return ctx.enter_context(nc.semaphore(name))

        xT = sb("xT", [P, DT, T])
        hT = sb("hT", [P, DT, T])
        wslots = sb("wslots", [P, 2 * SLOT])
        cols = sb("cols", [P, NCOL])
        cons = sb("cons", [P, NCON])
        trig = sb("trig", [P, 4, T])
        rstd = sb("rstd", [P, T])
        square = sb("square", [P, 2, T])
        mod = sb("mod", [P, 6 * DT])
        modg = sb("modg", [P, 2, DT])
        silu_c = sb("silu_c", [P, DT])
        small = sb("small", [P, 128])
        ARENA = 31900
        arena = sb("arena", [P, ARENA])

        taken = [0]

        def region(*shape, at=None):
            if at is not None:
                taken[0] = at
            a = taken[0]
            n = int(np.prod(shape))
            taken[0] += n
            assert taken[0] <= ARENA, taken[0]
            v = arena[:, a:a + n]
            return v if len(shape) == 1 else v.rearrange("p (a b) -> p a b", b=shape[1])

        a_pad = region(DT, T + KW - 1, at=0)
        y_conv = arena[:, 0:DT * T].rearrange("p (a b) -> p a b", b=T)
        conv = region(DT, T)
        qk = region(16, T + QW - 1)
        v_tok = region(TB, D)
        o_gate = region(DT, T)
        probs_t = region(TB, T)
        sig = probs_t[:, 0:2, :]
        conv_acc = probs_t[:, 2:4, :]
        merge_gate = probs_t
        soft, logf = sig[0:HEADS, 0, :], sig[0:HEADS, 1, :]
        decay = region(2, T)
        tail = region(3, T)
        ones_row = tail[0:HEADS, 0, :]
        v_bias = tail[0:1, 1:3, :].rearrange("p a b -> p (a b)")
        em_all, abs_n, den = tail[:, 0, :], tail[:, 1, :], tail[:, 2, :]
        rows = region(4, T)
        cum_f, g_row, neg_m, em_row = (rows[0:HEADS, i, :] for i in range(4))
        trig_tmp = conv[:, 0:3, :]
        pos_int = conv[:, 3, :].bitcast(I32)

        hid = region(FT, T, at=0)
        up_gate = region(2, T)
        up_pad = region(2, T + 2)
        up_acc = region(2, T)

        qkr = region(18, T, at=0)
        k_heads = region(A_HEADS, T)
        v_heads = region(TB, D)
        kv_low = region(2, T)
        q_mem = region(2, T)
        k_mem = region(2, MEM)
        v_mem = region(2, MEM)
        mem_out = region(2, T)
        chosen = region(sum(P * (b + 1) for b in range(1, TB)))
        scores_left = region(T)
        relu_idx = region(3, T)
        probs = region(3, T)
        probs_turned = region(2, T)
        memT = region(DT, MEM, at=ARENA - DT * MEM)
        rot_cos, rot_sin = relu_idx[:, 0:2, :], probs[:, 0:2, :]
        chosen_at = lambda b: chosen[:, P * (b * (b + 1) // 2 - 1):P * ((b + 1) * (b + 2) // 2 - 1)]
        kw_heads = k_heads

        banks = [ctx.enter_context(nc.psum_tensor(f"bank{i}", [P, T], F32)) for i in range(8)]

        weights_in = [sem("weights_in0"), sem("weights_in1")]
        product_done = [sem("product_done0"), sem("product_done1")]
        bank_free = [sem("bank_free0"), sem("bank_free1")]
        act_steps, dve_steps, pool_steps = sem("act_steps"), sem("dve_steps"), sem("pool_steps")
        S = {n: sem(n) for n in (
            "x_in cols_in cons_in pos_in vbias_in mem_in out_written pads_zero silu_c_ready modg_ready angle_ready trig_ready "
            "square_ready square_used root_ready norm_ready sig_ready conv_acc_ready conv_acc_free qk_ready "
            "softplus_ready g_turned decay_ready g_cols_ready nm_ready em_ready merge_used o_ready "
            "spread_ready logit_ready score_ready weight_ready num_ready abs_ready head_ready mean_ready dev_ready "
            "dev_square var_ready head_root hm_ready ym_ready conv_ready "
            "ln_mean ln_dev ln_square ln_square_used ln_root ln_scaled ln_ready yconv_ready mixed_ready "
            "act_gate conv3_in conv3_ready uk_pad_zero rot_ready rot_cos_ready rot_sin_ready rope_ready k_made k_taken "
            "v_made v_taken w_idx_turned w_idx_ready idx_dots relu_ready relu_used chosen_ready dup_made dup_ready "
            "at_scores at_logits at_neg_max at_exp at_probs at_turned at_copied at_sums at_out").split()}

        def col(name, i):
            return cols[:, COL[name] + i:COL[name] + i + 1]

        def col_at(name, n, r):
            return cols[:, COL[name]:COL[name] + n].rearrange("p (a b) -> p a b", b=1)[:, r, :]

        def con(name, n=P, p=P):
            return cons[0:p, CON[name]:CON[name] + n]

        def slot(p, kc, n):
            return wslots[:, p * SLOT:p * SLOT + kc * n].rearrange("p (c n) -> p c n", n=n)

        JOBS = dict(STAGES)

        def pairs(eng, name, first=0):
            n0 = FIRST[name]
            assert JOBS[name] % 2 == 0
            with eng.Fori(first, JOBS[name] // 2) as i:
                for u in range(2):
                    yield i, u, (n0 + u) % 2, (n0 + u) // 2 + i

        def one(name, j):
            n = FIRST[name] + j
            return n % 2, n // 2

        def weights_of(name, u, i):
            n = FIRST[name] + u
            if JOBS[name] == 2:
                return LOADED[n]
            return i * (LOADED[n + 2] - LOADED[n]) + LOADED[n]

        def wait_emptied(eng, name):
            n = FIRST[name] + JOBS[name] - 1
            for m in (n - 1, n):
                eng.wait_ge(bank_free[m % 2], m // 2 + 2)

        NORMS = [("mix", DT, T), ("ffn0", DT, T), ("mem", DT, MEM), ("final0", DT, T), ("a_mix", DT, T), ("kv", 2, T),
                 ("ffn1", DT, T), ("b_mix", DT, T), ("ffn2", DT, T), ("last", DT, T)]
        TILES_BEFORE, NORM_NO = {}, {}
        for k, (name, _, _) in enumerate(NORMS):
            NORM_NO[name] = k
            TILES_BEFORE[name] = sum(t for _, t, _ in NORMS[:k])
        NORM_TILES = {name: (t, w) for name, t, w in NORMS}

        def wait_norm(eng, name):
            eng.wait_ge(S["norm_ready"], TILES_BEFORE[name] + NORM_TILES[name][0])

        def norm_act(act, name, src):
            tiles, w = NORM_TILES[name]
            for c in range(tiles):
                n = TILES_BEFORE[name] + c
                if n >= 2:
                    act.wait_ge(S["square_used"], n - 1)
                nc.scalar.activation(square[:, n % 2, 0:w], src[:, c, 0:w], ACT.Square).then_inc(S["square_ready"], 1)
            act.wait_ge(S["square_used"], TILES_BEFORE[name] + tiles)
            if TILES_BEFORE[name]:
                act.wait_ge(S["norm_ready"], TILES_BEFORE[name])
            nc.scalar.activation(rstd[:, 0:w], banks[4][:, 0:w], ACT.Sqrt, bias=con("eps", 1)).then_inc(S["root_ready"], 1)

        def norm_pe(pe, name):
            tiles, w = NORM_TILES[name]
            mean = con("mean_d") if tiles == DT else con("mean_r")
            if NORM_NO[name]:
                pe.wait_ge(S["root_ready"], NORM_NO[name])
            for c in range(tiles):
                n = TILES_BEFORE[name] + c
                pe.wait_ge(S["square_ready"], n + 1)
                nc.tensor.matmul(banks[4][:, 0:w], mean, square[:, n % 2, 0:w], start=(c == 0),
                                 stop=(c == tiles - 1)).then_inc(S["square_used"], 1)

        def norm_dve(dve, steps, name, src, dst, gain, shift=None):
            tiles, w = NORM_TILES[name]
            dve.wait_ge(S["root_ready"], NORM_NO[name] + 1)
            steps.did(nc.vector.reciprocal(rstd[:, 0:w], rstd[:, 0:w]))
            steps.settle()
            for c in range(tiles):
                ins = nc.vector.scalar_tensor_tensor(out=dst[:, c, 0:w], in0=src[:, c, 0:w], scalar=gain(c),
                                                     in1=rstd[:, 0:w], op0=ALU.mult, op1=ALU.mult)
                if shift is not None:
                    steps.did(ins)
                    steps.settle()
                    ins = nc.vector.tensor_scalar(dst[:, c, 0:w], dst[:, c, 0:w], shift(c), None, ALU.add)
                ins.then_inc(S["norm_ready"], 1)

        def a_groups():
            for hd in range(A_HEADS):
                for b in range(TB):
                    n = (b + 1) * P
                    mask = con("causal_bias") if b == 0 else chosen_at(b)
                    yield dict(b=b, n=n, scores=[(n, qkr[:, hd, b * P:(b + 1) * P], k_heads[:, hd, 0:n])], mask=mask,
                               scale=P ** -0.5, heads=[(0, n)], out=hT[:, hd, :],
                               sums=[(0, P, [(v_heads[:, j, hd * P:(hd + 1) * P], j * P) for j in range(b + 1)])])

        def mem_groups():
            for t in range(2):
                for b in range(TB):
                    half = lambda e: slice(64 * e, 64 * e + 64)
                    yield dict(b=b, n=2 * MEM, mask=None, scale=0.125, heads=[(e * MEM, MEM) for e in range(2)], out=mem_out[:, t, :],
                               scores=[(MEM, q_mem[half(e), t, b * P:(b + 1) * P], k_mem[half(e), t, :]) for e in range(2)],
                               sums=[(64 * e, 64, [(v_mem[:, m, 64 * (2 * t + e):64 * (2 * t + e + 1)], e * MEM + m * P) for m in range(2)])
                                     for e in range(2)])

        def b_groups():
            for t in range(B_HEADS // 2):
                kv = t // 2
                for b in range(TB):
                    first = max(b - 1, 0)
                    n = (b + 1 - first) * P
                    half = lambda e: slice(64 * e, 64 * e + 64)
                    mask = con("band", 2 * P) if b else con("band", 2 * P)[:, P:]
                    yield dict(b=b, n=2 * n, mask=mask, scale=0.125, heads=[(e * n, n) for e in range(2)], out=hT[:, t, :], sink=2 * t,
                               scores=[(n, qkr[half(e), t, b * P:(b + 1) * P], kw_heads[half(e), kv, first * P:(b + 1) * P])
                                       for e in range(2)],
                               sums=[(64 * e, 64, [(v_heads[:, first + j, 64 * kv:64 * kv + 64], e * n + j * P) for j in range(b + 1 - first)])
                                     for e in range(2)])

        ATTENTION = [list(a_groups()), list(mem_groups()), list(b_groups()), list(mem_groups())]
        GROUPS_BEFORE = [sum(len(g) for g in ATTENTION[:k]) for k in range(5)]
        score_bank = lambda g, e: banks[2 + 2 * (g % 2) + e]
        NSTAT = 8
        stat = lambda g, lo, n=1: small[:, 64 + NSTAT * (g % 3) + lo:64 + NSTAT * (g % 3) + lo + n]

        block = ctx.enter_context(nc.Block())

        @block.sync
        def _(sp):
            w_ada = io["w_ada"][0].rearrange("(c p) n -> p c n", p=P)
            w_in = io["w_in"][0].rearrange("(c p) n -> p c n", p=P)

            sp.dma_start(cols[:], io["columns"]).then_inc(S["cols_in"], 16)
            sp.dma_start(cons[:], io["constants"]).then_inc(S["cons_in"], 16)

            def load(name, kc, width, pieces, first=0):
                for i, u, p, use in pairs(sp, name, first):
                    sp.wait_ge(product_done[p], use)
                    for lo, hi, src in pieces:
                        sp.dma_start(slot(p, kc, width)[:, :, lo:hi], src[:, :, 2 * i + u, :]).then_inc(weights_in[p], 16)

            def cut(w, lo, hi, n):
                return w[:, :, lo:hi].rearrange("p c (j n) -> p c j n", n=n)

            def load_one(name, j, kc, width, pieces):
                p, use = one(name, j)
                sp.wait_ge(product_done[p], use)
                for lo, hi, src in pieces:
                    sp.dma_start(slot(p, kc, width)[:, :, lo:hi], src).then_inc(weights_in[p], 16)

            def load_ffn(k, w_up, w_down):
                up = w_up.rearrange("(c p) n -> p c n", p=P)
                load(f"ffn{k}_up", DT, 2 * P, [(0, P, cut(up, 0, FF, P)), (P, 2 * P, cut(up, FF, 2 * FF, P))])
                down = w_down.rearrange("(c p) n -> p c n", p=P)
                load(f"ffn{k}_down", FT, P, [(0, P, cut(down, 0, D, P))])

            ada = cut(w_ada, 0, 6 * D, 2 * P)
            for j in range(2):
                sp.dma_start(slot(j, DT, 2 * P), ada[:, :, j, :]).then_inc(weights_in[j], 16)
            load("ada_first", DT, 2 * P, [(0, 2 * P, ada)], first=1)
            load("glu", DT, 2 * P, [(0, P, cut(w_in, 0, D, P)), (P, 2 * P, cut(w_in, D, 2 * D, P))])
            load("qk", DT, 2 * P, [(0, 2 * P, cut(w_in, 2 * D, 4 * D, 2 * P))])
            for j in range(2):
                load_one("gates", j, DT, HEADS, [(0, HEADS, w_in[:, :, 6 * D + HEADS * j:6 * D + HEADS * (j + 1)])])
            load("v", DT, 2 * P, [(0, 2 * P, cut(w_in, 4 * D, 5 * D, 2 * P))])
            load("o", DT, 2 * P, [(0, 2 * P, cut(w_in, 5 * D, 6 * D, 2 * P))])
            load("ada_rest", DT, 2 * P, [(0, 2 * P, cut(w_ada, 2 * D, 6 * D, 2 * P))])
            merge0 = 6 * D + 2 * HEADS
            load("merge_mlstm", DT, 2 * P, [(0, 2 * P, cut(w_in, merge0 + D, merge0 + 2 * D, 2 * P))])
            load("conv_pw", DT, 2 * P, [(0, 2 * P, cut(io["w_conv_pw"][0].rearrange("(c p) n -> p c n", p=P), 0, D, 2 * P))])
            load("merge_conv", DT, 2 * P, [(0, 2 * P, cut(w_in, merge0, merge0 + D, 2 * P))])
            load("mix_out", DT, 2 * P, [(0, 2 * P, cut(io["w_out"][0].rearrange("(c p) n -> p c n", p=P), 0, D, 2 * P))])
            load_ffn(0, io["w_ffn_up"][0], io["w_ffn_down"][0])
            wait_emptied(sp, "mix_out")
            sp.dma_start(memT, io["mem"].rearrange("(c p) t -> p c t", p=P)).then_inc(S["mem_in"], 16)

            def load_mem(name, k):
                w = io["w_mem_kv_2"][k].rearrange("(c p) n -> p c n", p=P)
                for j in range(2):
                    load_one(name, j, DT, 2 * P, [(0, 2 * P, w[:, :, 2 * P * j:2 * P * (j + 1)])])

            w_a = io["a_w_in_2"][0].rearrange("(c p) n -> p c n", p=P)
            kv0 = D
            kr0 = kv0 + R
            iq0 = kr0 + 32
            ik0 = iq0 + IDX_HEADS * 64
            iw0 = ik0 + 64
            mq0 = iw0 + IDX_HEADS
            load_mem("a_mem", 0)
            load("a_q", DT, 2 * P, [(0, 2 * P, cut(w_a, 0, D, 2 * P))])
            load("a_idx", DT, 2 * P, [(0, 2 * P, cut(w_a, iq0, ik0, 2 * P))])
            load_one("a_keys", 0, DT, 176, [(0, 32, w_a[:, :, kr0:iq0]), (32, 48, w_a[:, :, iw0:mq0]),
                                            (48, 112, w_a[:, :, ik0:iw0]), (112, 176, w_a[:, :, ik0:iw0])])
            load_one("a_keys", 1, DT, 2 * P, [(0, 2 * P, w_a[:, :, kv0:kr0])])
            load_one("a_qmem", 0, DT, 2 * P, [(0, 2 * P, w_a[:, :, mq0:mq0 + 2 * P])])
            p, use = one("a_uk", 0)
            sp.wait_ge(S["uk_pad_zero"], 1)
            uk = io["a_w_uk_2"][0].rearrange("(c p) h n -> p c h n", p=P)
            for c in range(2):
                sp.dma_start(slot(p, 2, D).rearrange("p c (h n) -> p c h n", n=P)[:, c, :, 32:P], uk[:, c]).then_inc(weights_in[p], 16)
            load_one("a_uv", 0, 2, D, [(0, D, io["a_w_uv_2"][0].rearrange("(c p) h n -> p c (h n)", p=P))])
            out_of = lambda w: cut(w.rearrange("(c p) n -> p c n", p=P), 0, D, 2 * P)
            load("a_out", OUT_K, 2 * P, [(0, 2 * P, out_of(io["a_w_out_2"][0]))])
            load_ffn(1, io["f_w_up_2"][0], io["f_w_down_2"][0])
            load_mem("b_mem", 1)
            w_b = io["b_w_in_2"][0].rearrange("(c p) n -> p c n", p=P)
            load("b_q", DT, 2 * P, [(0, 2 * P, cut(w_b, 0, D, 2 * P))])
            for name, lo in (("b_k", D), ("b_v", D + 2 * P), ("b_qmem", D + 4 * P)):
                load_one(name, 0, DT, 2 * P, [(0, 2 * P, w_b[:, :, lo:lo + 2 * P])])
            load("b_out", OUT_K, 2 * P, [(0, 2 * P, out_of(io["b_w_out_2"][0]))])
            load_ffn(2, io["f_w_up_2"][1], io["f_w_down_2"][1])
            wait_norm(sp, "last")
            sp.dma_start(io["out"].rearrange("(c p) t -> p c t", p=P), xT[:]).then_inc(S["out_written"], 16)
            sp.wait_ge(S["out_written"], 16)

        @block.tensor
        def _(pe):
            def product(name, kc, width, rhs, tiles=2):
                for i, u, p, use in pairs(pe, name):
                    pe.wait_ge(weights_in[p], weights_of(name, u, i))
                    pe.wait_ge(bank_free[p], use + 1)
                    w = slot(p, kc, width)
                    for m in range(tiles):
                        for c in range(kc):
                            last = nc.tensor.matmul(banks[2 * p + m][:], w[:, c, m * P:(m + 1) * P], rhs(c),
                                                    start=(c == 0), stop=(c == kc - 1))
                    last.then_inc(product_done[p], 1)

            def start_one(name, j):
                p, use = one(name, j)
                pe.wait_ge(weights_in[p], LOADED[FIRST[name] + j])
                pe.wait_ge(bank_free[p], use + 1)
                return p

            def product_one(name, j, kc, sizes, rhs, width=T):
                p = start_one(name, j)
                w = slot(p, kc, sum(sizes))
                for m, n in enumerate(sizes):
                    lo = sum(sizes[:m])
                    for c in range(kc):
                        last = nc.tensor.matmul(banks[2 * p + m][0:n, 0:width], w[:, c, lo:lo + n], rhs(c),
                                                start=(c == 0), stop=(c == kc - 1))
                last.then_inc(product_done[p], 1)

            def modulation(name):
                for i, u, p, use in pairs(pe, name):
                    pe.wait_ge(weights_in[p], weights_of(name, u, i))
                    pe.wait_ge(bank_free[p], use + 1)
                    w = slot(p, DT, 2 * P)
                    for m in range(2):
                        for c in range(DT):
                            last = nc.tensor.matmul(banks[2 * p][:, m:m + 1], w[:, c, m * P:(m + 1) * P], silu_c[:, c:c + 1],
                                                    start=(c == 0), stop=(c == DT - 1))
                    last.then_inc(product_done[p], 1)

            h = lambda c: hT[:, c, :]
            hidden = lambda c: hid[:, c, :]

            pe.wait_ge(S["cons_in"], 16)
            norm_pe(pe, "mix")
            pe.wait_ge(S["silu_c_ready"], 1)
            modulation("ada_first")
            wait_norm(pe, "mix")
            product("glu", DT, 2 * P, h)
            product("qk", DT, 2 * P, h)
            for j in range(2):
                product_one("gates", j, DT, [HEADS], h)
            pe.wait_ge(S["vbias_in"], 16)
            for i, u, p, use in pairs(pe, "v"):
                pe.wait_ge(weights_in[p], weights_of("v", u, i))
                pe.wait_ge(bank_free[p], use + 1)
                w = slot(p, DT, 2 * P)
                for b in range(TB):
                    out = banks[2 * p + b // 2][:, (b % 2) * 2 * P:(b % 2 + 1) * 2 * P]
                    nc.tensor.matmul(out, con("one", p=1), v_bias.rearrange("p (j n) -> p j n", n=2 * P)[:, 2 * i + u, :],
                                     start=True, stop=False)
                    for c in range(DT):
                        last = nc.tensor.matmul(out, hT[:, c, b * P:(b + 1) * P], w[:, c, :], start=False, stop=(c == DT - 1))
                last.then_inc(product_done[p], 1)
            product("o", DT, 2 * P, h)
            wait_emptied(pe, "gates")
            for b in range(TB):
                last = nc.tensor.transpose(banks[4][:, b * HEADS:(b + 1) * HEADS], g_row[:, b * P:(b + 1) * P],
                                           con("ident", HEADS, HEADS))
            last.then_inc(S["g_turned"], 1)
            modulation("ada_rest")
            product("merge_mlstm", DT, 2 * P, h)

            wait_emptied(pe, "merge_mlstm")
            pe.wait_ge(S["conv_acc_free"], 16 + 2)
            pe.wait_ge(S["nm_ready"], 2)
            pe.wait_ge(S["em_ready"], 1)
            pe.wait_ge(S["g_cols_ready"], 1)
            for hd in range(HEADS):
                if hd:
                    pe.wait_ge(S["head_ready"], 2 * hd)
                nc.tensor.matmul(banks[4][:], con("head_row", HEADS * P, HEADS)[:, hd * P:(hd + 1) * P], neg_m,
                                 start=True, stop=True).then_inc(S["spread_ready"], 1)
                nc.tensor.matmul(banks[5][:], con("head_row", HEADS * P, HEADS)[:, hd * P:(hd + 1) * P], em_row,
                                 start=True, stop=True).then_inc(S["spread_ready"], 1)

                def scores(j):
                    n = TB * hd + j
                    if n >= 2:
                        pe.wait_ge(S["weight_ready"], n - 1)
                    for e in range(2):
                        last = nc.tensor.matmul(banks[6 + j % 2][:, 0:T - j * P],
                                                qk[:, 8 + 2 * hd + e, QW - 1 + j * P:QW - 1 + (j + 1) * P],
                                                qk[:, 2 * hd + e, QW - 1 + j * P:QW - 1 + T], start=(e == 0), stop=(e == 1))
                    last.then_inc(S["score_ready"], 1)

                def sums(j):
                    pe.wait_ge(S["weight_ready"], TB * hd + j + 1)
                    rhs = probs_t[:, j, j * P:T]
                    for e in range(2):
                        nc.tensor.matmul(banks[e][:, j * P:T], v_tok[:, j, (2 * hd + e) * P:(2 * hd + e + 1) * P], rhs,
                                         start=(j == 0), stop=(j == TB - 1))
                    last = nc.tensor.matmul(banks[2][:, j * P:T], con("one"), rhs, start=(j == 0), stop=(j == TB - 1))
                    if j == TB - 1:
                        last.then_inc(S["num_ready"], 1)

                scores(0)
                for j in range(1, TB):
                    scores(j)
                    sums(j - 1)
                sums(TB - 1)
                pe.wait_ge(S["head_ready"], 2 * hd + 2)
                for e in range(2):
                    last = nc.tensor.matmul(banks[3][:], con("mean_r"), qk[:, 2 * hd + e, QW - 1:], start=(e == 0), stop=(e == 1))
                last.then_inc(S["mean_ready"], 1)
                pe.wait_ge(S["dev_ready"], 2 * hd + 2)
                for e in range(2):
                    pe.wait_ge(S["dev_square"], 2 * hd + e + 1)
                    last = nc.tensor.matmul(banks[3][:], con("mean_r"), square[:, e, :], start=(e == 0), stop=(e == 1))
                last.then_inc(S["var_ready"], 1)

            pe.wait_ge(S["conv_ready"], DT)
            pe.wait_ge(S["head_root"], HEADS)
            for c in range(DT):
                last = nc.tensor.matmul(banks[4][:], con("mean_d"), conv[:, c, :], start=(c == 0), stop=(c == DT - 1))
            last.then_inc(S["ln_mean"], 1)
            for c in range(DT):
                pe.wait_ge(S["ln_square"], c + 1)
                nc.tensor.matmul(banks[5][:], con("mean_d"), square[:, c % 2, :], start=(c == 0),
                                 stop=(c == DT - 1)).then_inc(S["ln_square_used"], 1)
            pe.wait_ge(S["ln_ready"], DT)
            product("conv_pw", DT, 2 * P, lambda c: conv[:, c, :])
            product("merge_conv", DT, 2 * P, h)
            pe.wait_ge(S["mixed_ready"], DT)
            product("mix_out", DT, 2 * P, lambda c: y_conv[:, c, :])

            def ffn(k):
                norm_pe(pe, f"ffn{k}")
                wait_norm(pe, f"ffn{k}")
                product(f"ffn{k}_up", DT, 2 * P, h)
                wait_emptied(pe, f"ffn{k}_up")
                product(f"ffn{k}_down", FT, P, hidden, tiles=1)

            ffn(0)

            def memory_kv(name):
                product_one(name, 0, DT, [P, P], lambda c: memT[:, c, :], MEM)
                p = start_one(name, 1)
                for m in range(2):
                    for c in range(DT):
                        last = nc.tensor.matmul(banks[2 * p + m][:, 0:MEM], memT[:, c, m * P:(m + 1) * P], slot(p, DT, 2 * P)[:, c, :],
                                                start=(c == 0), stop=(c == DT - 1))
                last.then_inc(product_done[p], 1)

            def rotate(tiles, name, rows, done):
                for k, t in enumerate(tiles):
                    n = done + k
                    if n >= 2:
                        pe.wait_ge(S["rot_sin_ready"], n - 1)
                    nc.tensor.matmul(banks[4 + n % 2][0:rows, :], con(name, rows, rows), qkr[0:rows, t, :],
                                     start=True, stop=True).then_inc(S["rot_ready"], 1)

            def attend(k):
                g0, groups = GROUPS_BEFORE[k], ATTENTION[k]

                def scores(g):
                    if g0 + g >= 2:
                        pe.wait_ge(S["at_logits"], g0 + g - 1)
                    for e, (n, q, kk) in enumerate(groups[g]["scores"]):
                        last = nc.tensor.matmul(score_bank(g0 + g, e)[:, 0:n], q, kk, start=True, stop=True)
                    last.then_inc(S["at_scores"], 1)

                def turn(g):
                    pe.wait_ge(S["at_probs"], g0 + g + 1)
                    if g0 + g >= 2:
                        pe.wait_ge(S["at_copied"], g0 + g - 1)
                    for j in range(groups[g]["n"] // P):
                        last = nc.tensor.transpose(banks[6 + (g0 + g) % 2][:, j * P:(j + 1) * P],
                                                   probs[:, (g0 + g) % 3, j * P:(j + 1) * P], con("ident"))
                    last.then_inc(S["at_turned"], 1)

                def sums(g):
                    pe.wait_ge(S["at_copied"], g0 + g + 1)
                    unit, b = divmod(g0 + g, TB)
                    if b == 0 and unit >= 2:
                        pe.wait_ge(S["at_out"], unit - 1)
                    for lo, n, parts in groups[g]["sums"]:
                        for i, (v, at) in enumerate(parts):
                            last = nc.tensor.matmul(banks[unit % 2][lo:lo + n, b * P:(b + 1) * P], v,
                                                    probs_turned[:, (g0 + g) % 2, at:at + P], start=(i == 0), stop=(i == len(parts) - 1))
                    last.then_inc(S["at_sums"], 1)

                for g in range(len(groups) + 2):
                    if g < len(groups):
                        scores(g)
                    if 1 <= g <= len(groups):
                        turn(g - 1)
                    if g >= 2:
                        sums(g - 2)

            def output(name, k):
                pe.wait_ge(S["at_out"], GROUPS_BEFORE[k] // TB)
                product(name, OUT_K, 2 * P, lambda c: hT[:, c, :] if c < DT else mem_out[:, c - DT, :])

            pe.wait_ge(S["norm_ready"], TILES_BEFORE["mem"])
            norm_pe(pe, "mem")
            norm_pe(pe, "final0")
            wait_norm(pe, "mem")
            memory_kv("a_mem")
            norm_pe(pe, "a_mix")
            wait_norm(pe, "a_mix")
            product("a_q", DT, 2 * P, h)
            product("a_idx", DT, 2 * P, h)
            product_one("a_keys", 0, DT, [48, P], h)
            product_one("a_keys", 1, DT, [P, P], h)
            product_one("a_qmem", 0, DT, [P, P], h)
            wait_emptied(pe, "a_qmem")
            norm_pe(pe, "kv")
            pe.wait_ge(S["root_ready"], NORM_NO["kv"] + 1)
            rotate([8], "rot32", 32, 0)
            rotate(range(8), "rot32", 32, 1)
            rotate(range(9, 18), "rot64", 80, 9)
            wait_norm(pe, "kv")
            p = start_one("a_uk", 0)
            pe.wait_ge(S["rope_ready"], 1)
            pe.wait_ge(S["rot_sin_ready"], 18)
            for hd in range(A_HEADS):
                bank = banks[(2 * p, 2 * p + 1, 6, 7)[hd % 4]]
                if hd >= 4:
                    pe.wait_ge(S["k_taken"], hd - 3)
                for c in range(2):
                    nc.tensor.matmul(bank[:], slot(p, 2, D)[:, c, hd * P:(hd + 1) * P], kv_low[:, c, :], start=(c == 0), stop=False)
                last = nc.tensor.matmul(bank[:], con("ident", P, 32), qkr[0:32, 8, :], start=False, stop=True)
                last.then_inc(S["k_made"] if hd < A_HEADS - 1 else product_done[p], 1)
            p = start_one("a_uv", 0)
            for n in range(2 * TB):
                b, half = divmod(n, 2)
                if n >= 2:
                    pe.wait_ge(S["v_taken"], n - 1)
                for c in range(2):
                    last = nc.tensor.matmul(banks[2 * p + n % 2][:], kv_low[:, c, b * P:(b + 1) * P],
                                            slot(p, 2, D)[:, c, half * T:(half + 1) * T], start=(c == 0), stop=(c == 1))
                last.then_inc(S["v_made"] if n < 2 * TB - 1 else product_done[p], 1)
            wait_emptied(pe, "a_uv")
            for b in range(TB):
                last = nc.tensor.transpose(banks[6][:, b * IDX_HEADS:(b + 1) * IDX_HEADS], qkr[32:48, 8, b * P:(b + 1) * P],
                                           cons[32:48, CON["ident"] + 32:CON["ident"] + 48])
            last.then_inc(S["w_idx_turned"], 1)
            pe.wait_ge(S["rope_ready"], 18)
            pe.wait_ge(S["w_idx_ready"], 1)
            n = 0
            for b in range(1, TB):
                for hd in range(IDX_HEADS):
                    half = slice(64 * (hd % 2), 64 * (hd % 2) + 64)
                    if n >= 4:
                        pe.wait_ge(S["relu_ready"], n - 3)
                    nc.tensor.matmul(banks[4 + n % 4][:, 0:(b + 1) * P], qkr[half, 9 + hd // 2, b * P:(b + 1) * P],
                                     qkr[half, 17, 0:(b + 1) * P], start=True, stop=True).then_inc(S["idx_dots"], 1)
                    n += 1
            pe.wait_ge(S["relu_ready"], n)
            attend(0)
            attend(1)
            output("a_out", 2)
            ffn(1)
            memory_kv("b_mem")
            norm_pe(pe, "b_mix")
            wait_norm(pe, "b_mix")
            product("b_q", DT, 2 * P, h)
            product_one("b_k", 0, DT, [P, P], h)
            p = start_one("b_v", 0)
            for b in range(TB):
                for c in range(DT):
                    last = nc.tensor.matmul(banks[2 * p + b // 2][:, (b % 2) * 2 * P:(b % 2 + 1) * 2 * P], hT[:, c, b * P:(b + 1) * P],
                                            slot(p, DT, 2 * P)[:, c, :], start=(c == 0), stop=(c == DT - 1))
            last.then_inc(product_done[p], 1)
            product_one("b_qmem", 0, DT, [P, P], h)
            wait_emptied(pe, "b_qmem")
            pe.wait_ge(S["root_ready"], NORM_NO["b_mix"] + 1)
            rotate([8, 9], "rot64", 80, 18)
            rotate(range(8), "rot64", 80, 20)
            for kv in range(4):
                pe.wait_ge(S["rope_ready"], 18 + kv // 2 + 1)
                if kv >= 2:
                    pe.wait_ge(S["dup_ready"], kv - 1)
                nc.tensor.matmul(banks[6 + kv % 2][:], con("dup_hi" if kv % 2 else "dup_lo"), qkr[:, 8 + kv // 2, :],
                                 start=True, stop=True).then_inc(S["dup_made"], 1)
            pe.wait_ge(S["dup_ready"], 4)
            pe.wait_ge(S["rope_ready"], 28)
            attend(2)
            attend(3)
            output("b_out", 4)
            ffn(2)
            norm_pe(pe, "last")

        @block.scalar
        def _(act):
            steps = Steps(act, act_steps)
            act.dma_start(xT[:], io["x"].rearrange("(c p) t -> p c t", p=P)).then_inc(S["x_in"], 16)
            act.dma_start(pos_int, io["positions"]).then_inc(S["pos_in"], 16)
            act.wait_ge(S["pos_in"], 16)
            for p in range(2):
                act.sem_inc(bank_free[p], 1)
            act.sem_inc(S["conv_acc_free"], 2)
            act.sem_inc(S["merge_used"], 2)
            act.wait_ge(S["x_in"], 16)
            act.wait_ge(S["cons_in"], 16)
            norm_act(act, "mix", xT)
            act.wait_ge(S["cols_in"], 16)
            nc.scalar.activation(silu_c[:], cols[:, COL["c"]:COL["c"] + DT], ACT.Silu).then_inc(S["silu_c_ready"], 1)

            def mod_columns(name, first):
                m0 = first // 2
                n = JOBS[name]
                mods = mod[:, 2 * m0:2 * (m0 + n)].rearrange("p (a b) -> p a b", b=2)
                bias = cols[:, COL["b_ada"] + 2 * m0:COL["b_ada"] + 2 * (m0 + n)].rearrange("p (a b) -> p a b", b=2)
                for i, u, p, use in pairs(act, name):
                    act.wait_ge(product_done[p], use + 1)
                    nc.scalar.activation(mods[:, 2 * i + u, 0:1], banks[2 * p][:, 0:1], ACT.Identity, bias=bias[:, 2 * i + u, 0:1])
                    nc.scalar.activation(mods[:, 2 * i + u, 1:2], banks[2 * p][:, 1:2], ACT.Identity,
                                         bias=bias[:, 2 * i + u, 1:2]).then_inc(bank_free[p], 1)

            mod_columns("ada_first", 0)
            for k in range(4):
                act.wait_ge(S["angle_ready"], k + 1)
                nc.scalar.activation(trig[:, k, :], trig[:, k, :], ACT.Sin).then_inc(S["trig_ready"], 1)
            act.wait_ge(S["trig_ready"], 4)
            act.dma_start(v_bias, io["v_bias"]).then_inc(S["vbias_in"], 16)
            for i, u, p, use in pairs(act, "glu"):
                act.wait_ge(product_done[p], use + 1)
                nc.scalar.activation(sig[:, p, :], banks[2 * p + 1][:], ACT.Sigmoid,
                                     bias=col_at("b_glu", 16, 8 + 2 * i + u)).then_inc(S["sig_ready"], 1)
            act.wait_ge(S["pads_zero"], 2)
            for i, u, p, use in pairs(act, "qk"):
                act.wait_ge(product_done[p], use + 1)
                for m in range(2):
                    last = nc.scalar.activation(qk[:, 4 * i + 2 * u + m, QW - 1:], banks[2 * p + m][:], ACT.Identity,
                                                bias=col_at("b_qk", 16, 4 * i + 2 * u + m))
                last.then_inc(bank_free[p], 1)
                for m in range(2):
                    act.wait_ge(S["conv_acc_ready"], 4 * i + 2 * u + m + 1)
                    nc.scalar.activation(qk[:, 4 * i + 2 * u + m, QW - 1:], conv_acc[:, m, :], ACT.Silu,
                                         bias=col_at("qk_b", 16, 4 * i + 2 * u + m)).then_inc(S["conv_acc_free"], 1)
            p, use = one("gates", 1)
            act.wait_ge(product_done[p], use + 1)
            steps.did(nc.scalar.activation(soft, banks[2 * p][0:HEADS, :], ACT.Abs, bias=cols[0:HEADS, COL["b_f"]:COL["b_f"] + 1]))
            steps.settle()
            steps.did(nc.scalar.activation(soft, soft, ACT.Exp, scale=-1.0))
            steps.settle()
            nc.scalar.activation(soft, soft, ACT.Ln, bias=1.0).then_inc(S["softplus_ready"], 1)
            v_cut = v_tok.rearrange("p b (j n) -> p b j n", n=2 * P)
            for i, u, p, use in pairs(act, "v"):
                act.wait_ge(product_done[p], use + 1)
                for m in range(2):
                    last = nc.scalar.activation(v_cut[:, 2 * m:2 * m + 2, 2 * i + u, :],
                                                banks[2 * p + m][:].rearrange("p (b n) -> p b n", n=2 * P), ACT.Copy)
                last.then_inc(bank_free[p], 1)
            act.wait_ge(S["nm_ready"], 2)
            nc.scalar.activation(em_row, em_row, ACT.Exp).then_inc(S["em_ready"], 1)
            for i, u, p, use in pairs(act, "o"):
                act.wait_ge(product_done[p], use + 1)
                for m in range(2):
                    last = nc.scalar.activation(o_gate[:, 4 * i + 2 * u + m, :], banks[2 * p + m][:], ACT.Sigmoid,
                                                bias=col_at("b_o", 8, 4 * i + 2 * u + m))
                last.then_inc(bank_free[p], 1)
            act.wait_ge(S["g_turned"], 1)
            nc.scalar.activation(small[:, 0:TB * HEADS], banks[4][:, 0:TB * HEADS], ACT.Copy).then_inc(S["g_cols_ready"], 1)
            mod_columns("ada_rest", 16)

            def merge_gates(name, b0, earlier):
                for i, u, p, use in pairs(act, name):
                    act.wait_ge(product_done[p], use + 1)
                    act.wait_ge(S["merge_used"], 2 * i + u + 1 + earlier)
                    for m in range(2):
                        last = nc.scalar.activation(merge_gate[:, 2 * u + m, :], banks[2 * p + m][:], ACT.Sigmoid,
                                                    bias=col_at("b_merge", 16, b0 + 4 * i + 2 * u + m))
                    last.then_inc(bank_free[p], 1)

            merge_gates("merge_mlstm", 8, 0)
            gcol = lambda j, hd: small[:, j * HEADS + hd:j * HEADS + hd + 1]
            for hd in range(HEADS):
                act.wait_ge(S["spread_ready"], 2 * hd + 2)
                steps.did(nc.scalar.activation(em_all, banks[5][:], ACT.Copy))
                for j in range(TB):
                    act.wait_ge(S["logit_ready"], TB * hd + j + 1)
                    nc.scalar.activation(decay[:, j % 2, 0:T - j * P], decay[:, j % 2, 0:T - j * P],
                                         ACT.Exp).then_inc(S["decay_ready"], 1)
                act.wait_ge(S["num_ready"], hd + 1)
                steps.settle()
                nc.scalar.activation(abs_n, banks[2][:], ACT.Abs).then_inc(S["abs_ready"], 1)
                for e in range(2):
                    act.wait_ge(S["dev_ready"], 2 * hd + e + 1)
                    nc.scalar.activation(square[:, e, :], qk[:, 2 * hd + e, QW - 1:], ACT.Square).then_inc(S["dev_square"], 1)
                act.wait_ge(S["var_ready"], hd + 1)
                nc.scalar.activation(rstd[:], banks[3][:], ACT.Sqrt, bias=con("eps", 1)).then_inc(S["head_root"], 1)
            for c in range(DT):
                act.wait_ge(S["ln_dev"], c + 1)
                if c >= 2:
                    act.wait_ge(S["ln_square_used"], c - 1)
                nc.scalar.activation(square[:, c % 2, :], conv[:, c, :], ACT.Square).then_inc(S["ln_square"], 1)
            act.wait_ge(S["ln_square_used"], DT)
            act.wait_ge(S["hm_ready"], 2 * HEADS)
            nc.scalar.activation(rstd[:], banks[5][:], ACT.Sqrt, bias=con("eps", 1)).then_inc(S["ln_root"], 1)
            for c in range(DT):
                act.wait_ge(S["ln_scaled"], c + 1)
                nc.scalar.activation(conv[:, c, :], conv[:, c, :], ACT.Silu, bias=col("ln_b", c)).then_inc(S["ln_ready"], 1)
            for i, u, p, use in pairs(act, "conv_pw"):
                act.wait_ge(product_done[p], use + 1)
                for m in range(2):
                    last = nc.scalar.activation(y_conv[:, 4 * i + 2 * u + m, :], banks[2 * p + m][:], ACT.Identity,
                                                bias=col_at("b_pw", 8, 4 * i + 2 * u + m))
                last.then_inc(bank_free[p], 1)
            merge_gates("merge_conv", 0, 4)

            def ffn0():
                for i, u, p, use in pairs(act, "ffn0_up"):
                    act.wait_ge(product_done[p], use + 1)
                    nc.scalar.activation(up_gate[:, p, :], banks[2 * p][:], ACT.Silu).then_inc(S["act_gate"], 1)

            wait_emptied(act, "mix_out")
            norm_act(act, "ffn0", xT)
            ffn0()

            def out_of_banks(name, dst, tiles=2):
                for i, u, p, use in pairs(act, name):
                    act.wait_ge(product_done[p], use + 1)
                    for m in range(2):
                        last = nc.scalar.activation(dst(4 * i + 2 * u + m), banks[2 * p + m][:], ACT.Copy)
                    last.then_inc(bank_free[p], 1)

            def out_of_job(name, j, parts):
                p, use = one(name, j)
                act.wait_ge(product_done[p], use + 1)
                for dst, m, r, w in parts:
                    last = nc.scalar.activation(dst, banks[2 * p + m][0:r, 0:w], ACT.Copy)
                last.then_inc(bank_free[p], 1)

            def memory_kv(name):
                out_of_job(name, 0, [(k_mem[:, m, :], m, P, MEM) for m in range(2)])
                out_of_job(name, 1, [(v_mem[:, m, :], m, P, MEM) for m in range(2)])

            def attend(k):
                g0, groups = GROUPS_BEFORE[k], ATTENTION[k]

                def exps(g):
                    n = g0 + g
                    act.wait_ge(S["at_neg_max"], n + 1)
                    heads = groups[g]["heads"]
                    sink = groups[g].get("sink")
                    if sink is not None:
                        for e in range(2):
                            steps.did(nc.scalar.activation(stat(n, 6 + e), col("sinks", sink + e), ACT.Exp, bias=stat(n, 2 + e)))
                        steps.settle()
                    for e, (lo, w) in enumerate(heads):
                        part = probs[:, n % 3, lo:lo + w]
                        last = nc.scalar.activation(part, part, ACT.Exp, bias=stat(n, 2 + e), accum_out=stat(n, 4 + e))
                    last.then_inc(S["at_exp"], 1)

                def copies(g):
                    n = g0 + g
                    act.wait_ge(S["at_turned"], n + 1)
                    if n >= 2:
                        act.wait_ge(S["at_sums"], n - 1)
                    w = groups[g]["n"]
                    nc.scalar.activation(probs_turned[:, n % 2, 0:w], banks[6 + n % 2][:, 0:w], ACT.Copy).then_inc(S["at_copied"], 1)

                def outputs(g):
                    n = g0 + g
                    act.wait_ge(S["at_sums"], n + 1)
                    nc.scalar.activation(groups[g]["out"], banks[n // TB % 2][:], ACT.Copy).then_inc(S["at_out"], 1)

                for g in range(len(groups) + 2):
                    if g < len(groups):
                        exps(g)
                    if 1 <= g <= len(groups):
                        copies(g - 1)
                    if g >= 2 and (g - 2) % TB == TB - 1:
                        outputs(g - 2)

            def ffn_conv(k):
                for i, u, p, use in pairs(act, f"ffn{k}_up"):
                    n = FT * (k - 1) + 2 * i + u
                    act.wait_ge(product_done[p], use + 1)
                    nc.scalar.activation(up_pad[:, p, 2:], banks[2 * p][:], ACT.Copy).then_inc(S["conv3_in"], 1)
                    act.wait_ge(S["conv3_ready"], n + 1)
                    nc.scalar.activation(up_gate[:, p, :], up_acc[:, p, :], ACT.Silu).then_inc(S["act_gate"], 1)

            act.wait_ge(S["mem_in"], 16)
            norm_act(act, "mem", memT)
            wait_emptied(act, "ffn0_down")
            norm_act(act, "final0", xT)
            memory_kv("a_mem")
            act.wait_ge(S["norm_ready"], TILES_BEFORE["a_mix"])
            norm_act(act, "a_mix", xT)
            out_of_banks("a_q", lambda t: qkr[:, 0:8, :][:, t, :])
            out_of_banks("a_idx", lambda t: qkr[:, 9:17, :][:, t, :])
            out_of_job("a_keys", 0, [(qkr[0:48, 8, :], 0, 48, T), (qkr[:, 17, :], 1, P, T)])
            out_of_job("a_keys", 1, [(kv_low[:, m, :], m, P, T) for m in range(2)])
            out_of_job("a_qmem", 0, [(q_mem[:, m, :], m, P, T) for m in range(2)])
            wait_emptied(act, "a_qmem")
            norm_act(act, "kv", kv_low)
            p, use = one("a_uk", 0)
            for hd in range(A_HEADS):
                if hd < A_HEADS - 1:
                    act.wait_ge(S["k_made"], hd + 1)
                else:
                    act.wait_ge(product_done[p], use + 1)
                nc.scalar.activation(k_heads[:, hd, :], banks[(2 * p, 2 * p + 1, 6, 7)[hd % 4]][:],
                                     ACT.Copy).then_inc(S["k_taken"] if hd < A_HEADS - 1 else bank_free[p], 1)
            p, use = one("a_uv", 0)
            for n in range(2 * TB):
                b, half = divmod(n, 2)
                if n < 2 * TB - 1:
                    act.wait_ge(S["v_made"], n + 1)
                else:
                    act.wait_ge(product_done[p], use + 1)
                nc.scalar.activation(v_heads[:, b, half * T:(half + 1) * T], banks[2 * p + n % 2][:],
                                     ACT.Copy).then_inc(S["v_taken"] if n < 2 * TB - 1 else bank_free[p], 1)
            act.wait_ge(S["w_idx_turned"], 1)
            nc.scalar.activation(small[:, 0:TB * IDX_HEADS], banks[6][:, 0:TB * IDX_HEADS], ACT.Copy,
                                 scale=(IDX_HEADS * 64) ** -0.5).then_inc(S["w_idx_ready"], 1)
            n = 0
            for b in range(1, TB):
                for hd in range(IDX_HEADS):
                    act.wait_ge(S["idx_dots"], n + 1)
                    if n >= 3:
                        act.wait_ge(S["relu_used"], n - 2)
                    w = (b + 1) * P
                    nc.scalar.activation(relu_idx[:, n % 3, 0:w], banks[4 + n % 4][:, 0:w], ACT.Relu).then_inc(S["relu_ready"], 1)
                    n += 1
            attend(0)
            attend(1)
            wait_emptied(act, "a_out")
            norm_act(act, "ffn1", xT)
            act.wait_ge(S["norm_ready"], TILES_BEFORE["b_mix"])
            ffn_conv(1)
            memory_kv("b_mem")
            wait_emptied(act, "ffn1_down")
            norm_act(act, "b_mix", xT)
            out_of_banks("b_q", lambda t: qkr[:, 0:8, :][:, t, :])
            out_of_job("b_k", 0, [(qkr[:, 8 + m, :], m, P, T) for m in range(2)])
            p, use = one("b_v", 0)
            act.wait_ge(product_done[p], use + 1)
            for m in range(2):
                last = nc.scalar.activation(v_heads[:, 2 * m:2 * m + 2, 0:2 * P], banks[2 * p + m][:].rearrange("p (b n) -> p b n", b=2), ACT.Copy)
            last.then_inc(bank_free[p], 1)
            out_of_job("b_qmem", 0, [(q_mem[:, m, :], m, P, T) for m in range(2)])
            for kv in range(4):
                act.wait_ge(S["dup_made"], kv + 1)
                nc.scalar.activation(kw_heads[:, kv, :], banks[6 + kv % 2][:], ACT.Copy).then_inc(S["dup_ready"], 1)
            attend(2)
            attend(3)
            wait_emptied(act, "b_out")
            norm_act(act, "ffn2", xT)
            act.wait_ge(S["norm_ready"], TILES_BEFORE["last"])
            ffn_conv(2)
            wait_emptied(act, "ffn2_down")
            norm_act(act, "last", xT)

        @block.vector
        def _(dve):
            steps = Steps(dve, dve_steps)
            dve.wait_ge(S["pos_in"], 16)
            dve.wait_ge(S["cons_in"], 16)
            pos, ang, turns = trig_tmp[:, 0, :], trig_tmp[:, 1, :], trig_tmp[:, 2, :]
            steps.did(nc.vector.tensor_copy(pos, pos_int))
            steps.settle()
            for k in range(4):
                out, quarter = trig[:, k, :], 0.25 if k % 2 == 0 else 0.0
                steps.did(nc.vector.tensor_scalar(ang, pos, con("inv32" if k < 2 else "inv64", 1), None, ALU.mult))
                steps.settle()
                steps.did(nc.vector.tensor_scalar(turns, ang, 1 / (2 * np.pi), quarter, ALU.mult, ALU.add))
                steps.settle()
                steps.did(nc.vector.tensor_scalar(turns, turns, ROUND, ROUND, ALU.add, ALU.subtract))
                for part in (TWO_PI_HI, TWO_PI_MID, TWO_PI_LO):
                    steps.settle()
                    steps.did(nc.vector.scalar_tensor_tensor(out=ang, in0=turns, scalar=-part, in1=ang, op0=ALU.mult, op1=ALU.add))
                steps.settle()
                if k % 2 == 0:
                    steps.did(nc.vector.tensor_scalar(ang, ang, np.pi / 2, None, ALU.add))
                    steps.settle()
                nc.vector.tensor_scalar(out, ang, PI_IN, -PI_IN, ALU.min, ALU.max).then_inc(S["angle_ready"], 1)
                dve.wait_ge(S["angle_ready"], k + 1)

            def gains(k, g):
                at = (3 * k + 1) * DT
                nc.vector.scalar_tensor_tensor(out=modg[:, k, :], in0=mod[:, at:at + DT], scalar=1.0,
                                               in1=cols[:, COL[g]:COL[g] + DT], op0=ALU.add, op1=ALU.mult).then_inc(S["modg_ready"], 1)
                dve.wait_ge(S["modg_ready"], k + 1)

            wait_emptied(dve, "ada_first")
            dve.wait_ge(S["cols_in"], 16)
            gains(0, "norm_mix_g")
            norm_dve(dve, steps, "mix", xT, hT, lambda c: modg[:, 0, c:c + 1], lambda c: mod[:, c:c + 1])
            dve.wait_ge(S["pads_zero"], 2)
            for i, u, p, use in pairs(dve, "glu"):
                dve.wait_ge(S["sig_ready"], 2 * i + u + 1)
                nc.vector.scalar_tensor_tensor(out=a_pad[:, 2 * i + u, KW - 1:], in0=banks[2 * p][:], scalar=col_at("b_glu", 16, 2 * i + u),
                                               in1=sig[:, p, :], op0=ALU.add, op1=ALU.mult).then_inc(bank_free[p], 1)
            qk_w = cols[:, COL["qk_w"]:COL["qk_w"] + 16 * QW].rearrange("p (a b) -> p a b", b=QW)
            for i, u, p, use in pairs(dve, "qk"):
                if u == 0:
                    steps.loop(i, 4 * (QW - 1))
                dve.wait_ge(bank_free[p], use + 2)
                for m in range(2):
                    t = 4 * i + 2 * u + m
                    dve.wait_ge(S["conv_acc_free"], t + 1)
                    steps.did(nc.vector.tensor_scalar(conv_acc[:, m, :], qk[:, t, 0:T], qk_w[:, t, 0:1], None, ALU.mult))
                    for k in range(1, QW):
                        steps.settle()
                        ins = nc.vector.scalar_tensor_tensor(out=conv_acc[:, m, :], in0=qk[:, t, k:k + T], scalar=qk_w[:, t, k:k + 1],
                                                             in1=conv_acc[:, m, :], op0=ALU.mult, op1=ALU.add)
                        if k < QW - 1:
                            steps.did(ins)
                        else:
                            ins.then_inc(S["conv_acc_ready"], 1)
            steps.end_loop(4)
            (pi, use_i), (pf, use_f) = one("gates", 0), one("gates", 1)
            dve.wait_ge(product_done[pi], use_i + 1)
            dve.wait_ge(product_done[pf], use_f + 1)
            steps.did(nc.vector.memset(ones_row, 1.0))
            dve.wait_ge(S["softplus_ready"], 1)
            steps.did(nc.vector.tensor_scalar(logf, banks[2 * pf][0:HEADS, :], cols[0:HEADS, COL["b_f"]:COL["b_f"] + 1], 0.0,
                                              ALU.add, ALU.min))
            steps.settle()
            steps.did(nc.vector.tensor_tensor(logf, logf, soft, ALU.subtract))
            steps.settle()
            nc.vector.tensor_tensor_scan(cum_f, ones_row, logf, 0.0, ALU.mult, ALU.add).then_inc(bank_free[pf], 1)
            dve.wait_ge(bank_free[pf], use_f + 2)
            nc.vector.scalar_tensor_tensor(out=g_row, in0=banks[2 * pi][0:HEADS, :], scalar=cols[0:HEADS, COL["b_i"]:COL["b_i"] + 1],
                                           in1=cum_f, op0=ALU.add, op1=ALU.subtract).then_inc(bank_free[pi], 1)
            dve.wait_ge(bank_free[pi], use_i + 2)
            steps.did(nc.vector.tensor_tensor_scan(neg_m, g_row, g_row, 0.0, ALU.max, ALU.max))
            steps.settle()
            nc.vector.scalar_tensor_tensor(out=em_row, in0=cum_f, scalar=-1.0, in1=neg_m, op0=ALU.mult,
                                           op1=ALU.subtract).then_inc(S["nm_ready"], 1)
            nc.vector.tensor_scalar(neg_m, neg_m, -1.0, None, ALU.mult).then_inc(S["nm_ready"], 1)
            dw_w = cols[:, COL["dw_w"]:COL["dw_w"] + DT * KW].rearrange("p (a b) -> p a b", b=KW)
            wait_emptied(dve, "glu")
            with dve.Fori(0, DT) as c:
                steps.loop(c, KW - 1)
                steps.did(nc.vector.tensor_scalar(conv[:, c, :], a_pad[:, c, 0:T], dw_w[:, c, 0:1], col_at("dw_b", DT, c),
                                                  ALU.mult, ALU.add))
                for k in range(1, KW):
                    steps.settle()
                    ins = nc.vector.scalar_tensor_tensor(out=conv[:, c, :], in0=a_pad[:, c, k:k + T], scalar=dw_w[:, c, k:k + 1],
                                                         in1=conv[:, c, :], op0=ALU.mult, op1=ALU.add)
                    if k < KW - 1:
                        steps.did(ins)
                    else:
                        ins.then_inc(S["conv_ready"], 1)
            steps.end_loop(DT)

            dve.wait_ge(S["merge_used"], 4 + 2)
            dve.wait_ge(S["g_cols_ready"], 1)
            for hd in range(HEADS):
                heads_out = lambda e: qk[:, 2 * hd + e, QW - 1:]
                dve.wait_ge(S["spread_ready"], 2 * hd + 1)

                def logits(j):
                    nc.vector.tensor_scalar(decay[:, j % 2, 0:T - j * P], banks[4][:, j * P:T], small[:, j * HEADS + hd:j * HEADS + hd + 1],
                                            0.0, ALU.add, ALU.min).then_inc(S["logit_ready"], 1)

                def weights(j):
                    n = TB * hd + j
                    if hd and j == 0:
                        dve.wait_ge(S["num_ready"], hd)
                    dve.wait_ge(S["score_ready"], n + 1)
                    dve.wait_ge(S["decay_ready"], n + 1)
                    steps.did(nc.vector.scalar_tensor_tensor(out=probs_t[:, j, j * P:T], in0=banks[6 + j % 2][:, 0:T - j * P],
                                                             scalar=(2 * P) ** -0.5, in1=decay[:, j % 2, 0:T - j * P],
                                                             op0=ALU.mult, op1=ALU.mult))
                    steps.settle()
                    diagonal = probs_t[:, j, j * P:(j + 1) * P]
                    nc.vector.tensor_tensor(diagonal, diagonal, con("causal_t"), ALU.mult).then_inc(S["weight_ready"], 1)

                logits(0)
                for j in range(1, TB):
                    logits(j)
                    weights(j - 1)
                weights(TB - 1)
                dve.wait_ge(S["abs_ready"], hd + 1)
                steps.did(nc.vector.tensor_tensor(den, abs_n, em_all, ALU.max))
                steps.settle()
                steps.did(nc.vector.reciprocal(den, den))
                steps.settle()
                for e in range(2):
                    nc.vector.tensor_tensor(heads_out(e), banks[e][:], den, ALU.mult).then_inc(S["head_ready"], 1)
                dve.wait_ge(S["mean_ready"], hd + 1)
                dve.wait_ge(S["head_ready"], 2 * hd + 2)
                for e in range(2):
                    nc.vector.tensor_tensor(heads_out(e), heads_out(e), banks[3][:], ALU.subtract).then_inc(S["dev_ready"], 1)
                dve.wait_ge(S["head_root"], hd + 1)
                steps.did(nc.vector.reciprocal(rstd[:], rstd[:]))
                steps.settle()
                dve.wait_ge(S["dev_ready"], 2 * hd + 2)
                for e in range(2):
                    nc.vector.scalar_tensor_tensor(out=heads_out(e), in0=heads_out(e), scalar=col("mlstm_g", 2 * hd + e), in1=rstd[:],
                                                   op0=ALU.mult, op1=ALU.mult).then_inc(S["hm_ready"], 1)

            dve.wait_ge(S["ln_mean"], 1)
            for c in range(DT):
                nc.vector.tensor_tensor(conv[:, c, :], conv[:, c, :], banks[4][:], ALU.subtract).then_inc(S["ln_dev"], 1)
            dve.wait_ge(S["ln_root"], 1)
            steps.did(nc.vector.reciprocal(rstd[:], rstd[:]))
            steps.settle()
            dve.wait_ge(S["ln_dev"], DT)
            for c in range(DT):
                nc.vector.scalar_tensor_tensor(out=conv[:, c, :], in0=conv[:, c, :], scalar=col("ln_g", c), in1=rstd[:],
                                               op0=ALU.mult, op1=ALU.mult).then_inc(S["ln_scaled"], 1)

            def residual(name, tiles, gate=None):
                for i, u, p, use in pairs(dve, name):
                    dve.wait_ge(product_done[p], use + 1)
                    for m in range(tiles):
                        t = tiles * (2 * i + u) + m
                        if gate is None:
                            last = nc.vector.tensor_tensor(xT[:, t, :], xT[:, t, :], banks[2 * p + m][:], ALU.add)
                        else:
                            g = mod[:, gate * DT:(gate + 1) * DT].rearrange("p (a b) -> p a b", b=1)[:, t, :]
                            last = nc.vector.scalar_tensor_tensor(out=xT[:, t, :], in0=banks[2 * p + m][:], scalar=g, in1=xT[:, t, :],
                                                                  op0=ALU.mult, op1=ALU.add)
                    last.then_inc(bank_free[p], 1)

            wait_emptied(dve, "ada_rest")
            gains(1, "norm_ffn_g")
            residual("mix_out", 2, 2)
            wait_emptied(dve, "mix_out")
            norm_dve(dve, steps, "ffn0", xT, hT, lambda c: modg[:, 1, c:c + 1], lambda c: mod[:, 3 * DT + c:3 * DT + c + 1])
            for i, u, p, use in pairs(dve, "ffn0_up"):
                dve.wait_ge(S["act_gate"], 2 * i + u + 1)
                nc.vector.tensor_tensor(hid[:, 2 * i + u, :], up_gate[:, p, :], banks[2 * p + 1][:], ALU.mult).then_inc(bank_free[p], 1)
            residual("ffn0_down", 1, 5)
            norm_dve(dve, steps, "mem", memT, memT, lambda c: col("g_mem", c))
            wait_emptied(dve, "ffn0_down")
            norm_dve(dve, steps, "final0", xT, xT, lambda c: col("final_g", c))
            dve.wait_ge(S["norm_ready"], TILES_BEFORE["a_mix"])
            norm_dve(dve, steps, "a_mix", xT, hT, lambda c: col("g_mix", c))

            def rope(tiles, table, rows, done):
                for k, t in enumerate(tiles):
                    n = done + k
                    dve.wait_ge(S["rot_ready"], n + 1)
                    nc.vector.tensor_tensor(rot_sin[0:rows, n % 2, :], banks[4 + n % 2][0:rows, :], trig[0:rows, table + 1, :],
                                            ALU.mult).then_inc(S["rot_sin_ready"], 1)
                    dve.wait_ge(S["rot_sin_ready"], n + 1)
                    dve.wait_ge(S["rot_cos_ready"], n + 1)
                    nc.vector.tensor_tensor(qkr[0:rows, t, :], rot_cos[0:rows, n % 2, :], rot_sin[0:rows, n % 2, :],
                                            ALU.add).then_inc(S["rope_ready"], 1)

            def attend(k):
                g0, groups = GROUPS_BEFORE[k], ATTENTION[k]

                def logits(g):
                    n = g0 + g
                    grp = groups[g]
                    heads = grp["heads"]
                    dve.wait_ge(S["at_scores"], n + 1)
                    if n >= 3:
                        dve.wait_ge(S["at_turned"], n - 2)
                    w, ne = grp["n"], len(heads)
                    by_head = probs[:, n % 3, 0:w].rearrange("p (e k) -> p e k", e=ne)
                    for e in range(ne):
                        src = score_bank(n, e)[:, 0:w // ne]
                        if grp["mask"] is None:
                            ins = nc.vector.tensor_scalar(by_head[:, e, :], src, grp["scale"], None, ALU.mult)
                        else:
                            ins = nc.vector.scalar_tensor_tensor(out=by_head[:, e, :], in0=src, scalar=grp["scale"], in1=grp["mask"],
                                                                 op0=ALU.mult, op1=ALU.add)
                    ins.then_inc(S["at_logits"], 1)
                    dve.wait_ge(S["at_logits"], n + 1)
                    steps.did(nc.vector.tensor_reduce(stat(n, 0, ne), by_head, AX, ALU.max))
                    steps.settle()
                    sink = grp.get("sink")
                    if sink is not None:
                        steps.did(nc.vector.tensor_tensor(stat(n, 0, 2), stat(n, 0, 2), cols[:, COL["sinks"] + sink:COL["sinks"] + sink + 2], ALU.max))
                        steps.settle()
                    nc.vector.tensor_scalar(stat(n, 2, ne), stat(n, 0, ne), -1.0, None, ALU.mult).then_inc(S["at_neg_max"], 1)

                def weights(g):
                    n = g0 + g
                    heads = groups[g]["heads"]
                    ne = len(heads)
                    dve.wait_ge(S["at_exp"], n + 1)
                    if groups[g].get("sink") is not None:
                        steps.did(nc.vector.tensor_tensor(stat(n, 4, 2), stat(n, 4, 2), stat(n, 6, 2), ALU.add))
                        steps.settle()
                    steps.did(nc.vector.reciprocal(stat(n, 0, ne), stat(n, 4, ne)))
                    steps.settle()
                    for e, (lo, w) in enumerate(heads):
                        part = probs[:, n % 3, lo:lo + w]
                        last = nc.vector.tensor_scalar(part, part, stat(n, e), None, ALU.mult)
                    last.then_inc(S["at_probs"], 1)

                for g in range(len(groups) + 1):
                    if g < len(groups):
                        logits(g)
                    if g >= 1:
                        weights(g - 1)

            def ffn_conv(k):
                w3 = cols[:, COL["fconv_w"] + (k - 1) * 3 * FT:COL["fconv_w"] + k * 3 * FT].rearrange("p (a b) -> p a b", b=3)
                b3 = cols[:, COL["fconv_b"] + (k - 1) * FT:COL["fconv_b"] + k * FT].rearrange("p (a b) -> p a b", b=1)
                steps.did(nc.vector.memset(up_pad[:, :, 0:2], 0.0))
                steps.settle()
                for i, u, p, use in pairs(dve, f"ffn{k}_up"):
                    if u == 0:
                        steps.loop(i, 4)
                    t = 2 * i + u
                    n = FT * (k - 1) + t
                    dve.wait_ge(S["conv3_in"], n + 1)
                    acc = up_acc[:, p, :]
                    steps.did(nc.vector.tensor_scalar(acc, up_pad[:, p, 0:T], w3[:, t, 0:1], b3[:, t, :], ALU.mult, ALU.add))
                    steps.settle()
                    steps.did(nc.vector.scalar_tensor_tensor(out=acc, in0=up_pad[:, p, 1:T + 1], scalar=w3[:, t, 1:2], in1=acc,
                                                             op0=ALU.mult, op1=ALU.add))
                    steps.settle()
                    nc.vector.scalar_tensor_tensor(out=acc, in0=up_pad[:, p, 2:T + 2], scalar=w3[:, t, 2:3], in1=acc,
                                                   op0=ALU.mult, op1=ALU.add).then_inc(S["conv3_ready"], 1)
                    dve.wait_ge(S["act_gate"], FT + n + 1)
                    nc.vector.tensor_tensor(hid[:, t, :], up_gate[:, p, :], banks[2 * p + 1][:], ALU.mult).then_inc(bank_free[p], 1)
                steps.end_loop(FT // 2)

            norm_dve(dve, steps, "kv", kv_low, kv_low, lambda c: col("kv_g", c))
            rope([8], 0, 32, 0)
            rope(range(8), 0, 32, 1)
            rope(range(9, 18), 2, 80, 9)
            dve.wait_ge(S["w_idx_ready"], 1)
            n = 0
            for b in range(1, TB):
                w = (b + 1) * P
                left = scores_left[:, 0:w]
                for hd in range(IDX_HEADS):
                    dve.wait_ge(S["relu_ready"], n + 1)
                    wcol = small[:, b * IDX_HEADS + hd:b * IDX_HEADS + hd + 1]
                    if hd == 0:
                        ins = nc.vector.tensor_scalar(left, relu_idx[:, n % 3, 0:w], wcol, None, ALU.mult)
                    else:
                        ins = nc.vector.scalar_tensor_tensor(out=left, in0=relu_idx[:, n % 3, 0:w], scalar=wcol, in1=left,
                                                             op0=ALU.mult, op1=ALU.add)
                    ins.then_inc(S["relu_used"], 1)
                    n += 1
                    dve.wait_ge(S["relu_used"], n)
                diagonal = left[:, b * P:w]
                steps.did(nc.vector.tensor_tensor(diagonal, diagonal, con("causal"), ALU.mult))
                steps.settle()
                steps.did(nc.vector.tensor_tensor(diagonal, diagonal, con("after_fill"), ALU.add))
                for _ in range(TOPK // 8):
                    steps.settle()
                    steps.did(nc.vector.max(small[:, 96:104], left))
                    steps.settle()
                    steps.did(nc.vector.match_replace(left, small[:, 96:104], left, CHOSEN))
                steps.settle()
                steps.did(nc.vector.tensor_scalar(chosen_at(b), left, CHOSEN, None, ALU.is_equal))
                steps.settle()
                steps.did(nc.vector.tensor_scalar(chosen_at(b), chosen_at(b), -1.0, -NEG, ALU.add, ALU.mult))
            steps.settle()
            attend(0)
            attend(1)
            residual("a_out", 2)
            wait_emptied(dve, "a_out")
            norm_dve(dve, steps, "ffn1", xT, hT, lambda c: col("g_ffn", c))
            ffn_conv(1)
            residual("ffn1_down", 1)
            wait_emptied(dve, "ffn1_down")
            norm_dve(dve, steps, "b_mix", xT, hT, lambda c: col("g_mix", DT + c))
            rope([8, 9], 2, 80, 18)
            rope(range(8), 2, 80, 20)
            attend(2)
            attend(3)
            residual("b_out", 2)
            wait_emptied(dve, "b_out")
            norm_dve(dve, steps, "ffn2", xT, hT, lambda c: col("g_ffn", DT + c))
            ffn_conv(2)
            residual("ffn2_down", 1)
            wait_emptied(dve, "ffn2_down")
            norm_dve(dve, steps, "last", xT, xT, lambda c: col("g_last", c))

        @block.gpsimd
        def _(pool):
            steps = Steps(pool, pool_steps)
            nc.gpsimd.memset(a_pad[:, :, 0:KW - 1], 0.0).then_inc(S["pads_zero"], 1)
            nc.gpsimd.memset(qk[:, :, 0:QW - 1], 0.0).then_inc(S["pads_zero"], 1)
            for j in range(4):
                p, use = one("merge_mlstm", j)
                pool.wait_ge(bank_free[p], use + 2)
                for m in range(2):
                    t = o_gate[:, 2 * j + m, :]
                    last = nc.gpsimd.tensor_tensor(t, t, merge_gate[:, 2 * (j % 2) + m, :], ALU.mult)
                last.then_inc(S["merge_used"], 1)
            pool.wait_ge(S["merge_used"], 4 + 2)
            for t in range(2 * HEADS):
                pool.wait_ge(S["hm_ready"], t + 1)
                steps.did(nc.gpsimd.tensor_tensor(qk[:, t, QW - 1:], qk[:, t, QW - 1:], o_gate[:, t, :], ALU.mult))
            steps.settle()
            for j in range(4):
                p, use = one("merge_conv", j)
                pool.wait_ge(bank_free[p], use + 2)
                for m in range(2):
                    y = y_conv[:, 2 * j + m, :]
                    last = nc.gpsimd.tensor_tensor(y, y, merge_gate[:, 2 * (j % 2) + m, :], ALU.mult)
                last.then_inc(S["merge_used"], 1)
                pool.wait_ge(S["merge_used"], 4 + 2 + j + 1)
                for m in range(2):
                    t = 2 * j + m
                    nc.gpsimd.tensor_tensor(y_conv[:, t, :], y_conv[:, t, :], qk[:, t, QW - 1:], ALU.add).then_inc(S["mixed_ready"], 1)
            p, use = one("a_uk", 0)
            pool.wait_ge(product_done[p], use)
            nc.gpsimd.memset(slot(p, 2, D).rearrange("p c (h n) -> p c h n", n=P)[:, :, :, 0:32], 0.0).then_inc(S["uk_pad_zero"], 1)

            def rope(tiles, table, rows, done):
                for k, t in enumerate(tiles):
                    n = done + k
                    if n >= 2:
                        pool.wait_ge(S["rope_ready"], n - 1)
                    nc.gpsimd.tensor_tensor(rot_cos[0:rows, n % 2, :], qkr[0:rows, t, :], trig[0:rows, table, :],
                                            ALU.mult).then_inc(S["rot_cos_ready"], 1)

            wait_emptied(pool, "a_qmem")
            rope([8], 0, 32, 0)
            rope(range(8), 0, 32, 1)
            rope(range(9, 18), 2, 80, 9)
            wait_emptied(pool, "b_qmem")
            rope([8, 9], 2, 80, 18)
            rope(range(8), 2, 80, 20)


def kernel(**inputs):
    import concourse.bacc as bacc
    from concourse.bass_utils import run_bass_kernel_spmd

    a = {k: np.ascontiguousarray(v) for k, v in inputs.items()}
    tiles = lambda v: v.reshape(-1, P).T

    b_in = a["b_in"][0]
    gates0 = 6 * D
    merge0 = gates0 + 2 * HEADS
    four = lambda v: np.pad(v.reshape(HEADS, 1), ((0, P - HEADS), (0, 0)))
    by_tap = lambda w: w.reshape(w.shape[0], -1, P).transpose(2, 1, 0).reshape(P, -1)
    parts = {
        "b_ada": tiles(a["b_ada"]), "c": tiles(a["c"]), "norm_mix_g": tiles(a["norm_mix_g"]), "b_glu": tiles(b_in[:2 * D]),
        "b_qk": tiles(b_in[2 * D:4 * D]), "b_o": tiles(b_in[5 * D:6 * D]), "b_merge": tiles(b_in[merge0:]),
        "dw_w": by_tap(a["conv_dw_w"][0]), "dw_b": tiles(a["conv_dw_b"]), "ln_g": tiles(a["conv_ln_g"]), "ln_b": tiles(a["conv_ln_b"]),
        "b_pw": tiles(a["b_conv_pw"]), "qk_w": by_tap(a["qk_conv_w"][0]), "qk_b": tiles(a["qk_conv_b"]),
        "mlstm_g": tiles(a["mlstm_norm_g"]), "norm_ffn_g": tiles(a["norm_ffn_g"]), "final_g": tiles(a["final_norm_g"]),
        "g_mix": tiles(a["g_mix_2"]), "g_ffn": tiles(a["g_ffn_2"]), "g_mem": tiles(a["g_mem_2"]), "g_last": tiles(a["g_final_2"]),
        "kv_g": tiles(a["a_kv_norm_2"]),
        "fconv_w": np.concatenate([by_tap(w) for w in a["f_conv_w_2"]], axis=1), "fconv_b": tiles(a["f_conv_b_2"]),
        "sinks": np.broadcast_to(a["b_sinks_2"][0], (P, B_HEADS)),
        "b_i": four(b_in[gates0:gates0 + HEADS]), "b_f": four(b_in[gates0 + HEADS:merge0]),
    }
    columns = np.concatenate([parts[name] for name, _ in COLUMNS], axis=1)
    assert columns.shape == (P, NCOL)

    feeds = {
        "columns": columns, "constants": constants(), "x": a["x"][0].T, "v_bias": b_in[None, 4 * D:5 * D],
        "mem": a["mem_2"][0].T, "positions": np.broadcast_to(a["positions_2"], (P, T)),
    }
    for name in ("w_ada", "w_in", "w_conv_pw", "w_out", "w_ffn_up", "w_ffn_down", "w_mem_kv_2", "a_w_in_2", "a_w_uk_2", "a_w_uv_2",
                 "a_w_out_2", "b_w_in_2", "b_w_out_2", "f_w_up_2", "f_w_down_2"):
        feeds[name] = a[name]
    feeds = {k: np.ascontiguousarray(v) for k, v in feeds.items()}

    nc = bacc.Bacc("TRN2", target_bir_lowering=False, num_devices=1)
    io = {k: nc.dram_tensor(f"in_{k}", v.shape, mybir.dt.from_np(v.dtype), kind="ExternalInput").ap() for k, v in feeds.items()}
    io["out"] = nc.dram_tensor("out", (D, T), F32, kind="ExternalOutput").ap()
    build(nc, io)
    r = run_bass_kernel_spmd(nc, [{f"in_{k}": v for k, v in feeds.items()}], core_ids=[0])
    return np.ascontiguousarray(r.results[0]["out"].T)[None]
```

```python
from contextlib import ExitStack

import concourse.bass as bass
import concourse.mybir as mybir
import numpy as np

F32 = mybir.dt.float32
F32R = mybir.dt.float32r
I32 = mybir.dt.int32
ACT = mybir.ActivationFunctionType
ALU = mybir.AluOpType
AX = mybir.AxisListType.X

P = 128
T = 512
TB = T // P
D = 1024
DT = D // P
HEADS = 4
KW = 31
QW = 4
FF = 2816
FT = FF // P
MEM = 256
R = 256
A_HEADS = 8
IDX_HEADS = 16
TOPK = 128
B_HEADS = 16
EPS = 1e-6
NEG = -1e30
OUTSIDE = -3.0e38
CHOSEN = -3.2e38
SLOT = FT * P
OUT_K = 10

HALVES = ((0, 12), (12, FT - 12))


def ffn_stages(k):
    return [(f"ffn{k}_{what}{half}", jobs) for half, (_, n) in enumerate(HALVES) for what, jobs in (("up", n), ("down", DT))]


STAGES = [
    ("ada_first", 8), ("glu", 8), ("qk", 8), ("gates", 2), ("v", 4), ("o", 4), ("ada_rest", 16),
    ("merge_mlstm", 4), ("conv_pw", 4), ("merge_conv", 4), ("mix_out", 4), *ffn_stages(0),
    ("a_mem", 2), ("a_q", 4), ("a_idx", 4), ("a_keys", 2), ("a_qmem", 1), ("a_uk", 1), ("a_uv", 1),
    ("a_out", 4), *ffn_stages(1),
    ("b_mem", 2), ("b_q", 4), ("b_k", 1), ("b_v", 1), ("b_qmem", 1), ("b_out", 4), *ffn_stages(2),
]
PIECES = {"a_uk": 2, "glu": 2, **{f"ffn{k}_up{half}": 2 for k in range(3) for half in range(2)}}
SPLIT = {name for k in range(3) for name, _ in ffn_stages(k)}


def job_table():
    first, loaded, split, before, n, count = {}, {}, [], {}, 0, [0, 0]
    for name, jobs in STAGES:
        first[name] = n
        before[name] = sum(split) // 2
        for j in range(jobs):
            pieces = 4 if (name, j) == ("a_keys", 0) else PIECES.get(name, 1)
            count[n % 2] += 16 * pieces
            loaded[n] = count[n % 2]
            split.append(name in SPLIT)
            n += 1
    return first, loaded, split, before


FIRST, LOADED, JOB_SPLIT, SPLITS_BEFORE = job_table()

COLUMNS = [("b_ada", 48), ("c", 8), ("norm_mix_g", 8), ("b_glu", 16), ("b_qk", 16), ("b_o", 8), ("b_merge", 16),
           ("dw_w", DT * KW), ("dw_b", 8), ("ln_g", 8), ("ln_b", 8), ("b_pw", 8), ("qk_w", 16 * QW), ("qk_b", 16),
           ("mlstm_g", 8), ("norm_ffn_g", 8), ("final_g", 8), ("g_mix", 16), ("g_ffn", 16), ("g_mem", 8),
           ("g_last", 8), ("kv_g", 2), ("fconv_w", 2 * FT * 3), ("fconv_b", 2 * FT), ("sinks", B_HEADS),
           ("b_i", 1), ("b_f", 1)]
COL, NCOL = {}, 0
for _name, _n in COLUMNS:
    COL[_name] = NCOL
    NCOL += _n

CONSTS = [("ident", P), ("rot32", P), ("rot64", P), ("dup_lo", P), ("dup_hi", P), ("one", P), ("mean_d", P), ("mean_r", P),
          ("head_row", HEADS * P), ("causal", P), ("causal_bias", P), ("after_fill", P), ("causal_t", P), ("band", 2 * P),
          ("inv32", 1), ("inv64", 1), ("eps", 1), ("zero", 1)]
CON, NCON = {}, 0
for _name, _n in CONSTS:
    CON[_name] = NCON
    NCON += _n


def constants():
    k = np.zeros((P, NCON), np.float32)
    put = lambda name, a: k[:, CON[name]:CON[name] + a.shape[1]].__setitem__(slice(0, a.shape[0]), a)
    put("ident", np.eye(P))
    for name, half, heads in (("rot32", 16, 1), ("rot64", 8, 2)):
        m = np.zeros((P, P))
        for h in range(heads):
            for j in range(half):
                m[64 * h + half + j, 64 * h + j] = -1.0
                m[64 * h + j, 64 * h + half + j] = 1.0
        put(name, m)
    for name, low in (("dup_lo", 0), ("dup_hi", 64)):
        m = np.zeros((P, P))
        m[low + np.arange(P) % 64, np.arange(P)] = 1.0
        put(name, m)
    put("one", np.ones((P, P)))
    put("mean_d", np.full((P, P), 1.0 / D))
    put("mean_r", np.full((P, P), 1.0 / R))
    put("head_row", np.repeat(np.eye(HEADS), P, axis=1))
    q, s = np.arange(P)[:, None], np.arange(P)[None, :]
    put("causal", (s <= q).astype(np.float32))
    put("causal_bias", np.where(s <= q, 0.0, NEG))
    put("after_fill", np.where(s <= q, 0.0, OUTSIDE))
    put("causal_t", (s >= q).astype(np.float32))
    band = np.concatenate([np.where(s > q, 0.0, NEG), np.where(s <= q, 0.0, NEG)], axis=1)
    put("band", band)
    for name, rot, period in (("inv32", 32, P), ("inv64", 16, 64)):
        inv = np.float32(500000.0) ** (-np.arange(0, rot, 2, dtype=np.float32) / np.float32(rot))
        col = np.zeros((P, 1), np.float32)
        for p in range(P):
            if p % period < rot:
                col[p] = inv[p % period % (rot // 2)]
        put(name, col)
    put("eps", np.full((P, 1), EPS))
    return k


TWO_PI_HI = 6.28125
TWO_PI_MID = 4058 / 2 ** 21
TWO_PI_LO = float(2 * np.pi - TWO_PI_HI - TWO_PI_MID)
ROUND = 1.5 * 2 ** 23
PI_IN = 3.1415925


class Steps:

    def __init__(self, eng, sem):
        self.eng, self.sem, self.base, self.n = eng, sem, 0, 0

    def did(self, ins):
        ins.then_inc(self.sem, 1)
        self.n += 1

    def settle(self):
        if not isinstance(self.base, int) or self.n:
            self.eng.wait_ge(self.sem, self.base + self.n)

    def loop(self, turn, per_turn):
        self.start, self.per_turn = self.n, per_turn
        self.base, self.n = turn * per_turn + self.start, 0

    def end_loop(self, turns):
        assert self.n == self.per_turn, (self.n, self.per_turn)
        self.base, self.n = 0, self.start + turns * self.per_turn


def build(nc, io):
    ctx = ExitStack()
    with ctx:
        def sb(name, shape, dt=F32):
            return ctx.enter_context(nc.sbuf_tensor(name, shape, dt))

        def sem(name):
            return ctx.enter_context(nc.semaphore(name))

        xT = sb("xT", [P, DT, T])
        hT_at = nc.sbuf_base
        hT = sb("hT", [P, DT, T])
        wslots = sb("wslots", [P, 2 * SLOT])
        cols = sb("cols", [P, NCOL])
        cons = sb("cons", [P, NCON])
        trig = sb("trig", [P, 4, T])
        rstd = sb("rstd", [P, T])
        square = sb("square", [P, 2, T])
        mod = sb("mod", [P, 6 * DT])
        modg = sb("modg", [P, 2, DT])
        silu_c = sb("silu_c", [P, DT])
        small = sb("small", [P, 128])
        ARENA = 31900
        arena_at = nc.sbuf_base
        arena = sb("arena", [P, ARENA])

        taken = [0]

        def region(*shape, at=None):
            if at is not None:
                taken[0] = at
            a = taken[0]
            n = int(np.prod(shape))
            taken[0] += n
            assert taken[0] <= ARENA, taken[0]
            v = arena[:, a:a + n]
            return v if len(shape) == 1 else v.rearrange("p (a b) -> p a b", b=shape[1])

        a_pad = region(DT, T + KW - 1, at=0)
        y_conv = arena[:, 0:DT * T].rearrange("p (a b) -> p a b", b=T)
        conv = region(DT, T)
        qk = region(16, T + QW - 1)
        v_tok = region(TB, D)
        o_gate = region(DT, T)
        probs_t = region(TB, T)
        sig = probs_t[:, 0:2, :]
        conv_acc = probs_t[:, 2:4, :]
        merge_gate = probs_t
        soft, logf = sig[0:HEADS, 0, :], sig[0:HEADS, 1, :]
        decay = region(2, T)
        tail = region(3, T)
        ones_row = tail[0:HEADS, 0, :]
        v_bias = tail[0:1, 1:3, :].rearrange("p a b -> p (a b)")
        em_all, abs_n, den = tail[:, 0, :], tail[:, 1, :], tail[:, 2, :]
        rows = region(4, T)
        cum_f, g_row, neg_m, em_row = (rows[0:HEADS, i, :] for i in range(4))
        trig_tmp = conv[:, 0:3, :]
        pos_int = conv[:, 3, :].bitcast(I32)

        def split_at(name, shape, at):
            return nc.alloc_sbuf_tensor_at(name, shape, F32R, offset=at)

        def split_region(name, *shape):
            at = arena_at + 4 * taken[0]
            region(int(np.prod(shape)))
            return split_at(name, [P, *shape], at)

        taken[0] = 0
        hid = split_region("hid", 2, HALVES[0][1], T)
        w_split = [split_region(f"w_split{p}", 2, DT * 2 * P) for p in range(2)]
        h_split = [split_at("h_hi", [P, DT, T], hT_at), split_region("h_lo", DT, T)]
        hid_raw = region(2, T)
        up_gate = region(2, T)
        up_pad = region(2, T + 2)
        up_acc = region(2, T)

        qkr = region(18, T, at=0)
        k_heads = region(A_HEADS, T)
        v_heads = region(TB, D)
        kv_low = region(2, T)
        q_mem = region(2, T)
        k_mem = region(2, MEM)
        v_mem = region(2, MEM)
        mem_out = region(2, T)
        chosen = region(sum(P * (b + 1) for b in range(1, TB)))
        scores_left = region(T)
        relu_idx = region(3, T)
        probs = region(3, T)
        probs_turned = region(2, T)
        memT = region(DT, MEM, at=ARENA - DT * MEM)
        rot_cos, rot_sin = relu_idx[:, 0:2, :], probs[:, 0:2, :]
        chosen_at = lambda b: chosen[:, P * (b * (b + 1) // 2 - 1):P * ((b + 1) * (b + 2) // 2 - 1)]
        kw_heads = k_heads

        banks = [ctx.enter_context(nc.psum_tensor(f"bank{i}", [P, T], F32)) for i in range(8)]

        weights_in = [sem("weights_in0"), sem("weights_in1")]
        hi_ready = [sem("hi_ready0"), sem("hi_ready1")]
        lo_ready = [sem("lo_ready0"), sem("lo_ready1")]
        product_done = [sem("product_done0"), sem("product_done1")]
        bank_free = [sem("bank_free0"), sem("bank_free1")]
        act_steps, dve_steps, pool_steps = sem("act_steps"), sem("dve_steps"), sem("pool_steps")
        S = {n: sem(n) for n in (
            "x_in cols_in cons_in pos_in vbias_in mem_in out_written pads_zero silu_c_ready modg_ready angle_ready trig_ready "
            "square_ready square_used root_ready norm_ready norm_scaled norm_hi hid_hi_ready hid_ready sig_ready conv_acc_ready conv_acc_free qk_ready "
            "softplus_ready g_turned decay_ready g_cols_ready nm_ready em_ready merge_used o_ready "
            "spread_ready logit_ready score_ready weight_ready num_ready abs_ready head_ready mean_ready dev_ready "
            "dev_square var_ready head_root hm_ready ym_ready conv_ready "
            "ln_mean ln_dev ln_square ln_square_used ln_root ln_scaled ln_ready yconv_ready mixed_ready "
            "act_gate conv3_in conv3_ready uk_pad_zero rot_ready rot_cos_ready rot_sin_ready rope_ready k_made k_taken "
            "v_made v_taken w_idx_turned w_idx_ready idx_dots relu_ready relu_used chosen_ready dup_made dup_ready "
            "at_scores at_logits at_neg_max at_exp at_probs at_turned at_copied at_sums at_out").split()}

        def col(name, i):
            return cols[:, COL[name] + i:COL[name] + i + 1]

        def col_at(name, n, r):
            return cols[:, COL[name]:COL[name] + n].rearrange("p (a b) -> p a b", b=1)[:, r, :]

        def con(name, n=P, p=P):
            return cons[0:p, CON[name]:CON[name] + n]

        def slot(p, kc, n):
            return wslots[:, p * SLOT:p * SLOT + kc * n].rearrange("p (c n) -> p c n", n=n)

        JOBS = dict(STAGES)
        SIZE = {f"ffn{k}_{what}{half}": n for k in range(3) for half, (_, tiles) in enumerate(HALVES)
                for what, n in (("up", DT * 2 * P), ("down", tiles * P))}

        def pairs(eng, name, first=0, end=None):
            n0 = FIRST[name]
            assert JOBS[name] % 2 == 0
            with eng.Fori(first, JOBS[name] // 2 if end is None else end) as i:
                for u in range(2):
                    yield i, u, (n0 + u) % 2, (n0 + u) // 2 + i

        def turn_of(name, i):
            for u in range(2):
                n = FIRST[name] + u
                yield i, u, n % 2, n // 2 + i

        def one(name, j):
            n = FIRST[name] + j
            return n % 2, n // 2

        def weights_of(name, u, i):
            n = FIRST[name] + u
            if JOBS[name] == 2:
                return LOADED[n]
            return i * (LOADED[n + 2] - LOADED[n]) + LOADED[n]

        def wait_emptied(eng, name):
            n = FIRST[name] + JOBS[name] - 1
            for m in (n - 1, n):
                eng.wait_ge(bank_free[m % 2], m // 2 + 2)

        NORMS = [("mix", DT, T), ("ffn0", DT, T), ("mem", DT, MEM), ("final0", DT, T), ("a_mix", DT, T), ("kv", 2, T),
                 ("ffn1", DT, T), ("b_mix", DT, T), ("ffn2", DT, T), ("last", DT, T)]
        TILES_BEFORE, NORM_NO = {}, {}
        for k, (name, _, _) in enumerate(NORMS):
            NORM_NO[name] = k
            TILES_BEFORE[name] = sum(t for _, t, _ in NORMS[:k])
        SPLIT_TILES_BEFORE = {"ffn0": 0, "ffn1": DT, "ffn2": 2 * DT}
        NORM_TILES = {name: (t, w) for name, t, w in NORMS}

        def wait_norm(eng, name):
            eng.wait_ge(S["norm_ready"], TILES_BEFORE[name] + NORM_TILES[name][0])

        def norm_act(act, name, src):
            tiles, w = NORM_TILES[name]
            for c in range(tiles):
                n = TILES_BEFORE[name] + c
                if n >= 2:
                    act.wait_ge(S["square_used"], n - 1)
                nc.scalar.activation(square[:, n % 2, 0:w], src[:, c, 0:w], ACT.Square).then_inc(S["square_ready"], 1)
            act.wait_ge(S["square_used"], TILES_BEFORE[name] + tiles)
            if TILES_BEFORE[name]:
                act.wait_ge(S["norm_ready"], TILES_BEFORE[name])
            nc.scalar.activation(rstd[:, 0:w], banks[4][:, 0:w], ACT.Sqrt, bias=con("eps", 1)).then_inc(S["root_ready"], 1)

        def norm_split(act, name, shift=None):
            for c in range(NORM_TILES[name][0]):
                n = SPLIT_TILES_BEFORE[name] + c
                act.wait_ge(S["norm_scaled"], n + 1)
                src = square[:, n % 2, :]
                if shift is None:
                    ins = nc.scalar.activation(h_split[0][:, c, :], src, ACT.Copy)
                else:
                    ins = nc.scalar.activation(h_split[0][:, c, :], src, ACT.Identity, bias=shift(c))
                ins.then_inc(S["norm_hi"], 1)

        def norm_pe(pe, name):
            tiles, w = NORM_TILES[name]
            mean = con("mean_d") if tiles == DT else con("mean_r")
            if NORM_NO[name]:
                pe.wait_ge(S["root_ready"], NORM_NO[name])
            for c in range(tiles):
                n = TILES_BEFORE[name] + c
                pe.wait_ge(S["square_ready"], n + 1)
                nc.tensor.matmul(banks[4][:, 0:w], mean, square[:, n % 2, 0:w], start=(c == 0),
                                 stop=(c == tiles - 1)).then_inc(S["square_used"], 1)

        def norm_dve(dve, steps, name, src, dst, gain, shift=None):
            tiles, w = NORM_TILES[name]
            dve.wait_ge(S["root_ready"], NORM_NO[name] + 1)
            steps.did(nc.vector.reciprocal(rstd[:, 0:w], rstd[:, 0:w]))
            steps.settle()
            for c in range(tiles):
                ins = nc.vector.scalar_tensor_tensor(out=dst[:, c, 0:w], in0=src[:, c, 0:w], scalar=gain(c),
                                                     in1=rstd[:, 0:w], op0=ALU.mult, op1=ALU.mult)
                if shift is not None:
                    steps.did(ins)
                    steps.settle()
                    ins = nc.vector.tensor_scalar(dst[:, c, 0:w], dst[:, c, 0:w], shift(c), None, ALU.add)
                ins.then_inc(S["norm_ready"], 1)

        def norm_dve_split(dve, steps, name, src, gain, shift=None):
            tiles = NORM_TILES[name][0]
            dve.wait_ge(S["root_ready"], NORM_NO[name] + 1)
            steps.did(nc.vector.reciprocal(rstd[:], rstd[:]))
            steps.settle()

            def scaled(c):
                if c >= 2:
                    dve.wait_ge(S["norm_ready"], TILES_BEFORE[name] + c - 1)
                nc.vector.scalar_tensor_tensor(out=square[:, c % 2, :], in0=src[:, c, :], scalar=gain(c), in1=rstd[:],
                                               op0=ALU.mult, op1=ALU.mult).then_inc(S["norm_scaled"], 1)

            def lower(c):
                n = SPLIT_TILES_BEFORE[name] + c
                dve.wait_ge(S["norm_scaled"], n + 1)
                dve.wait_ge(S["norm_hi"], n + 1)
                a, hi = square[:, c % 2, :], h_split[0][:, c, :].bitcast(F32)
                if shift is None:
                    ins = nc.vector.tensor_tensor(h_split[1][:, c, :], a, hi, ALU.subtract)
                else:
                    ins = nc.vector.scalar_tensor_tensor(out=h_split[1][:, c, :], in0=a, scalar=shift(c), in1=hi,
                                                         op0=ALU.add, op1=ALU.subtract)
                ins.then_inc(S["norm_ready"], 1)

            scaled(0)
            for c in range(1, tiles):
                scaled(c)
                lower(c - 1)
            lower(tiles - 1)

        def a_groups():
            for hd in range(A_HEADS):
                for b in range(TB):
                    n = (b + 1) * P
                    mask = con("causal_bias") if b == 0 else chosen_at(b)
                    yield dict(b=b, n=n, scores=[(n, qkr[:, hd, b * P:(b + 1) * P], k_heads[:, hd, 0:n])], mask=mask,
                               scale=P ** -0.5, heads=[(0, n)], out=hT[:, hd, :],
                               sums=[(0, P, [(v_heads[:, j, hd * P:(hd + 1) * P], j * P) for j in range(b + 1)])])

        def mem_groups():
            for t in range(2):
                for b in range(TB):
                    half = lambda e: slice(64 * e, 64 * e + 64)
                    yield dict(b=b, n=2 * MEM, mask=None, scale=0.125, heads=[(e * MEM, MEM) for e in range(2)], out=mem_out[:, t, :],
                               scores=[(MEM, q_mem[half(e), t, b * P:(b + 1) * P], k_mem[half(e), t, :]) for e in range(2)],
                               sums=[(64 * e, 64, [(v_mem[:, m, 64 * (2 * t + e):64 * (2 * t + e + 1)], e * MEM + m * P) for m in range(2)])
                                     for e in range(2)])

        def b_groups():
            for t in range(B_HEADS // 2):
                kv = t // 2
                for b in range(TB):
                    first = max(b - 1, 0)
                    n = (b + 1 - first) * P
                    half = lambda e: slice(64 * e, 64 * e + 64)
                    mask = con("band", 2 * P) if b else con("band", 2 * P)[:, P:]
                    yield dict(b=b, n=2 * n, mask=mask, scale=0.125, heads=[(e * n, n) for e in range(2)], out=hT[:, t, :], sink=2 * t,
                               scores=[(n, qkr[half(e), t, b * P:(b + 1) * P], kw_heads[half(e), kv, first * P:(b + 1) * P])
                                       for e in range(2)],
                               sums=[(64 * e, 64, [(v_heads[:, first + j, 64 * kv:64 * kv + 64], e * n + j * P) for j in range(b + 1 - first)])
                                     for e in range(2)])

        ATTENTION = [list(a_groups()), list(mem_groups()), list(b_groups()), list(mem_groups())]
        GROUPS_BEFORE = [sum(len(g) for g in ATTENTION[:k]) for k in range(5)]
        score_bank = lambda g, e: banks[2 + 2 * (g % 2) + e]
        NSTAT = 8
        stat = lambda g, lo, n=1: small[:, 64 + NSTAT * (g % 3) + lo:64 + NSTAT * (g % 3) + lo + n]

        block = ctx.enter_context(nc.Block())

        @block.sync
        def _(sp):
            w_ada = io["w_ada"][0].rearrange("(c p) n -> p c n", p=P)
            w_in = io["w_in"][0].rearrange("(c p) n -> p c n", p=P)

            sp.dma_start(cols[:], io["columns"]).then_inc(S["cols_in"], 16)
            sp.dma_start(cons[:], io["constants"]).then_inc(S["cons_in"], 16)

            def slot_free(name, i, u, p, use, last_split):
                if last_split:
                    sp.wait_ge(lo_ready[p], SPLITS_BEFORE[name] + i)
                else:
                    sp.wait_ge(product_done[p], use)

            def load(name, kc, width, pieces, first=0):
                split = name in SPLIT

                def fetch(i, u, p):
                    for lo, hi, src in pieces:
                        sp.dma_start(slot(p, kc, width)[:, :, lo:hi], src[:, :, 2 * i + u, :]).then_inc(weights_in[p], 16)

                if first == 0 and JOB_SPLIT[FIRST[name] - 1] != split:
                    for i, u, p, use in turn_of(name, 0):
                        slot_free(name, i, u, p, use, not split)
                        fetch(i, u, p)
                    first = 1
                for i, u, p, use in pairs(sp, name, first):
                    slot_free(name, i, u, p, use, split)
                    fetch(i, u, p)

            def cut(w, lo, hi, n):
                return w[:, :, lo:hi].rearrange("p c (j n) -> p c j n", n=n)

            def load_one(name, j, kc, width, pieces):
                p, use = one(name, j)
                slot_free(name, 0, 0, p, use, JOB_SPLIT[FIRST[name] + j - 2])
                for lo, hi, src in pieces:
                    sp.dma_start(slot(p, kc, width)[:, :, lo:hi], src).then_inc(weights_in[p], 16)

            def load_ffn(k, w_up, w_down):
                up = w_up.rearrange("(c p) n -> p c n", p=P)
                down = w_down.rearrange("(c p) n -> p c n", p=P)
                for half, (t0, n) in enumerate(HALVES):
                    lo, hi = t0 * P, (t0 + n) * P
                    load(f"ffn{k}_up{half}", DT, 2 * P, [(0, P, cut(up, lo, hi, P)), (P, 2 * P, cut(up, FF + lo, FF + hi, P))])
                    load(f"ffn{k}_down{half}", n, P, [(0, P, cut(down[:, t0:t0 + n, :], 0, D, P))])

            ada = cut(w_ada, 0, 6 * D, 2 * P)
            for j in range(2):
                sp.dma_start(slot(j, DT, 2 * P), ada[:, :, j, :]).then_inc(weights_in[j], 16)
            load("ada_first", DT, 2 * P, [(0, 2 * P, ada)], first=1)
            load("glu", DT, 2 * P, [(0, P, cut(w_in, 0, D, P)), (P, 2 * P, cut(w_in, D, 2 * D, P))])
            load("qk", DT, 2 * P, [(0, 2 * P, cut(w_in, 2 * D, 4 * D, 2 * P))])
            for j in range(2):
                load_one("gates", j, DT, HEADS, [(0, HEADS, w_in[:, :, 6 * D + HEADS * j:6 * D + HEADS * (j + 1)])])
            load("v", DT, 2 * P, [(0, 2 * P, cut(w_in, 4 * D, 5 * D, 2 * P))])
            load("o", DT, 2 * P, [(0, 2 * P, cut(w_in, 5 * D, 6 * D, 2 * P))])
            load("ada_rest", DT, 2 * P, [(0, 2 * P, cut(w_ada, 2 * D, 6 * D, 2 * P))])
            merge0 = 6 * D + 2 * HEADS
            load("merge_mlstm", DT, 2 * P, [(0, 2 * P, cut(w_in, merge0 + D, merge0 + 2 * D, 2 * P))])
            load("conv_pw", DT, 2 * P, [(0, 2 * P, cut(io["w_conv_pw"][0].rearrange("(c p) n -> p c n", p=P), 0, D, 2 * P))])
            load("merge_conv", DT, 2 * P, [(0, 2 * P, cut(w_in, merge0, merge0 + D, 2 * P))])
            load("mix_out", DT, 2 * P, [(0, 2 * P, cut(io["w_out"][0].rearrange("(c p) n -> p c n", p=P), 0, D, 2 * P))])
            load_ffn(0, io["w_ffn_up"][0], io["w_ffn_down"][0])
            wait_emptied(sp, "mix_out")
            sp.dma_start(memT, io["mem"].rearrange("(c p) t -> p c t", p=P)).then_inc(S["mem_in"], 16)

            def load_mem(name, k):
                w = io["w_mem_kv_2"][k].rearrange("(c p) n -> p c n", p=P)
                for j in range(2):
                    load_one(name, j, DT, 2 * P, [(0, 2 * P, w[:, :, 2 * P * j:2 * P * (j + 1)])])

            w_a = io["a_w_in_2"][0].rearrange("(c p) n -> p c n", p=P)
            kv0 = D
            kr0 = kv0 + R
            iq0 = kr0 + 32
            ik0 = iq0 + IDX_HEADS * 64
            iw0 = ik0 + 64
            mq0 = iw0 + IDX_HEADS
            load_mem("a_mem", 0)
            load("a_q", DT, 2 * P, [(0, 2 * P, cut(w_a, 0, D, 2 * P))])
            load("a_idx", DT, 2 * P, [(0, 2 * P, cut(w_a, iq0, ik0, 2 * P))])
            load_one("a_keys", 0, DT, 176, [(0, 32, w_a[:, :, kr0:iq0]), (32, 48, w_a[:, :, iw0:mq0]),
                                            (48, 112, w_a[:, :, ik0:iw0]), (112, 176, w_a[:, :, ik0:iw0])])
            load_one("a_keys", 1, DT, 2 * P, [(0, 2 * P, w_a[:, :, kv0:kr0])])
            load_one("a_qmem", 0, DT, 2 * P, [(0, 2 * P, w_a[:, :, mq0:mq0 + 2 * P])])
            p, use = one("a_uk", 0)
            sp.wait_ge(S["uk_pad_zero"], 1)
            uk = io["a_w_uk_2"][0].rearrange("(c p) h n -> p c h n", p=P)
            for c in range(2):
                sp.dma_start(slot(p, 2, D).rearrange("p c (h n) -> p c h n", n=P)[:, c, :, 32:P], uk[:, c]).then_inc(weights_in[p], 16)
            load_one("a_uv", 0, 2, D, [(0, D, io["a_w_uv_2"][0].rearrange("(c p) h n -> p c (h n)", p=P))])
            out_of = lambda w: cut(w.rearrange("(c p) n -> p c n", p=P), 0, D, 2 * P)
            load("a_out", OUT_K, 2 * P, [(0, 2 * P, out_of(io["a_w_out_2"][0]))])
            load_ffn(1, io["f_w_up_2"][0], io["f_w_down_2"][0])
            load_mem("b_mem", 1)
            w_b = io["b_w_in_2"][0].rearrange("(c p) n -> p c n", p=P)
            load("b_q", DT, 2 * P, [(0, 2 * P, cut(w_b, 0, D, 2 * P))])
            for name, lo in (("b_k", D), ("b_v", D + 2 * P), ("b_qmem", D + 4 * P)):
                load_one(name, 0, DT, 2 * P, [(0, 2 * P, w_b[:, :, lo:lo + 2 * P])])
            load("b_out", OUT_K, 2 * P, [(0, 2 * P, out_of(io["b_w_out_2"][0]))])
            load_ffn(2, io["f_w_up_2"][1], io["f_w_down_2"][1])
            wait_norm(sp, "last")
            sp.dma_start(io["out"].rearrange("(c p) t -> p c t", p=P), xT[:]).then_inc(S["out_written"], 16)
            sp.wait_ge(S["out_written"], 16)

        @block.tensor
        def _(pe):
            def product(name, kc, width, rhs, tiles=2):
                for i, u, p, use in pairs(pe, name):
                    pe.wait_ge(weights_in[p], weights_of(name, u, i))
                    pe.wait_ge(bank_free[p], use + 1)
                    w = slot(p, kc, width)
                    for m in range(tiles):
                        for c in range(kc):
                            last = nc.tensor.matmul(banks[2 * p + m][:], w[:, c, m * P:(m + 1) * P], rhs(c),
                                                    start=(c == 0), stop=(c == kc - 1))
                    last.then_inc(product_done[p], 1)

            def split_product(name, kc, width, rhs, ready, before, tiles=2):
                for i, u, p, use in pairs(pe, name):
                    pe.wait_ge(lo_ready[p], SPLITS_BEFORE[name] + i + 1)
                    pe.wait_ge(bank_free[p], use + 1)
                    w = [w_split[p][:, part, 0:kc * width].rearrange("p (c n) -> p c n", n=width) for part in range(2)]
                    for m in range(tiles):
                        for c in range(kc):
                            if u == 0 and m == 0:
                                pe.wait_ge(S[ready], before + c + 1)
                            for wp, hp in ((0, 0), (0, 1), (1, 0)):
                                last = nc.tensor.matmul(banks[2 * p + m][:], w[wp][:, c, m * P:(m + 1) * P], rhs(c, hp),
                                                        start=(c == 0 and wp + hp == 0), stop=(c == kc - 1 and wp == 1))
                    last.then_inc(product_done[p], 1)

            def start_one(name, j):
                p, use = one(name, j)
                pe.wait_ge(weights_in[p], LOADED[FIRST[name] + j])
                pe.wait_ge(bank_free[p], use + 1)
                return p

            def product_one(name, j, kc, sizes, rhs, width=T):
                p = start_one(name, j)
                w = slot(p, kc, sum(sizes))
                for m, n in enumerate(sizes):
                    lo = sum(sizes[:m])
                    for c in range(kc):
                        last = nc.tensor.matmul(banks[2 * p + m][0:n, 0:width], w[:, c, lo:lo + n], rhs(c),
                                                start=(c == 0), stop=(c == kc - 1))
                last.then_inc(product_done[p], 1)

            def modulation(name):
                for i, u, p, use in pairs(pe, name):
                    pe.wait_ge(weights_in[p], weights_of(name, u, i))
                    pe.wait_ge(bank_free[p], use + 1)
                    w = slot(p, DT, 2 * P)
                    for m in range(2):
                        for c in range(DT):
                            last = nc.tensor.matmul(banks[2 * p][:, m:m + 1], w[:, c, m * P:(m + 1) * P], silu_c[:, c:c + 1],
                                                    start=(c == 0), stop=(c == DT - 1))
                    last.then_inc(product_done[p], 1)

            h = lambda c: hT[:, c, :]
            h_parts = lambda c, part: h_split[part][:, c, :]

            pe.wait_ge(S["cons_in"], 16)
            norm_pe(pe, "mix")
            pe.wait_ge(S["silu_c_ready"], 1)
            modulation("ada_first")
            wait_norm(pe, "mix")
            product("glu", DT, 2 * P, h)
            product("qk", DT, 2 * P, h)
            for j in range(2):
                product_one("gates", j, DT, [HEADS], h)
            pe.wait_ge(S["vbias_in"], 16)
            for i, u, p, use in pairs(pe, "v"):
                pe.wait_ge(weights_in[p], weights_of("v", u, i))
                pe.wait_ge(bank_free[p], use + 1)
                w = slot(p, DT, 2 * P)
                for b in range(TB):
                    out = banks[2 * p + b // 2][:, (b % 2) * 2 * P:(b % 2 + 1) * 2 * P]
                    nc.tensor.matmul(out, con("one", p=1), v_bias.rearrange("p (j n) -> p j n", n=2 * P)[:, 2 * i + u, :],
                                     start=True, stop=False)
                    for c in range(DT):
                        last = nc.tensor.matmul(out, hT[:, c, b * P:(b + 1) * P], w[:, c, :], start=False, stop=(c == DT - 1))
                last.then_inc(product_done[p], 1)
            product("o", DT, 2 * P, h)
            wait_emptied(pe, "gates")
            for b in range(TB):
                last = nc.tensor.transpose(banks[4][:, b * HEADS:(b + 1) * HEADS], g_row[:, b * P:(b + 1) * P],
                                           con("ident", HEADS, HEADS))
            last.then_inc(S["g_turned"], 1)
            modulation("ada_rest")
            product("merge_mlstm", DT, 2 * P, h)

            wait_emptied(pe, "merge_mlstm")
            pe.wait_ge(S["conv_acc_free"], 16 + 2)
            pe.wait_ge(S["nm_ready"], 2)
            pe.wait_ge(S["em_ready"], 1)
            pe.wait_ge(S["g_cols_ready"], 1)
            for hd in range(HEADS):
                if hd:
                    pe.wait_ge(S["head_ready"], 2 * hd)
                nc.tensor.matmul(banks[4][:], con("head_row", HEADS * P, HEADS)[:, hd * P:(hd + 1) * P], neg_m,
                                 start=True, stop=True).then_inc(S["spread_ready"], 1)
                nc.tensor.matmul(banks[5][:], con("head_row", HEADS * P, HEADS)[:, hd * P:(hd + 1) * P], em_row,
                                 start=True, stop=True).then_inc(S["spread_ready"], 1)

                def scores(j):
                    n = TB * hd + j
                    if n >= 2:
                        pe.wait_ge(S["weight_ready"], n - 1)
                    for e in range(2):
                        last = nc.tensor.matmul(banks[6 + j % 2][:, 0:T - j * P],
                                                qk[:, 8 + 2 * hd + e, QW - 1 + j * P:QW - 1 + (j + 1) * P],
                                                qk[:, 2 * hd + e, QW - 1 + j * P:QW - 1 + T], start=(e == 0), stop=(e == 1))
                    last.then_inc(S["score_ready"], 1)

                def sums(j):
                    pe.wait_ge(S["weight_ready"], TB * hd + j + 1)
                    rhs = probs_t[:, j, j * P:T]
                    for e in range(2):
                        nc.tensor.matmul(banks[e][:, j * P:T], v_tok[:, j, (2 * hd + e) * P:(2 * hd + e + 1) * P], rhs,
                                         start=(j == 0), stop=(j == TB - 1))
                    last = nc.tensor.matmul(banks[2][:, j * P:T], con("one"), rhs, start=(j == 0), stop=(j == TB - 1))
                    if j == TB - 1:
                        last.then_inc(S["num_ready"], 1)

                scores(0)
                for j in range(1, TB):
                    scores(j)
                    sums(j - 1)
                sums(TB - 1)
                pe.wait_ge(S["head_ready"], 2 * hd + 2)
                for e in range(2):
                    last = nc.tensor.matmul(banks[3][:], con("mean_r"), qk[:, 2 * hd + e, QW - 1:], start=(e == 0), stop=(e == 1))
                last.then_inc(S["mean_ready"], 1)
                pe.wait_ge(S["dev_ready"], 2 * hd + 2)
                for e in range(2):
                    pe.wait_ge(S["dev_square"], 2 * hd + e + 1)
                    last = nc.tensor.matmul(banks[3][:], con("mean_r"), square[:, e, :], start=(e == 0), stop=(e == 1))
                last.then_inc(S["var_ready"], 1)

            pe.wait_ge(S["conv_ready"], DT)
            pe.wait_ge(S["head_root"], HEADS)
            for c in range(DT):
                last = nc.tensor.matmul(banks[4][:], con("mean_d"), conv[:, c, :], start=(c == 0), stop=(c == DT - 1))
            last.then_inc(S["ln_mean"], 1)
            for c in range(DT):
                pe.wait_ge(S["ln_square"], c + 1)
                nc.tensor.matmul(banks[5][:], con("mean_d"), square[:, c % 2, :], start=(c == 0),
                                 stop=(c == DT - 1)).then_inc(S["ln_square_used"], 1)
            pe.wait_ge(S["ln_ready"], DT)
            product("conv_pw", DT, 2 * P, lambda c: conv[:, c, :])
            product("merge_conv", DT, 2 * P, h)
            pe.wait_ge(S["mixed_ready"], DT)
            product("mix_out", DT, 2 * P, lambda c: y_conv[:, c, :])

            def ffn(k):
                norm_pe(pe, f"ffn{k}")
                for half, (t0, n) in enumerate(HALVES):
                    split_product(f"ffn{k}_up{half}", DT, 2 * P, h_parts, "norm_ready", TILES_BEFORE[f"ffn{k}"])
                    split_product(f"ffn{k}_down{half}", n, P, lambda c, part: hid[:, part, c, :], "hid_ready", 2 + FT * k + t0, tiles=1)

            ffn(0)

            def memory_kv(name):
                product_one(name, 0, DT, [P, P], lambda c: memT[:, c, :], MEM)
                p = start_one(name, 1)
                for m in range(2):
                    for c in range(DT):
                        last = nc.tensor.matmul(banks[2 * p + m][:, 0:MEM], memT[:, c, m * P:(m + 1) * P], slot(p, DT, 2 * P)[:, c, :],
                                                start=(c == 0), stop=(c == DT - 1))
                last.then_inc(product_done[p], 1)

            def rotate(tiles, name, rows, done):
                for k, t in enumerate(tiles):
                    n = done + k
                    if n >= 2:
                        pe.wait_ge(S["rot_sin_ready"], n - 1)
                    nc.tensor.matmul(banks[4 + n % 2][0:rows, :], con(name, rows, rows), qkr[0:rows, t, :],
                                     start=True, stop=True).then_inc(S["rot_ready"], 1)

            def attend(k):
                g0, groups = GROUPS_BEFORE[k], ATTENTION[k]

                def scores(g):
                    if g0 + g >= 2:
                        pe.wait_ge(S["at_logits"], g0 + g - 1)
                    for e, (n, q, kk) in enumerate(groups[g]["scores"]):
                        last = nc.tensor.matmul(score_bank(g0 + g, e)[:, 0:n], q, kk, start=True, stop=True)
                    last.then_inc(S["at_scores"], 1)

                def turn(g):
                    pe.wait_ge(S["at_probs"], g0 + g + 1)
                    if g0 + g >= 2:
                        pe.wait_ge(S["at_copied"], g0 + g - 1)
                    for j in range(groups[g]["n"] // P):
                        last = nc.tensor.transpose(banks[6 + (g0 + g) % 2][:, j * P:(j + 1) * P],
                                                   probs[:, (g0 + g) % 3, j * P:(j + 1) * P], con("ident"))
                    last.then_inc(S["at_turned"], 1)

                def sums(g):
                    pe.wait_ge(S["at_copied"], g0 + g + 1)
                    unit, b = divmod(g0 + g, TB)
                    if b == 0 and unit >= 2:
                        pe.wait_ge(S["at_out"], unit - 1)
                    for lo, n, parts in groups[g]["sums"]:
                        for i, (v, at) in enumerate(parts):
                            last = nc.tensor.matmul(banks[unit % 2][lo:lo + n, b * P:(b + 1) * P], v,
                                                    probs_turned[:, (g0 + g) % 2, at:at + P], start=(i == 0), stop=(i == len(parts) - 1))
                    last.then_inc(S["at_sums"], 1)

                for g in range(len(groups) + 3):
                    if g < len(groups):
                        scores(g)
                    if 2 <= g <= len(groups) + 1:
                        turn(g - 2)
                    if g >= 3:
                        sums(g - 3)

            def output(name, k):
                pe.wait_ge(S["at_out"], GROUPS_BEFORE[k] // TB)
                product(name, OUT_K, 2 * P, lambda c: hT[:, c, :] if c < DT else mem_out[:, c - DT, :])

            pe.wait_ge(S["norm_ready"], TILES_BEFORE["mem"])
            norm_pe(pe, "mem")
            norm_pe(pe, "final0")
            wait_norm(pe, "mem")
            memory_kv("a_mem")
            norm_pe(pe, "a_mix")
            wait_norm(pe, "a_mix")
            product("a_q", DT, 2 * P, h)
            product("a_idx", DT, 2 * P, h)
            product_one("a_keys", 0, DT, [48, P], h)
            product_one("a_keys", 1, DT, [P, P], h)
            product_one("a_qmem", 0, DT, [P, P], h)
            wait_emptied(pe, "a_qmem")
            norm_pe(pe, "kv")
            pe.wait_ge(S["root_ready"], NORM_NO["kv"] + 1)
            rotate([8], "rot32", 32, 0)
            rotate(range(8), "rot32", 32, 1)
            rotate(range(9, 18), "rot64", 80, 9)
            wait_norm(pe, "kv")
            p = start_one("a_uk", 0)
            pe.wait_ge(S["rope_ready"], 1)
            pe.wait_ge(S["rot_sin_ready"], 18)
            for hd in range(A_HEADS):
                bank = banks[(2 * p, 2 * p + 1, 6, 7)[hd % 4]]
                if hd >= 4:
                    pe.wait_ge(S["k_taken"], hd - 3)
                for c in range(2):
                    nc.tensor.matmul(bank[:], slot(p, 2, D)[:, c, hd * P:(hd + 1) * P], kv_low[:, c, :], start=(c == 0), stop=False)
                last = nc.tensor.matmul(bank[:], con("ident", P, 32), qkr[0:32, 8, :], start=False, stop=True)
                last.then_inc(S["k_made"] if hd < A_HEADS - 1 else product_done[p], 1)
            p = start_one("a_uv", 0)
            for n in range(2 * TB):
                b, half = divmod(n, 2)
                if n >= 2:
                    pe.wait_ge(S["v_taken"], n - 1)
                for c in range(2):
                    last = nc.tensor.matmul(banks[2 * p + n % 2][:], kv_low[:, c, b * P:(b + 1) * P],
                                            slot(p, 2, D)[:, c, half * T:(half + 1) * T], start=(c == 0), stop=(c == 1))
                last.then_inc(S["v_made"] if n < 2 * TB - 1 else product_done[p], 1)
            wait_emptied(pe, "a_uv")
            for b in range(TB):
                last = nc.tensor.transpose(banks[6][:, b * IDX_HEADS:(b + 1) * IDX_HEADS], qkr[32:48, 8, b * P:(b + 1) * P],
                                           cons[32:48, CON["ident"] + 32:CON["ident"] + 48])
            last.then_inc(S["w_idx_turned"], 1)
            pe.wait_ge(S["rope_ready"], 18)
            pe.wait_ge(S["w_idx_ready"], 1)
            n = 0
            for b in range(1, TB):
                for hd in range(IDX_HEADS):
                    half = slice(64 * (hd % 2), 64 * (hd % 2) + 64)
                    if n >= 4:
                        pe.wait_ge(S["relu_ready"], n - 3)
                    nc.tensor.matmul(banks[4 + n % 4][:, 0:(b + 1) * P], qkr[half, 9 + hd // 2, b * P:(b + 1) * P],
                                     qkr[half, 17, 0:(b + 1) * P], start=True, stop=True).then_inc(S["idx_dots"], 1)
                    n += 1
            pe.wait_ge(S["relu_ready"], n)
            attend(0)
            attend(1)
            output("a_out", 2)
            ffn(1)
            memory_kv("b_mem")
            norm_pe(pe, "b_mix")
            wait_norm(pe, "b_mix")
            product("b_q", DT, 2 * P, h)
            product_one("b_k", 0, DT, [P, P], h)
            p = start_one("b_v", 0)
            for b in range(TB):
                for c in range(DT):
                    last = nc.tensor.matmul(banks[2 * p + b // 2][:, (b % 2) * 2 * P:(b % 2 + 1) * 2 * P], hT[:, c, b * P:(b + 1) * P],
                                            slot(p, DT, 2 * P)[:, c, :], start=(c == 0), stop=(c == DT - 1))
            last.then_inc(product_done[p], 1)
            product_one("b_qmem", 0, DT, [P, P], h)
            wait_emptied(pe, "b_qmem")
            pe.wait_ge(S["root_ready"], NORM_NO["b_mix"] + 1)
            rotate([8, 9], "rot64", 80, 18)
            rotate(range(8), "rot64", 80, 20)
            for kv in range(4):
                pe.wait_ge(S["rope_ready"], 18 + kv // 2 + 1)
                if kv >= 2:
                    pe.wait_ge(S["dup_ready"], kv - 1)
                nc.tensor.matmul(banks[6 + kv % 2][:], con("dup_hi" if kv % 2 else "dup_lo"), qkr[:, 8 + kv // 2, :],
                                 start=True, stop=True).then_inc(S["dup_made"], 1)
            pe.wait_ge(S["dup_ready"], 4)
            pe.wait_ge(S["rope_ready"], 28)
            attend(2)
            attend(3)
            output("b_out", 4)
            ffn(2)
            norm_pe(pe, "last")

        @block.scalar
        def _(act):
            steps = Steps(act, act_steps)
            act.dma_start(xT[:], io["x"].rearrange("(c p) t -> p c t", p=P)).then_inc(S["x_in"], 16)
            act.dma_start(pos_int, io["positions"]).then_inc(S["pos_in"], 16)
            act.wait_ge(S["pos_in"], 16)
            for p in range(2):
                act.sem_inc(bank_free[p], 1)
            act.sem_inc(S["conv_acc_free"], 2)
            act.sem_inc(S["merge_used"], 2)
            act.sem_inc(S["hid_ready"], 2)
            act.wait_ge(S["x_in"], 16)
            act.wait_ge(S["cons_in"], 16)
            norm_act(act, "mix", xT)
            act.wait_ge(S["cols_in"], 16)
            nc.scalar.activation(silu_c[:], cols[:, COL["c"]:COL["c"] + DT], ACT.Silu).then_inc(S["silu_c_ready"], 1)

            def mod_columns(name, first):
                m0 = first // 2
                n = JOBS[name]
                mods = mod[:, 2 * m0:2 * (m0 + n)].rearrange("p (a b) -> p a b", b=2)
                bias = cols[:, COL["b_ada"] + 2 * m0:COL["b_ada"] + 2 * (m0 + n)].rearrange("p (a b) -> p a b", b=2)
                for i, u, p, use in pairs(act, name):
                    act.wait_ge(product_done[p], use + 1)
                    nc.scalar.activation(mods[:, 2 * i + u, 0:1], banks[2 * p][:, 0:1], ACT.Identity, bias=bias[:, 2 * i + u, 0:1])
                    nc.scalar.activation(mods[:, 2 * i + u, 1:2], banks[2 * p][:, 1:2], ACT.Identity,
                                         bias=bias[:, 2 * i + u, 1:2]).then_inc(bank_free[p], 1)

            mod_columns("ada_first", 0)
            for k in range(4):
                act.wait_ge(S["angle_ready"], k + 1)
                nc.scalar.activation(trig[:, k, :], trig[:, k, :], ACT.Sin).then_inc(S["trig_ready"], 1)
            act.wait_ge(S["trig_ready"], 4)
            act.dma_start(v_bias, io["v_bias"]).then_inc(S["vbias_in"], 16)
            for i, u, p, use in pairs(act, "glu"):
                act.wait_ge(product_done[p], use + 1)
                nc.scalar.activation(sig[:, p, :], banks[2 * p + 1][:], ACT.Sigmoid,
                                     bias=col_at("b_glu", 16, 8 + 2 * i + u)).then_inc(S["sig_ready"], 1)
            act.wait_ge(S["pads_zero"], 2)
            for i, u, p, use in pairs(act, "qk"):
                act.wait_ge(product_done[p], use + 1)
                for m in range(2):
                    last = nc.scalar.activation(qk[:, 4 * i + 2 * u + m, QW - 1:], banks[2 * p + m][:], ACT.Identity,
                                                bias=col_at("b_qk", 16, 4 * i + 2 * u + m))
                last.then_inc(bank_free[p], 1)
                for m in range(2):
                    act.wait_ge(S["conv_acc_ready"], 4 * i + 2 * u + m + 1)
                    nc.scalar.activation(qk[:, 4 * i + 2 * u + m, QW - 1:], conv_acc[:, m, :], ACT.Silu,
                                         bias=col_at("qk_b", 16, 4 * i + 2 * u + m)).then_inc(S["conv_acc_free"], 1)
            p, use = one("gates", 1)
            act.wait_ge(product_done[p], use + 1)
            steps.did(nc.scalar.activation(soft, banks[2 * p][0:HEADS, :], ACT.Abs, bias=cols[0:HEADS, COL["b_f"]:COL["b_f"] + 1]))
            steps.settle()
            steps.did(nc.scalar.activation(soft, soft, ACT.Exp, scale=-1.0))
            steps.settle()
            nc.scalar.activation(soft, soft, ACT.Ln, bias=1.0).then_inc(S["softplus_ready"], 1)
            v_cut = v_tok.rearrange("p b (j n) -> p b j n", n=2 * P)
            for i, u, p, use in pairs(act, "v"):
                act.wait_ge(product_done[p], use + 1)
                for m in range(2):
                    last = nc.scalar.activation(v_cut[:, 2 * m:2 * m + 2, 2 * i + u, :],
                                                banks[2 * p + m][:].rearrange("p (b n) -> p b n", n=2 * P), ACT.Copy)
                last.then_inc(bank_free[p], 1)
            act.wait_ge(S["nm_ready"], 2)
            nc.scalar.activation(em_row, em_row, ACT.Exp).then_inc(S["em_ready"], 1)
            for i, u, p, use in pairs(act, "o"):
                act.wait_ge(product_done[p], use + 1)
                for m in range(2):
                    last = nc.scalar.activation(o_gate[:, 4 * i + 2 * u + m, :], banks[2 * p + m][:], ACT.Sigmoid,
                                                bias=col_at("b_o", 8, 4 * i + 2 * u + m))
                last.then_inc(bank_free[p], 1)
            act.wait_ge(S["g_turned"], 1)
            nc.scalar.activation(small[:, 0:TB * HEADS], banks[4][:, 0:TB * HEADS], ACT.Copy).then_inc(S["g_cols_ready"], 1)
            mod_columns("ada_rest", 16)

            def merge_gates(name, b0, earlier):
                for i, u, p, use in pairs(act, name):
                    act.wait_ge(product_done[p], use + 1)
                    act.wait_ge(S["merge_used"], 2 * i + u + 1 + earlier)
                    for m in range(2):
                        last = nc.scalar.activation(merge_gate[:, 2 * u + m, :], banks[2 * p + m][:], ACT.Sigmoid,
                                                    bias=col_at("b_merge", 16, b0 + 4 * i + 2 * u + m))
                    last.then_inc(bank_free[p], 1)

            merge_gates("merge_mlstm", 8, 0)
            gcol = lambda j, hd: small[:, j * HEADS + hd:j * HEADS + hd + 1]
            for hd in range(HEADS):
                act.wait_ge(S["spread_ready"], 2 * hd + 2)
                steps.did(nc.scalar.activation(em_all, banks[5][:], ACT.Copy))
                for j in range(TB):
                    act.wait_ge(S["logit_ready"], TB * hd + j + 1)
                    nc.scalar.activation(decay[:, j % 2, 0:T - j * P], decay[:, j % 2, 0:T - j * P],
                                         ACT.Exp).then_inc(S["decay_ready"], 1)
                act.wait_ge(S["num_ready"], hd + 1)
                steps.settle()
                nc.scalar.activation(abs_n, banks[2][:], ACT.Abs).then_inc(S["abs_ready"], 1)
                for e in range(2):
                    act.wait_ge(S["dev_ready"], 2 * hd + e + 1)
                    nc.scalar.activation(square[:, e, :], qk[:, 2 * hd + e, QW - 1:], ACT.Square).then_inc(S["dev_square"], 1)
                act.wait_ge(S["var_ready"], hd + 1)
                nc.scalar.activation(rstd[:], banks[3][:], ACT.Sqrt, bias=con("eps", 1)).then_inc(S["head_root"], 1)
            for c in range(DT):
                act.wait_ge(S["ln_dev"], c + 1)
                if c >= 2:
                    act.wait_ge(S["ln_square_used"], c - 1)
                nc.scalar.activation(square[:, c % 2, :], conv[:, c, :], ACT.Square).then_inc(S["ln_square"], 1)
            act.wait_ge(S["ln_square_used"], DT)
            act.wait_ge(S["hm_ready"], 2 * HEADS)
            nc.scalar.activation(rstd[:], banks[5][:], ACT.Sqrt, bias=con("eps", 1)).then_inc(S["ln_root"], 1)
            for c in range(DT):
                act.wait_ge(S["ln_scaled"], c + 1)
                nc.scalar.activation(conv[:, c, :], conv[:, c, :], ACT.Silu, bias=col("ln_b", c)).then_inc(S["ln_ready"], 1)
            for i, u, p, use in pairs(act, "conv_pw"):
                act.wait_ge(product_done[p], use + 1)
                for m in range(2):
                    last = nc.scalar.activation(y_conv[:, 4 * i + 2 * u + m, :], banks[2 * p + m][:], ACT.Identity,
                                                bias=col_at("b_pw", 8, 4 * i + 2 * u + m))
                last.then_inc(bank_free[p], 1)
            merge_gates("merge_conv", 0, 4)

            def split_weights(name, i, u, p, use):
                n = SIZE[name]
                act.wait_ge(weights_in[p], weights_of(name, u, i))
                act.wait_ge(product_done[p], use)
                nc.scalar.activation(w_split[p][:, 0, 0:n], slot(p, 1, n)[:, 0, :], ACT.Copy).then_inc(hi_ready[p], 1)

            def split_first(name, u):
                i, u, p, use = list(turn_of(name, 0))[u]
                split_weights(name, i, u, p, use)

            def split_ahead(name, following, take=None):
                turns = JOBS[name] // 2
                for i, u, p, use in pairs(act, name, 0, turns - 1):
                    split_weights(name, i + 1, u, p, use + 1)
                    if take:
                        take(i, u, p, use)
                for i, u, p, use in turn_of(name, turns - 1):
                    if following:
                        split_first(following, u)
                    if take:
                        take(i, u, p, use)

            def ffn(k):
                for half, (t0, tiles) in enumerate(HALVES):
                    def take(i, u, p, use):
                        n = FT * k + t0 + 2 * i + u
                        act.wait_ge(product_done[p], use + 1)
                        gates = banks[2 * p][:]
                        if k:
                            nc.scalar.activation(up_pad[:, p, 2:], gates, ACT.Copy).then_inc(S["conv3_in"], 1)
                            act.wait_ge(S["conv3_ready"], n - FT + 1)
                            gates = up_acc[:, p, :]
                        nc.scalar.activation(up_gate[:, p, :], gates, ACT.Silu).then_inc(S["act_gate"], 1)
                        act.wait_ge(bank_free[p], use + 2)
                        nc.scalar.activation(hid[:, 0, 0:tiles, :][:, 2 * i + u, :], hid_raw[:, p, :], ACT.Copy).then_inc(S["hid_hi_ready"], 1)

                    split_ahead(f"ffn{k}_up{half}", f"ffn{k}_down{half}", take)
                    split_ahead(f"ffn{k}_down{half}", f"ffn{k}_up1" if half == 0 else None)

            split_first("ffn0_up0", 0)
            wait_emptied(act, "mix_out")
            norm_act(act, "ffn0", xT)
            split_first("ffn0_up0", 1)
            norm_split(act, "ffn0", lambda c: mod[:, 3 * DT + c:3 * DT + c + 1])
            ffn(0)

            def out_of_banks(name, dst, tiles=2):
                for i, u, p, use in pairs(act, name):
                    act.wait_ge(product_done[p], use + 1)
                    for m in range(2):
                        last = nc.scalar.activation(dst(4 * i + 2 * u + m), banks[2 * p + m][:], ACT.Copy)
                    last.then_inc(bank_free[p], 1)

            def out_of_job(name, j, parts):
                p, use = one(name, j)
                act.wait_ge(product_done[p], use + 1)
                for dst, m, r, w in parts:
                    last = nc.scalar.activation(dst, banks[2 * p + m][0:r, 0:w], ACT.Copy)
                last.then_inc(bank_free[p], 1)

            def memory_kv(name):
                out_of_job(name, 0, [(k_mem[:, m, :], m, P, MEM) for m in range(2)])
                out_of_job(name, 1, [(v_mem[:, m, :], m, P, MEM) for m in range(2)])

            def attend(k):
                g0, groups = GROUPS_BEFORE[k], ATTENTION[k]

                def exps(g):
                    n = g0 + g
                    act.wait_ge(S["at_neg_max"], n + 1)
                    heads = groups[g]["heads"]
                    sink = groups[g].get("sink")
                    if sink is not None:
                        for e in range(2):
                            steps.did(nc.scalar.activation(stat(n, 6 + e), col("sinks", sink + e), ACT.Exp, bias=stat(n, 2 + e)))
                        steps.settle()
                    for e, (lo, w) in enumerate(heads):
                        part = probs[:, n % 3, lo:lo + w]
                        last = nc.scalar.activation(part, part, ACT.Exp, bias=stat(n, 2 + e), accum_out=stat(n, 4 + e))
                    last.then_inc(S["at_exp"], 1)

                def copies(g):
                    n = g0 + g
                    act.wait_ge(S["at_turned"], n + 1)
                    if n >= 2:
                        act.wait_ge(S["at_sums"], n - 1)
                    w = groups[g]["n"]
                    nc.scalar.activation(probs_turned[:, n % 2, 0:w], banks[6 + n % 2][:, 0:w], ACT.Copy).then_inc(S["at_copied"], 1)

                def outputs(g):
                    n = g0 + g
                    act.wait_ge(S["at_sums"], n + 1)
                    nc.scalar.activation(groups[g]["out"], banks[n // TB % 2][:], ACT.Copy).then_inc(S["at_out"], 1)

                for g in range(len(groups) + 3):
                    if g < len(groups):
                        exps(g)
                    if 2 <= g <= len(groups) + 1:
                        copies(g - 2)
                    if g >= 3 and (g - 3) % TB == TB - 1:
                        outputs(g - 3)

            act.wait_ge(S["mem_in"], 16)
            norm_act(act, "mem", memT)
            wait_emptied(act, "ffn0_down1")
            norm_act(act, "final0", xT)
            memory_kv("a_mem")
            act.wait_ge(S["norm_ready"], TILES_BEFORE["a_mix"])
            norm_act(act, "a_mix", xT)
            out_of_banks("a_q", lambda t: qkr[:, 0:8, :][:, t, :])
            out_of_banks("a_idx", lambda t: qkr[:, 9:17, :][:, t, :])
            out_of_job("a_keys", 0, [(qkr[0:48, 8, :], 0, 48, T), (qkr[:, 17, :], 1, P, T)])
            out_of_job("a_keys", 1, [(kv_low[:, m, :], m, P, T) for m in range(2)])
            out_of_job("a_qmem", 0, [(q_mem[:, m, :], m, P, T) for m in range(2)])
            wait_emptied(act, "a_qmem")
            norm_act(act, "kv", kv_low)
            p, use = one("a_uk", 0)
            for hd in range(A_HEADS):
                if hd < A_HEADS - 1:
                    act.wait_ge(S["k_made"], hd + 1)
                else:
                    act.wait_ge(product_done[p], use + 1)
                nc.scalar.activation(k_heads[:, hd, :], banks[(2 * p, 2 * p + 1, 6, 7)[hd % 4]][:],
                                     ACT.Copy).then_inc(S["k_taken"] if hd < A_HEADS - 1 else bank_free[p], 1)
            p, use = one("a_uv", 0)
            for n in range(2 * TB):
                b, half = divmod(n, 2)
                if n < 2 * TB - 1:
                    act.wait_ge(S["v_made"], n + 1)
                else:
                    act.wait_ge(product_done[p], use + 1)
                nc.scalar.activation(v_heads[:, b, half * T:(half + 1) * T], banks[2 * p + n % 2][:],
                                     ACT.Copy).then_inc(S["v_taken"] if n < 2 * TB - 1 else bank_free[p], 1)
            act.wait_ge(S["w_idx_turned"], 1)
            nc.scalar.activation(small[:, 0:TB * IDX_HEADS], banks[6][:, 0:TB * IDX_HEADS], ACT.Copy,
                                 scale=(IDX_HEADS * 64) ** -0.5).then_inc(S["w_idx_ready"], 1)
            n = 0
            for b in range(1, TB):
                for hd in range(IDX_HEADS):
                    act.wait_ge(S["idx_dots"], n + 1)
                    if n >= 3:
                        act.wait_ge(S["relu_used"], n - 2)
                    w = (b + 1) * P
                    nc.scalar.activation(relu_idx[:, n % 3, 0:w], banks[4 + n % 4][:, 0:w], ACT.Relu).then_inc(S["relu_ready"], 1)
                    n += 1
            attend(0)
            attend(1)
            split_first("ffn1_up0", 0)
            wait_emptied(act, "a_out")
            norm_act(act, "ffn1", xT)
            split_first("ffn1_up0", 1)
            norm_split(act, "ffn1")
            ffn(1)
            memory_kv("b_mem")
            wait_emptied(act, "ffn1_down1")
            norm_act(act, "b_mix", xT)
            out_of_banks("b_q", lambda t: qkr[:, 0:8, :][:, t, :])
            out_of_job("b_k", 0, [(qkr[:, 8 + m, :], m, P, T) for m in range(2)])
            p, use = one("b_v", 0)
            act.wait_ge(product_done[p], use + 1)
            for m in range(2):
                last = nc.scalar.activation(v_heads[:, 2 * m:2 * m + 2, 0:2 * P], banks[2 * p + m][:].rearrange("p (b n) -> p b n", b=2), ACT.Copy)
            last.then_inc(bank_free[p], 1)
            out_of_job("b_qmem", 0, [(q_mem[:, m, :], m, P, T) for m in range(2)])
            for kv in range(4):
                act.wait_ge(S["dup_made"], kv + 1)
                nc.scalar.activation(kw_heads[:, kv, :], banks[6 + kv % 2][:], ACT.Copy).then_inc(S["dup_ready"], 1)
            attend(2)
            attend(3)
            split_first("ffn2_up0", 0)
            wait_emptied(act, "b_out")
            norm_act(act, "ffn2", xT)
            split_first("ffn2_up0", 1)
            norm_split(act, "ffn2")
            ffn(2)
            wait_emptied(act, "ffn2_down1")
            norm_act(act, "last", xT)

        @block.vector
        def _(dve):
            steps = Steps(dve, dve_steps)
            dve.wait_ge(S["pos_in"], 16)
            dve.wait_ge(S["cons_in"], 16)
            pos, ang, turns = trig_tmp[:, 0, :], trig_tmp[:, 1, :], trig_tmp[:, 2, :]
            steps.did(nc.vector.tensor_copy(pos, pos_int))
            steps.settle()
            for k in range(4):
                out, quarter = trig[:, k, :], 0.25 if k % 2 == 0 else 0.0
                steps.did(nc.vector.tensor_scalar(ang, pos, con("inv32" if k < 2 else "inv64", 1), None, ALU.mult))
                steps.settle()
                steps.did(nc.vector.tensor_scalar(turns, ang, 1 / (2 * np.pi), quarter, ALU.mult, ALU.add))
                steps.settle()
                steps.did(nc.vector.tensor_scalar(turns, turns, ROUND, ROUND, ALU.add, ALU.subtract))
                for part in (TWO_PI_HI, TWO_PI_MID, TWO_PI_LO):
                    steps.settle()
                    steps.did(nc.vector.scalar_tensor_tensor(out=ang, in0=turns, scalar=-part, in1=ang, op0=ALU.mult, op1=ALU.add))
                steps.settle()
                if k % 2 == 0:
                    steps.did(nc.vector.tensor_scalar(ang, ang, np.pi / 2, None, ALU.add))
                    steps.settle()
                nc.vector.tensor_scalar(out, ang, PI_IN, -PI_IN, ALU.min, ALU.max).then_inc(S["angle_ready"], 1)
                dve.wait_ge(S["angle_ready"], k + 1)

            def gains(k, g):
                at = (3 * k + 1) * DT
                nc.vector.scalar_tensor_tensor(out=modg[:, k, :], in0=mod[:, at:at + DT], scalar=1.0,
                                               in1=cols[:, COL[g]:COL[g] + DT], op0=ALU.add, op1=ALU.mult).then_inc(S["modg_ready"], 1)
                dve.wait_ge(S["modg_ready"], k + 1)

            wait_emptied(dve, "ada_first")
            dve.wait_ge(S["cols_in"], 16)
            gains(0, "norm_mix_g")
            norm_dve(dve, steps, "mix", xT, hT, lambda c: modg[:, 0, c:c + 1], lambda c: mod[:, c:c + 1])
            dve.wait_ge(S["pads_zero"], 2)
            for i, u, p, use in pairs(dve, "glu"):
                dve.wait_ge(S["sig_ready"], 2 * i + u + 1)
                nc.vector.scalar_tensor_tensor(out=a_pad[:, 2 * i + u, KW - 1:], in0=banks[2 * p][:], scalar=col_at("b_glu", 16, 2 * i + u),
                                               in1=sig[:, p, :], op0=ALU.add, op1=ALU.mult).then_inc(bank_free[p], 1)
            qk_w = cols[:, COL["qk_w"]:COL["qk_w"] + 16 * QW].rearrange("p (a b) -> p a b", b=QW)
            for i, u, p, use in pairs(dve, "qk"):
                if u == 0:
                    steps.loop(i, 4 * (QW - 1))
                dve.wait_ge(bank_free[p], use + 2)
                for m in range(2):
                    t = 4 * i + 2 * u + m
                    dve.wait_ge(S["conv_acc_free"], t + 1)
                    steps.did(nc.vector.tensor_scalar(conv_acc[:, m, :], qk[:, t, 0:T], qk_w[:, t, 0:1], None, ALU.mult))
                    for k in range(1, QW):
                        steps.settle()
                        ins = nc.vector.scalar_tensor_tensor(out=conv_acc[:, m, :], in0=qk[:, t, k:k + T], scalar=qk_w[:, t, k:k + 1],
                                                             in1=conv_acc[:, m, :], op0=ALU.mult, op1=ALU.add)
                        if k < QW - 1:
                            steps.did(ins)
                        else:
                            ins.then_inc(S["conv_acc_ready"], 1)
            steps.end_loop(4)
            (pi, use_i), (pf, use_f) = one("gates", 0), one("gates", 1)
            dve.wait_ge(product_done[pi], use_i + 1)
            dve.wait_ge(product_done[pf], use_f + 1)
            steps.did(nc.vector.memset(ones_row, 1.0))
            dve.wait_ge(S["softplus_ready"], 1)
            steps.did(nc.vector.tensor_scalar(logf, banks[2 * pf][0:HEADS, :], cols[0:HEADS, COL["b_f"]:COL["b_f"] + 1], 0.0,
                                              ALU.add, ALU.min))
            steps.settle()
            steps.did(nc.vector.tensor_tensor(logf, logf, soft, ALU.subtract))
            steps.settle()
            nc.vector.tensor_tensor_scan(cum_f, ones_row, logf, 0.0, ALU.mult, ALU.add).then_inc(bank_free[pf], 1)
            dve.wait_ge(bank_free[pf], use_f + 2)
            nc.vector.scalar_tensor_tensor(out=g_row, in0=banks[2 * pi][0:HEADS, :], scalar=cols[0:HEADS, COL["b_i"]:COL["b_i"] + 1],
                                           in1=cum_f, op0=ALU.add, op1=ALU.subtract).then_inc(bank_free[pi], 1)
            dve.wait_ge(bank_free[pi], use_i + 2)
            steps.did(nc.vector.tensor_tensor_scan(neg_m, g_row, g_row, 0.0, ALU.max, ALU.max))
            steps.settle()
            nc.vector.scalar_tensor_tensor(out=em_row, in0=cum_f, scalar=-1.0, in1=neg_m, op0=ALU.mult,
                                           op1=ALU.subtract).then_inc(S["nm_ready"], 1)
            nc.vector.tensor_scalar(neg_m, neg_m, -1.0, None, ALU.mult).then_inc(S["nm_ready"], 1)
            dw_w = cols[:, COL["dw_w"]:COL["dw_w"] + DT * KW].rearrange("p (a b) -> p a b", b=KW)
            wait_emptied(dve, "glu")
            with dve.Fori(0, DT) as c:
                steps.loop(c, KW - 1)
                steps.did(nc.vector.tensor_scalar(conv[:, c, :], a_pad[:, c, 0:T], dw_w[:, c, 0:1], col_at("dw_b", DT, c),
                                                  ALU.mult, ALU.add))
                for k in range(1, KW):
                    steps.settle()
                    ins = nc.vector.scalar_tensor_tensor(out=conv[:, c, :], in0=a_pad[:, c, k:k + T], scalar=dw_w[:, c, k:k + 1],
                                                         in1=conv[:, c, :], op0=ALU.mult, op1=ALU.add)
                    if k < KW - 1:
                        steps.did(ins)
                    else:
                        ins.then_inc(S["conv_ready"], 1)
            steps.end_loop(DT)

            dve.wait_ge(S["merge_used"], 4 + 2)
            dve.wait_ge(S["g_cols_ready"], 1)
            for hd in range(HEADS):
                heads_out = lambda e: qk[:, 2 * hd + e, QW - 1:]
                dve.wait_ge(S["spread_ready"], 2 * hd + 1)

                def logits(j):
                    nc.vector.tensor_scalar(decay[:, j % 2, 0:T - j * P], banks[4][:, j * P:T], small[:, j * HEADS + hd:j * HEADS + hd + 1],
                                            0.0, ALU.add, ALU.min).then_inc(S["logit_ready"], 1)

                def weights(j):
                    n = TB * hd + j
                    if hd and j == 0:
                        dve.wait_ge(S["num_ready"], hd)
                    dve.wait_ge(S["score_ready"], n + 1)
                    dve.wait_ge(S["decay_ready"], n + 1)
                    steps.did(nc.vector.scalar_tensor_tensor(out=probs_t[:, j, j * P:T], in0=banks[6 + j % 2][:, 0:T - j * P],
                                                             scalar=(2 * P) ** -0.5, in1=decay[:, j % 2, 0:T - j * P],
                                                             op0=ALU.mult, op1=ALU.mult))
                    steps.settle()
                    diagonal = probs_t[:, j, j * P:(j + 1) * P]
                    nc.vector.tensor_tensor(diagonal, diagonal, con("causal_t"), ALU.mult).then_inc(S["weight_ready"], 1)

                logits(0)
                for j in range(1, TB):
                    logits(j)
                    weights(j - 1)
                weights(TB - 1)
                dve.wait_ge(S["abs_ready"], hd + 1)
                steps.did(nc.vector.tensor_tensor(den, abs_n, em_all, ALU.max))
                steps.settle()
                steps.did(nc.vector.reciprocal(den, den))
                steps.settle()
                for e in range(2):
                    nc.vector.tensor_tensor(heads_out(e), banks[e][:], den, ALU.mult).then_inc(S["head_ready"], 1)
                dve.wait_ge(S["mean_ready"], hd + 1)
                dve.wait_ge(S["head_ready"], 2 * hd + 2)
                for e in range(2):
                    nc.vector.tensor_tensor(heads_out(e), heads_out(e), banks[3][:], ALU.subtract).then_inc(S["dev_ready"], 1)
                dve.wait_ge(S["head_root"], hd + 1)
                steps.did(nc.vector.reciprocal(rstd[:], rstd[:]))
                steps.settle()
                dve.wait_ge(S["dev_ready"], 2 * hd + 2)
                for e in range(2):
                    nc.vector.scalar_tensor_tensor(out=heads_out(e), in0=heads_out(e), scalar=col("mlstm_g", 2 * hd + e), in1=rstd[:],
                                                   op0=ALU.mult, op1=ALU.mult).then_inc(S["hm_ready"], 1)

            dve.wait_ge(S["ln_mean"], 1)
            for c in range(DT):
                nc.vector.tensor_tensor(conv[:, c, :], conv[:, c, :], banks[4][:], ALU.subtract).then_inc(S["ln_dev"], 1)
            dve.wait_ge(S["ln_root"], 1)
            steps.did(nc.vector.reciprocal(rstd[:], rstd[:]))
            steps.settle()
            dve.wait_ge(S["ln_dev"], DT)
            for c in range(DT):
                nc.vector.scalar_tensor_tensor(out=conv[:, c, :], in0=conv[:, c, :], scalar=col("ln_g", c), in1=rstd[:],
                                               op0=ALU.mult, op1=ALU.mult).then_inc(S["ln_scaled"], 1)

            def residual(name, tiles, gate=None):
                for i, u, p, use in pairs(dve, name):
                    dve.wait_ge(product_done[p], use + 1)
                    for m in range(tiles):
                        t = tiles * (2 * i + u) + m
                        if gate is None:
                            last = nc.vector.tensor_tensor(xT[:, t, :], xT[:, t, :], banks[2 * p + m][:], ALU.add)
                        else:
                            g = mod[:, gate * DT:(gate + 1) * DT].rearrange("p (a b) -> p a b", b=1)[:, t, :]
                            last = nc.vector.scalar_tensor_tensor(out=xT[:, t, :], in0=banks[2 * p + m][:], scalar=g, in1=xT[:, t, :],
                                                                  op0=ALU.mult, op1=ALU.add)
                    last.then_inc(bank_free[p], 1)

            wait_emptied(dve, "ada_rest")
            gains(1, "norm_ffn_g")
            residual("mix_out", 2, 2)
            wait_emptied(dve, "mix_out")
            norm_dve_split(dve, steps, "ffn0", xT, lambda c: modg[:, 1, c:c + 1], lambda c: mod[:, 3 * DT + c:3 * DT + c + 1])

            def hidden(n, t, tiles, p, use):
                dve.wait_ge(S["act_gate"], n + 1)
                dve.wait_ge(S["hid_ready"], n + 1)
                nc.vector.tensor_tensor(hid_raw[:, p, :], up_gate[:, p, :], banks[2 * p + 1][:], ALU.mult).then_inc(bank_free[p], 1)
                dve.wait_ge(S["hid_hi_ready"], n + 1)
                nc.vector.tensor_tensor(hid[:, 1, 0:tiles, :][:, t, :], hid_raw[:, p, :], hid[:, 0, 0:tiles, :][:, t, :].bitcast(F32),
                                        ALU.subtract).then_inc(S["hid_ready"], 1)

            for half, (t0, tiles) in enumerate(HALVES):
                for i, u, p, use in pairs(dve, f"ffn0_up{half}"):
                    hidden(t0 + 2 * i + u, 2 * i + u, tiles, p, use)
                residual(f"ffn0_down{half}", 1, 5)
            norm_dve(dve, steps, "mem", memT, memT, lambda c: col("g_mem", c))
            wait_emptied(dve, "ffn0_down1")
            norm_dve(dve, steps, "final0", xT, xT, lambda c: col("final_g", c))
            dve.wait_ge(S["norm_ready"], TILES_BEFORE["a_mix"])
            norm_dve(dve, steps, "a_mix", xT, hT, lambda c: col("g_mix", c))

            def rope(tiles, table, rows, done):
                for k, t in enumerate(tiles):
                    n = done + k
                    dve.wait_ge(S["rot_ready"], n + 1)
                    nc.vector.tensor_tensor(rot_sin[0:rows, n % 2, :], banks[4 + n % 2][0:rows, :], trig[0:rows, table + 1, :],
                                            ALU.mult).then_inc(S["rot_sin_ready"], 1)
                    dve.wait_ge(S["rot_sin_ready"], n + 1)
                    dve.wait_ge(S["rot_cos_ready"], n + 1)
                    nc.vector.tensor_tensor(qkr[0:rows, t, :], rot_cos[0:rows, n % 2, :], rot_sin[0:rows, n % 2, :],
                                            ALU.add).then_inc(S["rope_ready"], 1)

            def attend(k):
                g0, groups = GROUPS_BEFORE[k], ATTENTION[k]

                def logits(g):
                    n = g0 + g
                    grp = groups[g]
                    heads = grp["heads"]
                    dve.wait_ge(S["at_scores"], n + 1)
                    if n >= 3:
                        dve.wait_ge(S["at_turned"], n - 2)
                    w, ne = grp["n"], len(heads)
                    by_head = probs[:, n % 3, 0:w].rearrange("p (e k) -> p e k", e=ne)
                    for e in range(ne):
                        src = score_bank(n, e)[:, 0:w // ne]
                        if grp["mask"] is None:
                            ins = nc.vector.tensor_scalar(by_head[:, e, :], src, grp["scale"], None, ALU.mult)
                        else:
                            ins = nc.vector.scalar_tensor_tensor(out=by_head[:, e, :], in0=src, scalar=grp["scale"], in1=grp["mask"],
                                                                 op0=ALU.mult, op1=ALU.add)
                    ins.then_inc(S["at_logits"], 1)
                    dve.wait_ge(S["at_logits"], n + 1)
                    steps.did(nc.vector.tensor_reduce(stat(n, 0, ne), by_head, AX, ALU.max))
                    steps.settle()
                    sink = grp.get("sink")
                    if sink is not None:
                        steps.did(nc.vector.tensor_tensor(stat(n, 0, 2), stat(n, 0, 2), cols[:, COL["sinks"] + sink:COL["sinks"] + sink + 2], ALU.max))
                        steps.settle()
                    nc.vector.tensor_scalar(stat(n, 2, ne), stat(n, 0, ne), -1.0, None, ALU.mult).then_inc(S["at_neg_max"], 1)

                def weights(g):
                    n = g0 + g
                    heads = groups[g]["heads"]
                    ne = len(heads)
                    dve.wait_ge(S["at_exp"], n + 1)
                    if groups[g].get("sink") is not None:
                        steps.did(nc.vector.tensor_tensor(stat(n, 4, 2), stat(n, 4, 2), stat(n, 6, 2), ALU.add))
                        steps.settle()
                    steps.did(nc.vector.reciprocal(stat(n, 0, ne), stat(n, 4, ne)))
                    steps.settle()
                    for e, (lo, w) in enumerate(heads):
                        part = probs[:, n % 3, lo:lo + w]
                        last = nc.vector.tensor_scalar(part, part, stat(n, e), None, ALU.mult)
                    last.then_inc(S["at_probs"], 1)

                for g in range(len(groups) + 1):
                    if g < len(groups):
                        logits(g)
                    if g >= 1:
                        weights(g - 1)

            def ffn(k):
                steps.did(nc.vector.memset(up_pad[:, :, 0:2], 0.0))
                steps.settle()
                for half, (t0, tiles) in enumerate(HALVES):
                    at = COL["fconv_w"] + ((k - 1) * FT + t0) * 3
                    w3 = cols[:, at:at + 3 * tiles].rearrange("p (a b) -> p a b", b=3)
                    at = COL["fconv_b"] + (k - 1) * FT + t0
                    b3 = cols[:, at:at + tiles].rearrange("p (a b) -> p a b", b=1)
                    for i, u, p, use in pairs(dve, f"ffn{k}_up{half}"):
                        if u == 0:
                            steps.loop(i, 4)
                        t = 2 * i + u
                        n = FT * k + t0 + t
                        dve.wait_ge(S["conv3_in"], n - FT + 1)
                        acc = up_acc[:, p, :]
                        steps.did(nc.vector.tensor_scalar(acc, up_pad[:, p, 0:T], w3[:, t, 0:1], b3[:, t, :], ALU.mult, ALU.add))
                        steps.settle()
                        steps.did(nc.vector.scalar_tensor_tensor(out=acc, in0=up_pad[:, p, 1:T + 1], scalar=w3[:, t, 1:2], in1=acc,
                                                                 op0=ALU.mult, op1=ALU.add))
                        steps.settle()
                        nc.vector.scalar_tensor_tensor(out=acc, in0=up_pad[:, p, 2:T + 2], scalar=w3[:, t, 2:3], in1=acc,
                                                       op0=ALU.mult, op1=ALU.add).then_inc(S["conv3_ready"], 1)
                        hidden(n, t, tiles, p, use)
                    steps.end_loop(tiles // 2)
                    residual(f"ffn{k}_down{half}", 1)

            norm_dve(dve, steps, "kv", kv_low, kv_low, lambda c: col("kv_g", c))
            rope([8], 0, 32, 0)
            rope(range(8), 0, 32, 1)
            rope(range(9, 18), 2, 80, 9)
            dve.wait_ge(S["w_idx_ready"], 1)
            n = 0
            for b in range(1, TB):
                w = (b + 1) * P
                left = scores_left[:, 0:w]
                for hd in range(IDX_HEADS):
                    dve.wait_ge(S["relu_ready"], n + 1)
                    wcol = small[:, b * IDX_HEADS + hd:b * IDX_HEADS + hd + 1]
                    if hd == 0:
                        ins = nc.vector.tensor_scalar(left, relu_idx[:, n % 3, 0:w], wcol, None, ALU.mult)
                    else:
                        ins = nc.vector.scalar_tensor_tensor(out=left, in0=relu_idx[:, n % 3, 0:w], scalar=wcol, in1=left,
                                                             op0=ALU.mult, op1=ALU.add)
                    ins.then_inc(S["relu_used"], 1)
                    n += 1
                    dve.wait_ge(S["relu_used"], n)
                diagonal = left[:, b * P:w]
                steps.did(nc.vector.tensor_tensor(diagonal, diagonal, con("causal"), ALU.mult))
                steps.settle()
                steps.did(nc.vector.tensor_tensor(diagonal, diagonal, con("after_fill"), ALU.add))
                for _ in range(TOPK // 8):
                    steps.settle()
                    steps.did(nc.vector.max(small[:, 96:104], left))
                    steps.settle()
                    steps.did(nc.vector.match_replace(left, small[:, 96:104], left, CHOSEN))
                steps.settle()
                steps.did(nc.vector.tensor_scalar(chosen_at(b), left, CHOSEN, None, ALU.is_equal))
                steps.settle()
                steps.did(nc.vector.tensor_scalar(chosen_at(b), chosen_at(b), -1.0, -NEG, ALU.add, ALU.mult))
            steps.settle()
            attend(0)
            attend(1)
            residual("a_out", 2)
            wait_emptied(dve, "a_out")
            norm_dve_split(dve, steps, "ffn1", xT, lambda c: col("g_ffn", c))
            ffn(1)
            wait_emptied(dve, "ffn1_down1")
            norm_dve(dve, steps, "b_mix", xT, hT, lambda c: col("g_mix", DT + c))
            rope([8, 9], 2, 80, 18)
            rope(range(8), 2, 80, 20)
            attend(2)
            attend(3)
            residual("b_out", 2)
            wait_emptied(dve, "b_out")
            norm_dve_split(dve, steps, "ffn2", xT, lambda c: col("g_ffn", DT + c))
            ffn(2)
            wait_emptied(dve, "ffn2_down1")
            norm_dve(dve, steps, "last", xT, xT, lambda c: col("g_last", c))

        @block.gpsimd
        def _(pool):
            steps = Steps(pool, pool_steps)
            nc.gpsimd.memset(a_pad[:, :, 0:KW - 1], 0.0).then_inc(S["pads_zero"], 1)
            nc.gpsimd.memset(qk[:, :, 0:QW - 1], 0.0).then_inc(S["pads_zero"], 1)
            for j in range(4):
                p, use = one("merge_mlstm", j)
                pool.wait_ge(bank_free[p], use + 2)
                for m in range(2):
                    t = o_gate[:, 2 * j + m, :]
                    last = nc.gpsimd.tensor_tensor(t, t, merge_gate[:, 2 * (j % 2) + m, :], ALU.mult)
                last.then_inc(S["merge_used"], 1)
            pool.wait_ge(S["merge_used"], 4 + 2)
            for t in range(2 * HEADS):
                pool.wait_ge(S["hm_ready"], t + 1)
                steps.did(nc.gpsimd.tensor_tensor(qk[:, t, QW - 1:], qk[:, t, QW - 1:], o_gate[:, t, :], ALU.mult))
            steps.settle()
            for j in range(4):
                p, use = one("merge_conv", j)
                pool.wait_ge(bank_free[p], use + 2)
                for m in range(2):
                    y = y_conv[:, 2 * j + m, :]
                    last = nc.gpsimd.tensor_tensor(y, y, merge_gate[:, 2 * (j % 2) + m, :], ALU.mult)
                last.then_inc(S["merge_used"], 1)
                pool.wait_ge(S["merge_used"], 4 + 2 + j + 1)
                for m in range(2):
                    t = 2 * j + m
                    nc.gpsimd.tensor_tensor(y_conv[:, t, :], y_conv[:, t, :], qk[:, t, QW - 1:], ALU.add).then_inc(S["mixed_ready"], 1)
            def split_weights(name):
                n = SIZE[name]
                for i, u, p, use in pairs(pool, name):
                    pool.wait_ge(hi_ready[p], SPLITS_BEFORE[name] + i + 1)
                    nc.gpsimd.tensor_tensor(w_split[p][:, 1, 0:n], slot(p, 1, n)[:, 0, :], w_split[p][:, 0, 0:n].bitcast(F32),
                                            ALU.subtract).then_inc(lo_ready[p], 1)

            def ffn(k):
                for name, _ in ffn_stages(k):
                    split_weights(name)

            ffn(0)
            p, use = one("a_uk", 0)
            pool.wait_ge(product_done[p], use)
            nc.gpsimd.memset(slot(p, 2, D).rearrange("p c (h n) -> p c h n", n=P)[:, :, :, 0:32], 0.0).then_inc(S["uk_pad_zero"], 1)

            def rope(tiles, table, rows, done):
                for k, t in enumerate(tiles):
                    n = done + k
                    if n >= 2:
                        pool.wait_ge(S["rope_ready"], n - 1)
                    nc.gpsimd.tensor_tensor(rot_cos[0:rows, n % 2, :], qkr[0:rows, t, :], trig[0:rows, table, :],
                                            ALU.mult).then_inc(S["rot_cos_ready"], 1)

            wait_emptied(pool, "a_qmem")
            rope([8], 0, 32, 0)
            rope(range(8), 0, 32, 1)
            rope(range(9, 18), 2, 80, 9)
            ffn(1)
            wait_emptied(pool, "b_qmem")
            rope([8, 9], 2, 80, 18)
            rope(range(8), 2, 80, 20)
            ffn(2)




def kernel(**inputs):
    import concourse.bacc as bacc
    from concourse.bass_utils import run_bass_kernel_spmd

    a = {k: np.ascontiguousarray(v) for k, v in inputs.items()}
    tiles = lambda v: v.reshape(-1, P).T

    b_in = a["b_in"][0]
    gates0 = 6 * D
    merge0 = gates0 + 2 * HEADS
    four = lambda v: np.pad(v.reshape(HEADS, 1), ((0, P - HEADS), (0, 0)))
    by_tap = lambda w: w.reshape(w.shape[0], -1, P).transpose(2, 1, 0).reshape(P, -1)
    parts = {
        "b_ada": tiles(a["b_ada"]), "c": tiles(a["c"]), "norm_mix_g": tiles(a["norm_mix_g"]), "b_glu": tiles(b_in[:2 * D]),
        "b_qk": tiles(b_in[2 * D:4 * D]), "b_o": tiles(b_in[5 * D:6 * D]), "b_merge": tiles(b_in[merge0:]),
        "dw_w": by_tap(a["conv_dw_w"][0]), "dw_b": tiles(a["conv_dw_b"]), "ln_g": tiles(a["conv_ln_g"]), "ln_b": tiles(a["conv_ln_b"]),
        "b_pw": tiles(a["b_conv_pw"]), "qk_w": by_tap(a["qk_conv_w"][0]), "qk_b": tiles(a["qk_conv_b"]),
        "mlstm_g": tiles(a["mlstm_norm_g"]), "norm_ffn_g": tiles(a["norm_ffn_g"]), "final_g": tiles(a["final_norm_g"]),
        "g_mix": tiles(a["g_mix_2"]), "g_ffn": tiles(a["g_ffn_2"]), "g_mem": tiles(a["g_mem_2"]), "g_last": tiles(a["g_final_2"]),
        "kv_g": tiles(a["a_kv_norm_2"]),
        "fconv_w": np.concatenate([by_tap(w) for w in a["f_conv_w_2"]], axis=1), "fconv_b": tiles(a["f_conv_b_2"]),
        "sinks": np.broadcast_to(a["b_sinks_2"][0], (P, B_HEADS)),
        "b_i": four(b_in[gates0:gates0 + HEADS]), "b_f": four(b_in[gates0 + HEADS:merge0]),
    }
    columns = np.concatenate([parts[name] for name, _ in COLUMNS], axis=1)
    assert columns.shape == (P, NCOL)

    feeds = {
        "columns": columns, "constants": constants(), "x": a["x"][0].T, "v_bias": b_in[None, 4 * D:5 * D],
        "mem": a["mem_2"][0].T, "positions": np.broadcast_to(a["positions_2"], (P, T)),
    }
    for name in ("w_ada", "w_in", "w_conv_pw", "w_out", "w_ffn_up", "w_ffn_down", "w_mem_kv_2", "a_w_in_2", "a_w_uk_2", "a_w_uv_2",
                 "a_w_out_2", "b_w_in_2", "b_w_out_2", "f_w_up_2", "f_w_down_2"):
        feeds[name] = a[name]
    feeds = {k: np.ascontiguousarray(v) for k, v in feeds.items()}

    nc = bacc.Bacc("TRN2", target_bir_lowering=False, num_devices=1)
    io = {k: nc.dram_tensor(f"in_{k}", v.shape, mybir.dt.from_np(v.dtype), kind="ExternalInput").ap() for k, v in feeds.items()}
    io["out"] = nc.dram_tensor("out", (D, T), F32, kind="ExternalOutput").ap()
    build(nc, io)
    r = run_bass_kernel_spmd(nc, [{f"in_{k}": v for k, v in feeds.items()}], core_ids=[0])
    return np.ascontiguousarray(r.results[0]["out"].T)[None]
```

```python
from contextlib import ExitStack

import concourse.bass as bass
import concourse.mybir as mybir
import numpy as np

F32 = mybir.dt.float32
F32R = mybir.dt.float32r
I32 = mybir.dt.int32
ACT = mybir.ActivationFunctionType
ALU = mybir.AluOpType
AX = mybir.AxisListType.X

P = 128
T = 512
TB = T // P
D = 1024
DT = D // P
HEADS = 4
KW = 31
QW = 4
FF = 2816
FT = FF // P
MEM = 256
R = 256
A_HEADS = 8
IDX_HEADS = 16
TOPK = 128
B_HEADS = 16
EPS = 1e-6
NEG = -1e30
OUTSIDE = -3.0e38
CHOSEN = -3.2e38
SLOT = DT * 2 * P
OUT_K = 10

HALVES = ((0, 12), (12, FT - 12))


def ffn_stages(k):
    return [(f"ffn{k}_{what}{half}", jobs) for half, (_, n) in enumerate(HALVES) for what, jobs in (("up", n), ("down", DT))]


STAGES = [
    ("glu", 8), ("qk", 8), ("gates", 2), ("v", 4), ("o", 4), 
    ("merge_mlstm", 4), ("merge_conv", 4), ("conv_pw", 4), ("mix_out", 4), *ffn_stages(0),
    ("a_mem", 2), ("a_idx", 4), ("a_keys", 1), ("a_kv", 1), ("a_qmem", 1), ("a_q", 4), ("a_uk", 1), ("a_uv", 1),
    ("a_out", 8), *ffn_stages(1),
    ("b_mem", 2), ("b_q", 4), ("b_k", 1), ("b_v", 1), ("b_qmem", 1), ("b_out", 8), *ffn_stages(2),
]
NO_SLOT = {"a_mem", "b_mem"}
PIECES = {"a_mem": 0, "b_mem": 0, "a_keys": 4, "a_uk": 2, "glu": 2, **{f"ffn{k}_up{half}": 2 for k in range(3) for half in range(2)}}
SPLIT = {"a_out", "b_out", "glu", "qk", "a_q", "a_idx", "a_keys", "a_kv", "a_qmem", "b_q", "b_k", "b_v", "b_qmem"} | {name for k in range(3) for name, _ in ffn_stages(k)}


def job_table():
    first, loaded, split, before, n, count = {}, {}, [], [], 0, [0, 0]
    for name, jobs in STAGES:
        first[name] = n
        for j in range(jobs):
            count[n % 2] += 16 * PIECES.get(name, 1)
            loaded[n] = count[n % 2]
            before.append(sum(split[n % 2::2]))
            split.append(name in SPLIT)
            n += 1
    return first, loaded, split, before


FIRST, LOADED, JOB_SPLIT, SPLITS_BEFORE = job_table()
JOB_STAGE = [name for name, jobs in STAGES for _ in range(jobs)]


def slot_before(n):
    n -= 2
    while JOB_STAGE[n] in NO_SLOT:
        n -= 2
    return n


def slot_after(n):
    n += 2
    while n < len(JOB_STAGE) and JOB_STAGE[n] in NO_SLOT:
        n += 2
    return n if n < len(JOB_STAGE) else None

COLUMNS = [("b_ada", 48), ("c", 8), ("norm_mix_g", 8), ("b_glu", 16), ("b_qk", 16), ("b_o", 8), ("b_merge", 16),
           ("dw_w", DT * KW), ("dw_b", 8), ("ln_g", 8), ("ln_b", 8), ("b_pw", 8), ("qk_w", 16 * QW), ("qk_b", 16),
           ("mlstm_g", 8), ("norm_ffn_g", 8), ("final_g", 8), ("g_mix", 16), ("g_ffn", 16), ("g_mem", 8),
           ("g_last", 8), ("kv_g", 2), ("fconv_w", 2 * FT * 3), ("fconv_b", 2 * FT), ("sinks", B_HEADS),
           ("b_i", 1), ("b_f", 1)]
COL, NCOL = {}, 0
for _name, _n in COLUMNS:
    COL[_name] = NCOL
    NCOL += _n

CONSTS = [("ident", P), ("rot32", P), ("rot64", P), ("dup_lo", P), ("dup_hi", P), ("one", P), ("mean_d", P), ("mean_r", P),
          ("head_row", HEADS * P), ("causal", P), ("causal_bias", P), ("after_fill", P), ("causal_t", P), ("band", 2 * P),
          ("inv32", 1), ("inv64", 1), ("eps", 1), ("zero", 1)]
CON, NCON = {}, 0
for _name, _n in CONSTS:
    CON[_name] = NCON
    NCON += _n


def constants():
    k = np.zeros((P, NCON), np.float32)
    put = lambda name, a: k[:, CON[name]:CON[name] + a.shape[1]].__setitem__(slice(0, a.shape[0]), a)
    put("ident", np.eye(P))
    for name, half, heads in (("rot32", 16, 1), ("rot64", 8, 2)):
        m = np.zeros((P, P))
        for h in range(heads):
            for j in range(half):
                m[64 * h + half + j, 64 * h + j] = -1.0
                m[64 * h + j, 64 * h + half + j] = 1.0
        put(name, m)
    for name, low in (("dup_lo", 0), ("dup_hi", 64)):
        m = np.zeros((P, P))
        m[low + np.arange(P) % 64, np.arange(P)] = 1.0
        put(name, m)
    put("one", np.ones((P, P)))
    put("mean_d", np.full((P, P), 1.0 / D))
    put("mean_r", np.full((P, P), 1.0 / R))
    put("head_row", np.repeat(np.eye(HEADS), P, axis=1))
    q, s = np.arange(P)[:, None], np.arange(P)[None, :]
    put("causal", (s <= q).astype(np.float32))
    put("causal_bias", np.where(s <= q, 0.0, NEG))
    put("after_fill", np.where(s <= q, 0.0, OUTSIDE))
    put("causal_t", (s >= q).astype(np.float32))
    band = np.concatenate([np.where(s > q, 0.0, NEG), np.where(s <= q, 0.0, NEG)], axis=1)
    put("band", band)
    for name, rot, period in (("inv32", 32, P), ("inv64", 16, 64)):
        inv = np.float32(500000.0) ** (-np.arange(0, rot, 2, dtype=np.float32) / np.float32(rot))
        col = np.zeros((P, 1), np.float32)
        for p in range(P):
            if p % period < rot:
                col[p] = inv[p % period % (rot // 2)]
        put(name, col)
    put("eps", np.full((P, 1), EPS))
    return k


TWO_PI_HI = 6.28125
TWO_PI_MID = 4058 / 2 ** 21
TWO_PI_LO = float(2 * np.pi - TWO_PI_HI - TWO_PI_MID)
ROUND = 1.5 * 2 ** 23
LARGEST_LOG = 42.0
PI_IN = 3.1415925


class Steps:

    def __init__(self, eng, sem):
        self.eng, self.sem, self.base, self.n = eng, sem, 0, 0

    def did(self, ins):
        ins.then_inc(self.sem, 1)
        self.n += 1

    def settle(self, but=0):
        if not isinstance(self.base, int) or self.n > but:
            self.eng.wait_ge(self.sem, self.base + self.n - but)

    def loop(self, turn, per_turn):
        self.start, self.per_turn = self.n, per_turn
        self.base, self.n = turn * per_turn + self.start, 0

    def end_loop(self, turns):
        assert self.n == self.per_turn, (self.n, self.per_turn)
        self.base, self.n = 0, self.start + turns * self.per_turn


def build(nc, io):
    ctx = ExitStack()
    with ctx:
        def sb(name, shape, dt=F32):
            return ctx.enter_context(nc.sbuf_tensor(name, shape, dt))

        def sem(name):
            return ctx.enter_context(nc.semaphore(name))

        xT = sb("xT", [P, DT, T])
        hT_at = nc.sbuf_base
        hT = sb("hT", [P, DT, T])
        wslots = sb("wslots", [P, 2 * SLOT])
        cols = sb("cols", [P, NCOL])
        cons = sb("cons", [P, NCON])
        trig = sb("trig", [P, 4, T])
        rstd = sb("rstd", [P, T])
        square = sb("square", [P, 2, T])
        mod = sb("mod", [P, 6 * DT])
        modg = sb("modg", [P, 2, DT])
        silu_c = sb("silu_c", [P, DT])
        small = sb("small", [P, 128])
        ARENA = 33436
        arena_at = nc.sbuf_base
        arena = sb("arena", [P, ARENA])

        taken = [0]

        def region(*shape, at=None):
            if at is not None:
                taken[0] = at
            a = taken[0]
            n = int(np.prod(shape))
            taken[0] += n
            assert taken[0] <= ARENA, taken[0]
            v = arena[:, a:a + n]
            return v if len(shape) == 1 else v.rearrange("p (a b) -> p a b", b=shape[1])

        a_pad = region(DT, T + KW - 1, at=0)
        y_conv = arena[:, 0:DT * T].rearrange("p (a b) -> p a b", b=T)
        conv = region(DT, T)
        qk = region(16, T + QW - 1)
        v_tok = region(TB, D)
        o_gate = region(DT, T)
        probs_t = region(TB, T)
        sig = probs_t[:, 0:2, :]
        conv_acc = probs_t[:, 2:4, :]
        merge_gate = probs_t
        conv_gate = y_conv
        soft, logf = sig[0:HEADS, 0, :], sig[0:HEADS, 1, :]
        ada_rest_at = taken[0]
        decay = region(2, T)
        tail = region(3, T)
        ones_row = tail[0:HEADS, 0, :]
        v_bias = tail[0:1, 1:3, :].rearrange("p a b -> p (a b)")
        den = tail[:, 0:2, :]
        n_squared = tail[:, 2, :]
        rows = region(4, T)
        cum_f, g_row, neg_m, em_row = (rows[0:HEADS, i, :] for i in range(4))
        trig_tmp = rows[:, 0:3, :]
        pos_int = rows[:, 3, :].bitcast(I32)
        ada_sums = tail[:, 2, :].rearrange("p (u n) -> p u n", n=2 * P)
        ada_first_sums = probs_t
        ada_first = [arena[:, k * DT * T:(k + 1) * DT * T].rearrange("p (c n) -> p c n", n=T) for k in range(4)]
        ada_rest = [arena[:, at:at + DT * 2 * P].rearrange("p (c n) -> p c n", n=2 * P)
                    for at in (ada_rest_at, ada_rest_at + 5 * T)]

        def split_at(name, shape, at):
            return nc.alloc_sbuf_tensor_at(name, shape, F32R, offset=at)

        def split_region(name, *shape):
            at = arena_at + 4 * taken[0]
            region(int(np.prod(shape)))
            return split_at(name, [P, *shape], at)

        CONV_AT, QK_AT, V_AT, PROBS_AT = DT * (T + KW - 1), DT * (2 * T + KW - 1), DT * (2 * T + KW - 1) + 16 * (T + QW - 1), ada_rest_at - TB * T
        taken[0] = CONV_AT
        h_split = [split_at("h_hi", [P, DT, T], hT_at), split_region("h_lo", DT, T)]
        taken[0] = V_AT
        w_split = [split_region(f"w_split{p}", 2, DT * 2 * P) for p in range(2)]

        taken[0] = 0
        up_gate = region(2, T)
        hid_raw = region(2, T)
        up_acc = region(2, T)
        up_pad = region(2, T + 2)
        taken[0] = QK_AT
        hid = [split_region("hid_hi", HALVES[0][1], T)]
        taken[0] = PROBS_AT
        hid.append(split_region("hid_lo", HALVES[0][1], T))
        memT = region(DT, MEM)

        RING = 4
        kv_low = region(2, T, at=0)
        q_mem = region(2, T)
        mem_out_at = arena_at + 4 * taken[0]
        mem_out = region(2, T)
        mem_weights = arena[:, 0:DT * 4 * P].rearrange("p (c n) -> p c n", n=4 * P)
        probs = region(RING, T + 2, at=CONV_AT)
        probs_turned = region(3, T)
        q_tiles = region(8, T, at=QK_AT)
        idx_tiles = region(8, T)
        k_heads = region(A_HEADS, T, at=V_AT)
        v_heads = region(TB, D)
        key_tiles = region(2, T, at=PROBS_AT)
        relu_idx = region(3, T)
        chosen = region(sum(P * (b + 1) for b in range(1, TB)))
        k_mem = region(2, MEM)
        v_mem = region(2, MEM)
        rot_cos, rot_sin = relu_idx[:, 0:2, :], mem_out
        chosen_at = lambda b: chosen[:, P * (b * (b + 1) // 2 - 1):P * ((b + 1) * (b + 2) // 2 - 1)]
        kw_heads = k_heads
        v_groups = region(TB, 2 * P, at=QK_AT + 2 * DT * T - TB * 2 * P)
        out_split = [h_split[0], split_at("out_lo", [P, DT, T], arena_at + 4 * QK_AT)]
        mem_split = [split_at("mem_hi", [P, 2, T], mem_out_at), split_at("mem_lo", [P, 2, T], mem_out_at - 4 * 2 * T)]
        w_split_out = [split_at(f"w_split_out{p}", [P, 2, OUT_K * P], arena_at + 4 * at) for p, at in enumerate((QK_AT + DT * T, PROBS_AT))]
        split_of = lambda name, p: (w_split_out if name in ("a_out", "b_out") else w_split)[p]
        KEYS = (8, 17)

        def tile(t):
            return q_tiles[:, t, :] if t < 8 else key_tiles[:, KEYS.index(t), :] if t in KEYS else idx_tiles[:, t - 9, :]

        banks = [ctx.enter_context(nc.psum_tensor(f"bank{i}", [P, T], F32)) for i in range(8)]

        weights_in = [sem("weights_in0"), sem("weights_in1")]
        ada_first_in = [sem(f"ada_first_in{k}") for k in range(4)]
        ada_summed = [sem("ada_summed0"), sem("ada_summed1")]
        ada_in = [sem("ada_in0"), sem("ada_in1")]
        ada_used = [sem("ada_used0"), sem("ada_used1")]
        hi_ready = [sem("hi_ready0"), sem("hi_ready1")]
        lo_ready = [sem("lo_ready0"), sem("lo_ready1")]
        product_done = [sem("product_done0"), sem("product_done1")]
        bank_free = [sem("bank_free0"), sem("bank_free1")]
        act_steps, dve_steps, pool_steps = sem("act_steps"), sem("dve_steps"), sem("pool_steps")
        S = {n: sem(n) for n in (
            "x_in ada_scaled ada_last_summed ada_first_step ada_first_summed ada_first_done gate_cum gate_ready h_whole cols_in cons_in pos_in vbias_in mem_in out_written pads_zero silu_c_ready modg_ready angle_ready trig_ready "
            "square_ready square_used root_ready norm_ready norm_scaled norm_hi hid_hi_ready hid_ready sig_ready conv_acc_ready conv_acc_free qk_ready "
            "softplus_ready g_turned decay_ready g_cols_ready nm_ready em_ready merge_used o_ready "
            "spread_ready logit_ready score_ready weight_ready num_ready num_taken em_copied den_ready v_centred "
            "dev_square var_ready var_used head_root hm_ready conv_ready "
            "ln_mean ln_dev ln_square ln_square_used ln_root ln_scaled ln_ready yconv_ready mixed_ready "
            "act_gate conv3_in conv3_ready uk_pad_zero rot_ready rot_cos_ready rot_sin_ready rope_ready k_made k_taken "
            "v_made v_taken w_idx_turned w_idx_ready idx_dots relu_ready relu_used chosen_ready dup_made dup_ready "
            "at_scores at_logits at_neg_max at_exp at_probs at_turned at_copied at_sums at_out at_low mem_weights_in").split()}

        def col(name, i):
            return cols[:, COL[name] + i:COL[name] + i + 1]

        def col_at(name, n, r):
            return cols[:, COL[name]:COL[name] + n].rearrange("p (a b) -> p a b", b=1)[:, r, :]

        def con(name, n=P, p=P):
            return cons[0:p, CON[name]:CON[name] + n]

        def slot(p, kc, n):
            return wslots[:, p * SLOT:p * SLOT + kc * n].rearrange("p (c n) -> p c n", n=n)

        JOBS = dict(STAGES)
        SIZE = {name: (OUT_K * P if name in ("a_out", "b_out") else DT * 2 * P) for name in SPLIT}
        SIZE |= {f"ffn{k}_{what}{half}": n for k in range(3) for half, (_, tiles) in enumerate(HALVES)
                for what, n in (("up", DT * 2 * P), ("down", tiles * P))}

        def pairs(eng, name, first=0, end=None):
            n0 = FIRST[name]
            assert JOBS[name] % 2 == 0
            with eng.Fori(first, JOBS[name] // 2 if end is None else end) as i:
                for u in range(2):
                    yield i, u, (n0 + u) % 2, (n0 + u) // 2 + i

        def turn_of(name, i):
            for u in range(2):
                n = FIRST[name] + u
                yield i, u, n % 2, n // 2 + i

        def one(name, j):
            n = FIRST[name] + j
            return n % 2, n // 2

        def weights_of(name, u, i):
            n = FIRST[name] + u
            if JOBS[name] == 2:
                return LOADED[n]
            return i * (LOADED[n + 2] - LOADED[n]) + LOADED[n]

        def wait_emptied(eng, name):
            n = FIRST[name] + JOBS[name] - 1
            for m in (n - 1, n):
                eng.wait_ge(bank_free[m % 2], m // 2 + 2)

        NORMS = [("mix", DT, T), ("mem", DT, MEM), ("ffn0", DT, T), ("final0", DT, T), ("a_mix", DT, T), ("kv", 2, T),
                 ("ffn1", DT, T), ("b_mix", DT, T), ("ffn2", DT, T), ("last", DT, T)]
        TILES_BEFORE, NORM_NO = {}, {}
        for k, (name, _, _) in enumerate(NORMS):
            NORM_NO[name] = k
            TILES_BEFORE[name] = sum(t for _, t, _ in NORMS[:k])
        SPLIT_TILES_BEFORE = {name: k * DT for k, name in enumerate(("mix", "ffn0", "a_mix", "ffn1", "b_mix", "ffn2"))}
        AFTER_FFN = ("final0", "b_mix", "last")
        NORM_TILES = {name: (t, w) for name, t, w in NORMS}

        def wait_norm(eng, name):
            eng.wait_ge(S["norm_ready"], TILES_BEFORE[name] + NORM_TILES[name][0])

        def norm_act(act, name, src, ready=0):
            tiles, w = NORM_TILES[name]
            for c in range(tiles):
                n = TILES_BEFORE[name] + c
                if ready:
                    act.wait_ge(S["norm_ready"], ready + c + 1)
                if n >= 2:
                    act.wait_ge(S["square_used"], n - 1)
                nc.scalar.activation(square[:, n % 2, 0:w], src[:, c, 0:w], ACT.Square).then_inc(S["square_ready"], 1)
            norm_root(act, name)

        def norm_root(act, name):
            tiles, w = NORM_TILES[name]
            act.wait_ge(S["square_used"], TILES_BEFORE[name] + tiles)
            if TILES_BEFORE[name]:
                act.wait_ge(S["norm_ready"], TILES_BEFORE[name])
            nc.scalar.activation(rstd[:, 0:w], banks[4][:, 0:w], ACT.Sqrt, bias=con("eps", 1)).then_inc(S["root_ready"], 1)

        def norm_split(act, name, shift=None, first=0, end=DT):
            for c in range(first, end):
                n = SPLIT_TILES_BEFORE[name] + c
                act.wait_ge(S["norm_scaled"], n + 1)
                src = square[:, n % 2, :]
                if shift is None:
                    ins = nc.scalar.activation(h_split[0][:, c, :], src, ACT.Copy)
                else:
                    ins = nc.scalar.activation(h_split[0][:, c, :], src, ACT.Identity, bias=shift(c))
                ins.then_inc(S["norm_hi"], 1)

        def norm_pe(pe, name):
            tiles, w = NORM_TILES[name]
            mean = con("mean_d") if tiles == DT else con("mean_r")
            if NORM_NO[name]:
                pe.wait_ge(S["root_ready"], NORM_NO[name])
            for c in range(tiles):
                n = TILES_BEFORE[name] + c
                pe.wait_ge(S["square_ready"], n + 1)
                nc.tensor.matmul(banks[4][:, 0:w], mean, square[:, n % 2, 0:w], start=(c == 0),
                                 stop=(c == tiles - 1)).then_inc(S["square_used"], 1)

        def norm_dve(dve, steps, name, src, dst, gain, shift=None):
            tiles, w = NORM_TILES[name]
            dve.wait_ge(S["root_ready"], NORM_NO[name] + 1)
            steps.did(nc.vector.reciprocal(rstd[:, 0:w], rstd[:, 0:w]))
            steps.settle()
            for c in range(tiles):
                ins = nc.vector.scalar_tensor_tensor(out=dst[:, c, 0:w], in0=src[:, c, 0:w], scalar=gain(c),
                                                     in1=rstd[:, 0:w], op0=ALU.mult, op1=ALU.mult)
                if shift is not None:
                    steps.did(ins)
                    steps.settle()
                    ins = nc.vector.tensor_scalar(dst[:, c, 0:w], dst[:, c, 0:w], shift(c), None, ALU.add)
                ins.then_inc(S["norm_ready"], 1)

        def inverse_root(dve, steps, name):
            dve.wait_ge(S["root_ready"], NORM_NO[name] + 1)
            steps.did(nc.vector.reciprocal(rstd[:], rstd[:]))

        def norm_dve_split(dve, steps, name, src, gain, shift=None):
            tiles = NORM_TILES[name][0]
            if NORM_NO[name]:
                inverse_root(dve, steps, name)
            steps.settle()

            def scaled(c):
                if c >= 2:
                    dve.wait_ge(S["norm_ready"], TILES_BEFORE[name] + c - 1)
                nc.vector.scalar_tensor_tensor(out=square[:, c % 2, :], in0=src[:, c, :], scalar=gain(c), in1=rstd[:],
                                               op0=ALU.mult, op1=ALU.mult).then_inc(S["norm_scaled"], 1)

            def lower(c):
                n = SPLIT_TILES_BEFORE[name] + c
                dve.wait_ge(S["norm_scaled"], n + 1)
                dve.wait_ge(S["norm_hi"], n + 1)
                a, hi = square[:, c % 2, :], h_split[0][:, c, :].bitcast(F32)
                if shift is None:
                    ins = nc.vector.tensor_tensor(h_split[1][:, c, :], a, hi, ALU.subtract)
                else:
                    ins = nc.vector.scalar_tensor_tensor(out=h_split[1][:, c, :], in0=a, scalar=shift(c), in1=hi,
                                                         op0=ALU.add, op1=ALU.subtract)
                ins.then_inc(S["norm_ready"], 1)

            scaled(0)
            for c in range(1, tiles):
                scaled(c)
                lower(c - 1)
            lower(tiles - 1)

        def a_groups():
            for hd in range(A_HEADS):
                for b in range(TB):
                    n = (b + 1) * P
                    mask = con("causal_bias") if b == 0 else chosen_at(b)
                    yield dict(b=b, n=n, scores=[(n, tile(hd)[:, b * P:(b + 1) * P], k_heads[:, hd, 0:n])], mask=mask,
                               scale=P ** -0.5, heads=[(0, n)], out=[part[:, hd, :] for part in out_split],
                               sums=[(0, P, [(v_heads[:, j, hd * P:(hd + 1) * P], j * P) for j in range(b + 1)])])

        def mem_groups():
            for t in range(2):
                for b in range(TB):
                    half = lambda e: slice(64 * e, 64 * e + 64)
                    yield dict(b=b, n=2 * MEM, mask=None, scale=0.125, heads=[(e * MEM, MEM) for e in range(2)], out=[part[:, t, :] for part in mem_split],
                               scores=[(MEM, q_mem[half(e), t, b * P:(b + 1) * P], k_mem[half(e), t, :]) for e in range(2)],
                               sums=[(64 * e, 64, [(v_mem[:, m, 64 * (2 * t + e):64 * (2 * t + e + 1)], e * MEM + m * P) for m in range(2)])
                                     for e in range(2)])

        def b_groups():
            for t in range(B_HEADS // 2):
                kv = t // 2
                for b in range(TB):
                    first = max(b - 1, 0)
                    n = (b + 1 - first) * P
                    half = lambda e: slice(64 * e, 64 * e + 64)
                    mask = con("band", 2 * P) if b else con("band", 2 * P)[:, P:]
                    yield dict(b=b, n=2 * n, mask=mask, scale=0.125, heads=[(e * (n + 1), n) for e in range(2)], out=[part[:, t, :] for part in out_split], sink=2 * t,
                               scores=[(n, tile(t)[half(e), b * P:(b + 1) * P], kw_heads[half(e), kv, first * P:(b + 1) * P])
                                       for e in range(2)],
                               sums=[(64 * e, 64, [(v_groups[:, first + j, 64 * kv:64 * kv + 64], e * n + j * P) for j in range(b + 1 - first)])
                                     for e in range(2)])

        ATTENTION = [list(a_groups()), list(mem_groups()), list(b_groups()), list(mem_groups())]
        GROUPS_BEFORE = [sum(len(g) for g in ATTENTION[:k]) for k in range(5)]
        score_bank = lambda g, e: banks[2 + 2 * (g % 2) + e]
        LAG = 3
        SUM_LAG = 5
        NSTAT = 6
        stat = lambda g, lo, n=1: small[:, 64 + NSTAT * (g % RING) + lo:64 + NSTAT * (g % RING) + lo + n]

        block = ctx.enter_context(nc.Block())

        @block.sync
        def _(sp):
            w_ada = io["w_ada"][0].rearrange("(c p) n -> p c n", p=P)
            w_in = io["w_in"][0].rearrange("(c p) n -> p c n", p=P)

            sp.dma_start(cons[:], io["constants"]).then_inc(S["cons_in"], 16)
            sp.dma_start(cols[:], io["columns"]).then_inc(S["cols_in"], 16)

            def fetch(name, kc, width, pieces, i, u, p):
                for lo, hi, src in pieces:
                    sp.dma_start(slot(p, kc, width)[:, :, lo:hi], src[:, :, 2 * i + u, :]).then_inc(weights_in[p], 16)

            def load(name, kc, width, pieces, also=None):
                n0, split = FIRST[name], name in SPLIT
                first = 0 if n0 and all(JOB_SPLIT[slot_before(n0 + u)] == split for u in range(2)) else 1
                if first:
                    for i, u, p, use in turn_of(name, 0):
                        if n0:
                            slot_free(n0 + u)
                        fetch(name, kc, width, pieces, i, u, p)
                        if also:
                            also(i, u, p)
                for i, u, p, use in pairs(sp, name, first):
                    if split:
                        sp.wait_ge(lo_ready[p], SPLITS_BEFORE[n0 + u] + i)
                    else:
                        sp.wait_ge(product_done[p], use)
                    fetch(name, kc, width, pieces, i, u, p)
                    if also:
                        also(i, u, p)

            def slot_free(n):
                p = n % 2
                before = slot_before(n)
                if JOB_SPLIT[before]:
                    sp.wait_ge(lo_ready[p], SPLITS_BEFORE[n])
                else:
                    sp.wait_ge(product_done[p], before // 2 + 1)

            def cut(w, lo, hi, n):
                return w[:, :, lo:hi].rearrange("p c (j n) -> p c j n", n=n)

            def load_one(name, j, kc, width, pieces):
                p, use = one(name, j)
                slot_free(FIRST[name] + j)
                for lo, hi, src in pieces:
                    sp.dma_start(slot(p, kc, width)[:, :, lo:hi], src).then_inc(weights_in[p], 16)

            def load_ffn(k, w_up, w_down):
                up = w_up.rearrange("(c p) n -> p c n", p=P)
                down = w_down.rearrange("(c p) n -> p c n", p=P)
                for half, (t0, n) in enumerate(HALVES):
                    lo, hi = t0 * P, (t0 + n) * P
                    load(f"ffn{k}_up{half}", DT, 2 * P, [(0, P, cut(up, lo, hi, P)), (P, 2 * P, cut(up, FF + lo, FF + hi, P))])
                    load(f"ffn{k}_down{half}", n, P, [(0, P, cut(down[:, t0:t0 + n, :], 0, D, P))])

            for k in range(2):
                sp.dma_start(ada_first[k], w_ada[:, :, k * T:(k + 1) * T]).then_inc(ada_first_in[k], 16)
            ada = cut(w_ada, 2 * D, 6 * D, 2 * P)

            def load_ada(stage):
                def also(i, u, p):
                    if stage or not isinstance(i, int):
                        sp.wait_ge(ada_summed[p], 4 * stage + i)
                    elif u == 1:
                        sp.wait_ge(S["angle_ready"], 4)
                    sp.dma_start(ada_rest[p], ada[:, :, 8 * stage + 2 * i + u, :]).then_inc(ada_in[p], 16)
                return also

            load("glu", DT, 2 * P, [(0, P, cut(w_in, 0, D, P)), (P, 2 * P, cut(w_in, D, 2 * D, P))], load_ada(0))
            load("qk", DT, 2 * P, [(0, 2 * P, cut(w_in, 2 * D, 4 * D, 2 * P))], load_ada(1))
            for j in range(2):
                load_one("gates", j, DT, HEADS, [(0, HEADS, w_in[:, :, 6 * D + HEADS * j:6 * D + HEADS * (j + 1)])])
            load("v", DT, 2 * P, [(0, 2 * P, cut(w_in, 4 * D, 5 * D, 2 * P))])
            load("o", DT, 2 * P, [(0, 2 * P, cut(w_in, 5 * D, 6 * D, 2 * P))])
            merge0 = 6 * D + 2 * HEADS
            load("merge_mlstm", DT, 2 * P, [(0, 2 * P, cut(w_in, merge0 + D, merge0 + 2 * D, 2 * P))])
            load("merge_conv", DT, 2 * P, [(0, 2 * P, cut(w_in, merge0, merge0 + D, 2 * P))])
            load("conv_pw", DT, 2 * P, [(0, 2 * P, cut(io["w_conv_pw"][0].rearrange("(c p) n -> p c n", p=P), 0, D, 2 * P))])
            sp.wait_ge(S["spread_ready"], 2 * HEADS)
            sp.dma_start(memT, io["mem"].rearrange("(c p) t -> p c t", p=P)).then_inc(S["mem_in"], 16)
            load("mix_out", DT, 2 * P, [(0, 2 * P, cut(io["w_out"][0].rearrange("(c p) n -> p c n", p=P), 0, D, 2 * P))])
            load_ffn(0, io["w_ffn_up"][0], io["w_ffn_down"][0])

            def load_mem(k):
                sp.wait_ge(S["hid_ready"], 2 + FT * (k + 1))
                sp.dma_start(mem_weights, io["w_mem_kv_2"][k].rearrange("(c p) n -> p c n", p=P)).then_inc(S["mem_weights_in"], 16)

            w_a = io["a_w_in_2"][0].rearrange("(c p) n -> p c n", p=P)
            kv0 = D
            kr0 = kv0 + R
            iq0 = kr0 + 32
            ik0 = iq0 + IDX_HEADS * 64
            iw0 = ik0 + 64
            mq0 = iw0 + IDX_HEADS
            load_mem(0)
            load("a_idx", DT, 2 * P, [(0, 2 * P, cut(w_a, iq0, ik0, 2 * P))])
            load_one("a_keys", 0, DT, 2 * P, [(0, 32, w_a[:, :, kr0:iq0]), (32, 48, w_a[:, :, iw0:mq0]),
                                              (P, P + 64, w_a[:, :, ik0:iw0]), (P + 64, 2 * P, w_a[:, :, ik0:iw0])])
            load_one("a_kv", 0, DT, 2 * P, [(0, 2 * P, w_a[:, :, kv0:kr0])])
            load_one("a_qmem", 0, DT, 2 * P, [(0, 2 * P, w_a[:, :, mq0:mq0 + 2 * P])])
            load("a_q", DT, 2 * P, [(0, 2 * P, cut(w_a, 0, D, 2 * P))])
            p, use = one("a_uk", 0)
            sp.wait_ge(S["uk_pad_zero"], 1)
            uk = io["a_w_uk_2"][0].rearrange("(c p) h n -> p c h n", p=P)
            for c in range(2):
                sp.dma_start(slot(p, 2, D).rearrange("p c (h n) -> p c h n", n=P)[:, c, :, 32:P], uk[:, c]).then_inc(weights_in[p], 16)
            load_one("a_uv", 0, 2, D, [(0, D, io["a_w_uv_2"][0].rearrange("(c p) h n -> p c (h n)", p=P))])
            out_of = lambda w: cut(w.rearrange("(c p) n -> p c n", p=P), 0, D, P)
            load("a_out", OUT_K, P, [(0, P, out_of(io["a_w_out_2"][0]))])
            load_ffn(1, io["f_w_up_2"][0], io["f_w_down_2"][0])
            load_mem(1)
            w_b = io["b_w_in_2"][0].rearrange("(c p) n -> p c n", p=P)
            load("b_q", DT, 2 * P, [(0, 2 * P, cut(w_b, 0, D, 2 * P))])
            for name, lo in (("b_k", D), ("b_v", D + 2 * P), ("b_qmem", D + 4 * P)):
                load_one(name, 0, DT, 2 * P, [(0, 2 * P, w_b[:, :, lo:lo + 2 * P])])
            load("b_out", OUT_K, P, [(0, P, out_of(io["b_w_out_2"][0]))])
            load_ffn(2, io["f_w_up_2"][1], io["f_w_down_2"][1])
            for c in range(0, DT, 2):
                sp.wait_ge(S["norm_ready"], TILES_BEFORE["last"] + c + 2)
                sp.dma_start(io["out"].rearrange("(c p) t -> p c t", p=P)[:, c:c + 2, :], xT[:, c:c + 2, :]).then_inc(S["out_written"], 16)
            sp.wait_ge(S["out_written"], 16 * DT // 2)

        @block.tensor
        def _(pe):
            def job(p, kc, width, rhs, tiles):
                w = slot(p, kc, width)
                for m in range(tiles):
                    for c in range(kc):
                        last = nc.tensor.matmul(banks[2 * p + m][:], w[:, c, m * P:(m + 1) * P], rhs(c),
                                                start=(c == 0), stop=(c == kc - 1))
                last.then_inc(product_done[p], 1)

            def product(name, kc, width, rhs, tiles=2, norm=None):
                def turn(i, u, p, use):
                    pe.wait_ge(weights_in[p], weights_of(name, u, i))
                    pe.wait_ge(bank_free[p], use + 1)
                    job(p, kc, width, rhs, tiles)

                stage(name, turn, norm, tiles)

            def stage(name, turn, norm, tiles):
                for i, u, p, use in pairs(pe, name):
                    turn(i, u, p, use)
                if norm:
                    before, left = TILES_BEFORE[norm], DT - tiles
                    pe.wait_ge(S["root_ready"], NORM_NO[norm])
                    pe.wait_ge(S["square_used"], before + left)
                    nc.tensor.matmul(banks[4][:], con("mean_d"), rstd[:], start=True, stop=False)
                    for c in range(left, DT):
                        pe.wait_ge(S["square_ready"], before + c + 1)
                        nc.tensor.matmul(banks[4][:], con("mean_d"), square[:, c % 2, :], start=False,
                                         stop=(c == DT - 1)).then_inc(S["square_used"], 1)

            def split_job(p, kc, width, rhs, waits, tiles=2, split=None, between=()):
                between = list(between)
                w = [(split or w_split)[p][:, part, 0:kc * width].rearrange("p (c n) -> p c n", n=width) for part in range(2)]
                order = [(m, c) for c in range(kc) for m in range(tiles)] if waits else [(m, c) for m in range(tiles) for c in range(kc)]
                for m, c in order:
                    if waits and m == 0:
                        pe.wait_ge(S[waits[0]], waits[1] + c + 1)
                    for wp, hp in ((0, 0), (0, 1), (1, 0)):
                        last = nc.tensor.matmul(banks[2 * p + m][:], w[wp][:, c, m * P:(m + 1) * P], rhs(c, hp),
                                                start=(c == 0 and wp + hp == 0), stop=(c == kc - 1 and wp == 1))
                    if between and (m * kc + c) % 2 == 1:
                        between.pop(0)()
                assert not between
                last.then_inc(product_done[p], 1)

            def split_product(name, kc, width, rhs, waits, tiles=2, also=None, norm=None, split=None):
                def turn(i, u, p, use):
                    pe.wait_ge(lo_ready[p], SPLITS_BEFORE[FIRST[name] + u] + i + 1)
                    pe.wait_ge(bank_free[p], use + 1)
                    split_job(p, kc, width, rhs, waits if u == 0 else None, tiles, split)
                    if also:
                        also(i, u, p)

                stage(name, turn, norm, tiles)

            def start_split(name, j):
                p, use = one(name, j)
                pe.wait_ge(lo_ready[p], SPLITS_BEFORE[FIRST[name] + j] + 1)
                pe.wait_ge(bank_free[p], use + 1)
                return p

            def start_one(name, j):
                p, use = one(name, j)
                pe.wait_ge(weights_in[p], LOADED[FIRST[name] + j])
                pe.wait_ge(bank_free[p], use + 1)
                return p

            def product_one(name, j, kc, sizes, rhs, width=T):
                p = start_one(name, j)
                w = slot(p, kc, sum(sizes))
                for m, n in enumerate(sizes):
                    lo = sum(sizes[:m])
                    for c in range(kc):
                        last = nc.tensor.matmul(banks[2 * p + m][0:n, 0:width], w[:, c, lo:lo + n], rhs(c),
                                                start=(c == 0), stop=(c == kc - 1))
                last.then_inc(product_done[p], 1)

            def modulation(stage):
                def also(i, u, p):
                    pe.wait_ge(ada_summed[p], i + 4 * stage + 1)
                    out = banks[6][:, 16 * stage:16 * (stage + 1)].rearrange("p (j m) -> p j m", m=2)
                    for m in range(2):
                        last = nc.tensor.matmul(out[:, 2 * i + u, m:m + 1], ada_sums[:, p, m * P:(m + 1) * P], con("one", 1), start=True, stop=True)
                    last.then_inc(ada_used[p], 1)
                return also

            h = lambda c: hT[:, c, :]
            h_parts = lambda c, part: h_split[part][:, c, :]

            pe.wait_ge(S["cons_in"], 16)
            norm_pe(pe, "mix")
            for k in range(4):
                if k < 3:
                    pe.wait_ge(S["ada_first_summed"], k + 1)
                else:
                    pe.wait_ge(S["ada_last_summed"], DT - 1)
                for m in range(4):
                    last = nc.tensor.matmul(banks[5][:, 4 * k + m:4 * k + m + 1], ada_first_sums[:, k, m * P:(m + 1) * P], con("one", 1),
                                            start=True, stop=True)
            last.then_inc(S["ada_first_done"], 1)
            split_product("glu", DT, 2 * P, h_parts, ("norm_ready", TILES_BEFORE["mix"]), also=modulation(0))
            split_product("qk", DT, 2 * P, h_parts, None, also=modulation(1))
            for j in range(2):
                p, use = one("gates", j)
                pe.wait_ge(weights_in[p], LOADED[FIRST["gates"] + j])
                for c in range(DT):
                    if j == 0:
                        pe.wait_ge(S["h_whole"], c + 1)
                    last = nc.tensor.matmul(banks[4 + j][0:HEADS, :], slot(p, DT, HEADS)[:, c, :], h(c), start=(c == 0), stop=(c == DT - 1))
                last.then_inc(product_done[p], 1)
            pe.wait_ge(S["vbias_in"], 16)
            for i, u, p, use in pairs(pe, "v"):
                pe.wait_ge(weights_in[p], weights_of("v", u, i))
                pe.wait_ge(bank_free[p], use + 1)
                w = slot(p, DT, 2 * P)
                for b in range(TB):
                    out = banks[2 * p + b // 2][:, (b % 2) * 2 * P:(b % 2 + 1) * 2 * P]
                    nc.tensor.matmul(out, con("one", p=1), v_bias.rearrange("p (j n) -> p j n", n=2 * P)[:, 2 * i + u, :],
                                     start=True, stop=False)
                    for c in range(DT):
                        last = nc.tensor.matmul(out, hT[:, c, b * P:(b + 1) * P], w[:, c, :], start=False, stop=(c == DT - 1))
                last.then_inc(product_done[p], 1)
            product("o", DT, 2 * P, h)
            pe.wait_ge(S["gate_ready"], 1)
            for b in range(TB):
                last = nc.tensor.transpose(banks[4][:, b * HEADS:(b + 1) * HEADS], g_row[:, b * P:(b + 1) * P],
                                           con("ident", HEADS, HEADS))
            last.then_inc(S["g_turned"], 1)
            product("merge_mlstm", DT, 2 * P, h)

            pe.wait_ge(S["g_cols_ready"], 1)
            pe.wait_ge(S["conv_ready"], DT)
            for c in range(DT):
                last = nc.tensor.matmul(banks[4][:], con("mean_d"), conv[:, c, :], start=(c == 0), stop=(c == DT - 1))
            last.then_inc(S["ln_mean"], 1)
            product_one("merge_conv", 0, DT, [P, P], h)
            for c in range(DT):
                pe.wait_ge(S["ln_square"], c + 1)
                nc.tensor.matmul(banks[5][:], con("mean_d"), square[:, c % 2, :], start=(c == 0),
                                 stop=(c == DT - 1)).then_inc(S["ln_square_used"], 1)
            for j in range(1, 4):
                product_one("merge_conv", j, DT, [P, P], h)

            wait_emptied(pe, "merge_conv")
            pe.wait_ge(S["conv_acc_free"], 16 + 2)
            pe.wait_ge(S["modg_ready"], 2)
            pe.wait_ge(S["nm_ready"], 2)
            pe.wait_ge(S["em_ready"], 1)
            pe.wait_ge(S["ln_root"], 1)
            pe.wait_ge(S["ln_dev"], DT)
            pe.wait_ge(S["v_centred"], TB * HEADS)

            def spread(hd):
                if hd:
                    pe.wait_ge(S["logit_ready"], TB * hd)
                    pe.wait_ge(S["em_copied"], hd)
                for bank, row in ((4, neg_m), (5, em_row)):
                    nc.tensor.matmul(banks[bank][:], con("head_row", HEADS * P, HEADS)[:, hd * P:(hd + 1) * P], row,
                                     start=True, stop=True).then_inc(S["spread_ready"], 1)

            def head_scores(hd, j):
                n = TB * hd + j
                if n >= 2:
                    pe.wait_ge(S["weight_ready"], n - 1)
                for e in range(2):
                    last = nc.tensor.matmul(banks[6 + j % 2][:, 0:T - j * P],
                                            qk[:, 8 + 2 * hd + e, QW - 1 + j * P:QW - 1 + (j + 1) * P],
                                            qk[:, 2 * hd + e, QW - 1 + j * P:QW - 1 + T], start=(e == 0), stop=(e == 1))
                last.then_inc(S["score_ready"], 1)

            def head_sums(hd, j):
                pe.wait_ge(S["weight_ready"], TB * hd + j + 1)
                if j == 0 and hd:
                    pe.wait_ge(S["num_taken"], 3 * hd)
                rhs = probs_t[:, j, j * P:T]
                for e in range(2):
                    nc.tensor.matmul(banks[e][:, j * P:T], v_tok[:, j, (2 * hd + e) * P:(2 * hd + e + 1) * P], rhs,
                                     start=(j == 0), stop=(j == TB - 1))
                last = nc.tensor.matmul(banks[2][:, j * P:T], con("one"), rhs, start=(j == 0), stop=(j == TB - 1))
                if j == TB - 1:
                    last.then_inc(S["num_ready"], 1)

            def variance(hd):
                if hd:
                    pe.wait_ge(S["var_used"], hd)
                for e in range(2):
                    pe.wait_ge(S["dev_square"], 2 * hd + e + 1)
                    last = nc.tensor.matmul(banks[3][:], con("mean_r"), square[:, e, :], start=(e == 0), stop=(e == 1))
                last.then_inc(S["var_ready"], 1)

            for hd in range(HEADS):
                spread(hd)
                head_scores(hd, 0)
                head_scores(hd, 1)
                if hd:
                    variance(hd - 1)
                head_sums(hd, 0)
                head_scores(hd, 2)
                head_sums(hd, 1)
                head_scores(hd, 3)
                head_sums(hd, 2)
                head_sums(hd, 3)

            pe.wait_ge(S["num_taken"], 3 * HEADS)
            pe.wait_ge(S["ln_ready"], DT)
            product_one("conv_pw", 0, DT, [P, P], lambda c: conv[:, c, :])
            variance(HEADS - 1)
            pe.wait_ge(S["var_used"], HEADS)
            for j in range(1, 4):
                product_one("conv_pw", j, DT, [P, P], lambda c: conv[:, c, :])
            norm_pe(pe, "mem")
            pe.wait_ge(S["mixed_ready"], DT)
            product("mix_out", DT, 2 * P, lambda c: y_conv[:, c, :], norm="ffn0")

            def ffn(k):
                for half, (t0, n) in enumerate(HALVES):
                    split_product(f"ffn{k}_up{half}", DT, 2 * P, h_parts, ("norm_ready", TILES_BEFORE[f"ffn{k}"]) if half == 0 else None)
                    split_product(f"ffn{k}_down{half}", n, P, lambda c, part: hid[part][:, c, :], ("hid_ready", 2 + FT * k + t0), tiles=1,
                                  norm=AFTER_FFN[k] if half else None)

            ffn(0)

            def memory_kv(name, k):
                pe.wait_ge(S["mem_weights_in"], 16 * (k + 1))
                for j in range(2):
                    p, use = one(name, j)
                    pe.wait_ge(bank_free[p], use + 1)
                    for m in range(2):
                        for c in range(DT):
                            keys = mem_weights[:, c, m * P:(m + 1) * P], memT[:, c, :]
                            values = memT[:, c, m * P:(m + 1) * P], mem_weights[:, c, 2 * P:]
                            lhs, rhs = values if j else keys
                            last = nc.tensor.matmul(banks[2 * p + m][:, 0:MEM], lhs, rhs, start=(c == 0), stop=(c == DT - 1))
                    last.then_inc(product_done[p], 1)

            def rotations(tiles, name, rows, done):
                def step(n, t):
                    if n >= 2:
                        pe.wait_ge(S["rot_sin_ready"], n - 1)
                    nc.tensor.matmul(banks[4 + n % 2][0:rows, :], con(name, rows, rows), tile(t)[0:rows, :],
                                     start=True, stop=True).then_inc(S["rot_ready"], 1)

                return [lambda n=done + k, t=t: step(n, t) for k, t in enumerate(tiles)]

            def rotate(tiles, name, rows, done):
                for step in rotations(tiles, name, rows, done):
                    step()

            def attend(k):
                g0, groups = GROUPS_BEFORE[k], ATTENTION[k]

                def scores(g):
                    if g0 + g >= 2:
                        pe.wait_ge(S["at_logits"], g0 + g - 1)
                    for e, (n, q, kk) in enumerate(groups[g]["scores"]):
                        last = nc.tensor.matmul(score_bank(g0 + g, e)[:, 0:n], q, kk, start=True, stop=True)
                    last.then_inc(S["at_scores"], 1)

                def turn(g):
                    pe.wait_ge(S["at_probs"], g0 + g + 1)
                    if g0 + g >= 2:
                        pe.wait_ge(S["at_copied"], g0 + g - 1)
                    blocks = [lo + k for lo, w in groups[g]["heads"] for k in range(0, w, P)]
                    for j, at in enumerate(blocks):
                        last = nc.tensor.transpose(banks[6 + (g0 + g) % 2][:, j * P:(j + 1) * P], probs[:, (g0 + g) % RING, at:at + P],
                                                   con("ident"))
                    last.then_inc(S["at_turned"], 1)

                def sums(g):
                    pe.wait_ge(S["at_copied"], g0 + g + 1)
                    unit, b = divmod(g0 + g, TB)
                    if b == 0 and unit >= 2:
                        pe.wait_ge(S["at_low"], unit - 1)
                    for lo, n, parts in groups[g]["sums"]:
                        for i, (v, at) in enumerate(parts):
                            last = nc.tensor.matmul(banks[unit % 2][lo:lo + n, b * P:(b + 1) * P], v,
                                                    probs_turned[:, (g0 + g) % 3, at:at + P], start=(i == 0), stop=(i == len(parts) - 1))
                    last.then_inc(S["at_sums"], 1)

                for g in range(len(groups) + SUM_LAG):
                    if g < len(groups):
                        scores(g)
                    if LAG <= g < len(groups) + LAG:
                        turn(g - LAG)
                    if g >= SUM_LAG:
                        sums(g - SUM_LAG)

            def output(name, k, norm):
                pe.wait_ge(S["at_low"], GROUPS_BEFORE[k] // TB)
                split_product(name, OUT_K, P, lambda c, part: out_split[part][:, c, :] if c < DT else mem_split[part][:, c - DT, :],
                              None, tiles=1, norm=norm, split=w_split_out)

            memory_kv("a_mem", 0)
            norm_pe(pe, "a_mix")
            split_product("a_idx", DT, 2 * P, h_parts, ("norm_ready", TILES_BEFORE["a_mix"]))
            split_job(start_split("a_keys", 0), DT, 2 * P, h_parts, None)
            wait_emptied(pe, "a_idx")
            pe.wait_ge(S["root_ready"], NORM_NO["a_mix"] + 1)
            split_job(start_split("a_kv", 0), DT, 2 * P, h_parts, None, between=rotations(range(9, 17), "rot64", 80, 0))
            wait_emptied(pe, "a_keys")
            for b in range(TB):
                last = nc.tensor.transpose(banks[6][:, b * IDX_HEADS:(b + 1) * IDX_HEADS], tile(8)[32:48, b * P:(b + 1) * P],
                                           cons[32:48, CON["ident"] + 32:CON["ident"] + 48])
            last.then_inc(S["w_idx_turned"], 1)
            split_job(start_split("a_qmem", 0), DT, 2 * P, h_parts, None,
                      between=rotations([8], "rot32", 32, 8) + rotations([17], "rot64", 80, 9))
            pe.wait_ge(S["rope_ready"], 10)
            pe.wait_ge(S["w_idx_ready"], 1)
            n = 0
            for b in range(1, TB):
                for hd in range(IDX_HEADS):
                    half = slice(64 * (hd % 2), 64 * (hd % 2) + 64)
                    if n >= 4:
                        pe.wait_ge(S["relu_ready"], n - 3)
                    nc.tensor.matmul(banks[4 + n % 4][:, 0:(b + 1) * P], tile(9 + hd // 2)[half, b * P:(b + 1) * P],
                                     tile(17)[half, 0:(b + 1) * P], start=True, stop=True).then_inc(S["idx_dots"], 1)
                    n += 1
            split_product("a_q", DT, 2 * P, h_parts, None)
            pe.wait_ge(S["relu_ready"], n)
            norm_pe(pe, "kv")
            pe.wait_ge(S["root_ready"], NORM_NO["kv"] + 1)
            rotate(range(8), "rot32", 32, 10)
            wait_norm(pe, "kv")
            p = start_one("a_uk", 0)
            pe.wait_ge(S["rope_ready"], 9)
            pe.wait_ge(S["rot_sin_ready"], 18)
            for hd in range(A_HEADS):
                bank = banks[(2 * p, 2 * p + 1, 6, 7)[hd % 4]]
                if hd >= 4:
                    pe.wait_ge(S["k_taken"], hd - 3)
                for c in range(2):
                    nc.tensor.matmul(bank[:], slot(p, 2, D)[:, c, hd * P:(hd + 1) * P], kv_low[:, c, :], start=(c == 0), stop=False)
                last = nc.tensor.matmul(bank[:], con("ident", P, 32), tile(8)[0:32, :], start=False, stop=True)
                last.then_inc(S["k_made"] if hd < A_HEADS - 1 else product_done[p], 1)
            p = start_one("a_uv", 0)
            for n in range(2 * TB):
                b, half = divmod(n, 2)
                if n >= 2:
                    pe.wait_ge(S["v_taken"], n - 1)
                for c in range(2):
                    last = nc.tensor.matmul(banks[2 * p + n % 2][:], kv_low[:, c, b * P:(b + 1) * P],
                                            slot(p, 2, D)[:, c, half * T:(half + 1) * T], start=(c == 0), stop=(c == 1))
                last.then_inc(S["v_made"] if n < 2 * TB - 1 else product_done[p], 1)
            wait_emptied(pe, "a_uv")
            pe.wait_ge(S["rope_ready"], 18)
            attend(0)
            attend(1)
            output("a_out", 2, "ffn1")
            ffn(1)
            memory_kv("b_mem", 1)
            split_product("b_q", DT, 2 * P, h_parts, ("norm_ready", TILES_BEFORE["b_mix"]))
            split_job(start_split("b_k", 0), DT, 2 * P, h_parts, None)
            wait_emptied(pe, "b_q")
            pe.wait_ge(S["root_ready"], NORM_NO["b_mix"] + 1)
            partners = rotations(range(8), "rot64", 80, 18)
            p = start_split("b_v", 0)
            w = [w_split[p][:, part, :].rearrange("p (c n) -> p c n", n=2 * P) for part in range(2)]
            for b in range(TB):
                for c in range(DT):
                    for hp, wp in ((0, 0), (0, 1), (1, 0)):
                        last = nc.tensor.matmul(banks[2 * p + b // 2][:, (b % 2) * 2 * P:(b % 2 + 1) * 2 * P],
                                                h_split[hp][:, c, b * P:(b + 1) * P], w[wp][:, c, :],
                                                start=(c == 0 and wp + hp == 0), stop=(c == DT - 1 and hp == 1))
                    if c % 4 == 3 and b * 2 + c // 4 < 7:
                        partners.pop(0)()
            last.then_inc(product_done[p], 1)
            wait_emptied(pe, "b_k")
            split_job(start_split("b_qmem", 0), DT, 2 * P, h_parts, None, between=partners + rotations(KEYS, "rot64", 80, 26))
            for kv in range(4):
                pe.wait_ge(S["rope_ready"], 26 + kv // 2 + 1)
                if kv >= 2:
                    pe.wait_ge(S["dup_ready"], kv - 1)
                nc.tensor.matmul(banks[6 + kv % 2][:], con("dup_hi" if kv % 2 else "dup_lo"), tile(KEYS[kv // 2]),
                                 start=True, stop=True).then_inc(S["dup_made"], 1)
            pe.wait_ge(S["dup_ready"], 4)
            pe.wait_ge(S["rope_ready"], 28)
            attend(2)
            attend(3)
            output("b_out", 4, "ffn2")
            ffn(2)

        @block.scalar
        def _(act):
            steps = Steps(act, act_steps)
            act.dma_start(pos_int, io["positions"]).then_inc(S["pos_in"], 16)
            act.dma_start(xT[:], io["x"].rearrange("(c p) t -> p c t", p=P)).then_inc(S["x_in"], 16)
            for k in range(2, 4):
                act.dma_start(ada_first[k], io["w_ada"][0].rearrange("(c p) n -> p c n", p=P)[:, :, k * T:(k + 1) * T]).then_inc(ada_first_in[k], 16)
            for p in range(2):
                act.sem_inc(bank_free[p], 1)
                act.sem_inc(ada_used[p], 1)
            act.sem_inc(S["conv_acc_free"], 2)
            act.sem_inc(S["merge_used"], 2)
            act.sem_inc(S["hid_ready"], 2)
            act.wait_ge(S["cols_in"], 16)
            nc.scalar.activation(silu_c[:], cols[:, COL["c"]:COL["c"] + DT], ACT.Silu).then_inc(S["silu_c_ready"], 1)
            act.wait_ge(S["x_in"], 16)
            act.wait_ge(S["cons_in"], 16)
            norm_act(act, "mix", xT)

            def split_job(n):
                p, size = n % 2, SIZE[JOB_STAGE[n]]
                act.wait_ge(weights_in[p], LOADED[n])
                if n >= 2:
                    act.wait_ge(product_done[p], slot_before(n) // 2 + 1)
                nc.scalar.activation(split_of(JOB_STAGE[n], p)[:, 0, 0:size], slot(p, 1, size)[:, 0, :], ACT.Copy).then_inc(hi_ready[p], 1)

            def split_first(name, u):
                split_job(FIRST[name] + u)

            def split_after(name, j, take):
                n = slot_after(FIRST[name] + j)
                if JOB_SPLIT[n]:
                    split_job(n)
                take()

            def split_ahead(name, take=None, last_first=False):
                turns = JOBS[name] // 2
                for i, u, p, use in pairs(act, name, 0, turns - 1):
                    if name in SPLIT:
                        size = SIZE[name]
                        act.wait_ge(weights_in[p], weights_of(name, u, i + 1))
                        act.wait_ge(product_done[p], use + 1)
                        nc.scalar.activation(split_of(name, p)[:, 0, 0:size], slot(p, 1, size)[:, 0, :], ACT.Copy).then_inc(hi_ready[p], 1)
                    if take:
                        take(i, u, p, use)
                for i, u, p, use in turn_of(name, turns - 1):
                    n = slot_after(FIRST[name] + 2 * i + u)
                    ahead = n is not None and JOB_SPLIT[n]
                    late = last_first and u == 1
                    if ahead and not late:
                        split_job(n)
                    if take:
                        take(i, u, p, use)
                    if ahead and late:
                        split_job(n)

            def squares(norm, tiles=1):
                nc.scalar.activation(small[:, 112 + NORM_NO[norm]:113 + NORM_NO[norm]], con("eps", 1), ACT.Sqrt)

                def take(i, u, p, use):
                    act.wait_ge(bank_free[p], use + 2)
                    for m in range(tiles):
                        n = i * (2 * tiles) + (TILES_BEFORE[norm] + u * tiles + m)
                        act.wait_ge(S["square_used"], n - 1)
                        nc.scalar.activation(square[:, (u * tiles + m) % 2, :], xT[:, i * (2 * tiles) + (u * tiles + m), :],
                                             ACT.Square).then_inc(S["square_ready"], 1)
                return take

            act.wait_ge(ada_first_in[3], 16)
            act.wait_ge(S["silu_c_ready"], 1)
            for c in range(DT):
                nc.scalar.activation(ada_first[3][:, c, :], ada_first[3][:, c, :], ACT.Copy, scale=silu_c[:, c:c + 1]).then_inc(S["ada_scaled"], 1)
            split_first("glu", 0)
            split_first("glu", 1)
            for k in range(4):
                act.wait_ge(S["angle_ready"], k + 1)
                nc.scalar.activation(trig[:, k, :], trig[:, k, :], ACT.Sin).then_inc(S["trig_ready"], 1)
            act.wait_ge(S["trig_ready"], 4)
            norm_split(act, "mix", lambda c: mod[:, c:c + 1])

            def take_gate(i, u, p, use):
                act.wait_ge(product_done[p], use + 1)
                nc.scalar.activation(sig[:, p, :], banks[2 * p + 1][:], ACT.Sigmoid,
                                     bias=col_at("b_glu", 16, 8 + 2 * i + u)).then_inc(S["sig_ready"], 1)

            split_ahead("glu", take_gate)
            act.wait_ge(S["pads_zero"], 2)

            def take_qk(i, u, p, use):
                act.wait_ge(product_done[p], use + 1)
                for m in range(2):
                    last = nc.scalar.activation(qk[:, 4 * i + 2 * u + m, QW - 1:], banks[2 * p + m][:], ACT.Identity,
                                                bias=col_at("b_qk", 16, 4 * i + 2 * u + m))
                last.then_inc(bank_free[p], 1)
                for m in range(2):
                    act.wait_ge(S["conv_acc_ready"], 4 * i + 2 * u + m + 1)
                    nc.scalar.activation(qk[:, 4 * i + 2 * u + m, QW - 1:], conv_acc[:, m, :], ACT.Silu,
                                         bias=col_at("qk_b", 16, 4 * i + 2 * u + m)).then_inc(S["conv_acc_free"], 1)

            split_ahead("qk", take_qk)
            for p in range(2):
                act.wait_ge(ada_used[p], 1 + 8)
            act.dma_start(v_bias, io["v_bias"]).then_inc(S["vbias_in"], 16)
            for p in range(2):
                act.sem_inc(bank_free[p], 1)
            p, use = one("gates", 1)
            act.wait_ge(product_done[p], use + 1)
            steps.did(nc.scalar.activation(soft, banks[5][0:HEADS, :], ACT.Abs, bias=cols[0:HEADS, COL["b_f"]:COL["b_f"] + 1]))
            steps.settle()
            steps.did(nc.scalar.activation(soft, soft, ACT.Exp, scale=-1.0))
            steps.settle()
            nc.scalar.activation(soft, soft, ACT.Ln, bias=1.0).then_inc(S["softplus_ready"], 1)
            v_cut = v_tok.rearrange("p b (j n) -> p b j n", n=2 * P)
            v_sums = small[:, 64:64 + TB * HEADS].rearrange("p (j b) -> p j b", b=TB)
            for i, u, p, use in pairs(act, "v"):
                act.wait_ge(product_done[p], use + 1)
                for b in range(TB):
                    last = nc.scalar.activation(v_cut[:, b, 2 * i + u, :], banks[2 * p + b // 2][:, (b % 2) * 2 * P:(b % 2 + 1) * 2 * P],
                                                ACT.Copy, accum_out=v_sums[:, 2 * i + u, b:b + 1])
                last.then_inc(bank_free[p], 1)
            act.wait_ge(S["nm_ready"], 2)
            nc.scalar.activation(em_row, em_row, ACT.Exp, scale=2.0).then_inc(S["em_ready"], 1)
            for i, u, p, use in pairs(act, "o"):
                act.wait_ge(product_done[p], use + 1)
                for m in range(2):
                    last = nc.scalar.activation(o_gate[:, 4 * i + 2 * u + m, :], banks[2 * p + m][:], ACT.Sigmoid,
                                                bias=col_at("b_o", 8, 4 * i + 2 * u + m))
                last.then_inc(bank_free[p], 1)
            act.wait_ge(S["g_turned"], 1)
            nc.scalar.activation(small[:, 0:TB * HEADS], banks[4][:, 0:TB * HEADS], ACT.Copy).then_inc(S["g_cols_ready"], 1)

            for i, u, p, use in pairs(act, "merge_mlstm"):
                act.wait_ge(product_done[p], use + 1)
                act.wait_ge(S["merge_used"], 2 * i + u + 1)
                for m in range(2):
                    last = nc.scalar.activation(merge_gate[:, 2 * u + m, :], banks[2 * p + m][:], ACT.Sigmoid,
                                                bias=col_at("b_merge", 16, 8 + 4 * i + 2 * u + m))
                last.then_inc(bank_free[p], 1)

            for c in range(DT):
                act.wait_ge(S["ln_dev"], c + 1)
                if c >= 2:
                    act.wait_ge(S["ln_square_used"], c - 1)
                nc.scalar.activation(square[:, c % 2, :], conv[:, c, :], ACT.Square).then_inc(S["ln_square"], 1)
            act.wait_ge(S["ln_square_used"], DT)
            nc.scalar.activation(rstd[:], banks[5][:], ACT.Sqrt, bias=con("eps", 1)).then_inc(S["ln_root"], 1)

            def conv_gates(j):
                p, use = one("merge_conv", j)
                act.wait_ge(product_done[p], use + 1)
                for m in range(2):
                    last = nc.scalar.activation(conv_gate[:, 2 * j + m, :], banks[2 * p + m][:], ACT.Sigmoid, bias=col("b_merge", 2 * j + m))
                last.then_inc(bank_free[p], 1)

            conv_gates(0)
            conv_gates(1)
            for c in range(DT):
                act.wait_ge(S["ln_scaled"], c + 1)
                nc.scalar.activation(conv[:, c, :], conv[:, c, :], ACT.Silu, bias=col("ln_b", c)).then_inc(S["ln_ready"], 1)
            conv_gates(2)
            conv_gates(3)
            def take_head(hd):
                act.wait_ge(S["num_ready"], hd + 1)
                for e in range(2):
                    nc.scalar.activation(qk[:, 2 * hd + e, QW - 1:], banks[e][:], ACT.Copy).then_inc(S["num_taken"], 1)
                    if hd:
                        act.wait_ge(S["var_ready"], hd)
                    nc.scalar.activation(square[:, e, :], banks[e][:], ACT.Square).then_inc(S["dev_square"], 1)
                if hd:
                    act.wait_ge(S["den_ready"], hd)
                nc.scalar.activation(n_squared, banks[2][:], ACT.Square).then_inc(S["num_taken"], 1)

            def decays(hd, j):
                act.wait_ge(S["logit_ready"], TB * hd + j + 1)
                nc.scalar.activation(decay[:, j % 2, 0:T - j * P], decay[:, j % 2, 0:T - j * P], ACT.Exp).then_inc(S["decay_ready"], 1)

            def head_root(hd):
                act.wait_ge(S["var_used"], hd + 1)
                nc.scalar.activation(rstd[:], rstd[:], ACT.Sqrt).then_inc(S["head_root"], 1)

            for hd in range(HEADS):
                if hd:
                    take_head(hd - 1)
                act.wait_ge(S["spread_ready"], 2 * hd + 2)
                if hd >= 2:
                    act.wait_ge(S["var_used"], hd - 1)
                nc.scalar.activation(den[:, hd % 2, :], banks[5][:], ACT.Copy).then_inc(S["em_copied"], 1)
                decays(hd, 0)
                decays(hd, 1)
                if hd:
                    head_root(hd - 1)
                decays(hd, 2)
                decays(hd, 3)
            take_head(HEADS - 1)
            head_root(HEADS - 1)

            def ffn(k):
                for half, (t0, tiles) in enumerate(HALVES):
                    def take(i, u, p, use):
                        n = FT * k + t0 + 2 * i + u
                        act.wait_ge(product_done[p], use + 1)
                        gates = banks[2 * p][:]
                        if k:
                            nc.scalar.activation(up_pad[:, p, 2:], gates, ACT.Copy).then_inc(S["conv3_in"], 1)
                            act.wait_ge(S["conv3_ready"], n - FT + 1)
                            gates = up_acc[:, p, :]
                        nc.scalar.activation(up_gate[:, p, :], gates, ACT.Silu).then_inc(S["act_gate"], 1)
                        act.wait_ge(bank_free[p], use + 2)
                        nc.scalar.activation(hid[0][:, 0:tiles, :][:, 2 * i + u, :], hid_raw[:, p, :], ACT.Copy).then_inc(S["hid_hi_ready"], 1)

                    split_ahead(f"ffn{k}_up{half}", take)
                    split_ahead(f"ffn{k}_down{half}", squares(AFTER_FFN[k]) if half else None, half == 1)
                norm_root(act, AFTER_FFN[k])

            act.wait_ge(S["mem_in"], 16)
            norm_act(act, "mem", memT)
            split_ahead("mix_out", squares("ffn0", 2), True)
            norm_root(act, "ffn0")
            norm_split(act, "ffn0", lambda c: mod[:, 3 * DT + c:3 * DT + c + 1])
            ffn(0)

            def take_tiles(dst):
                def take(i, u, p, use):
                    act.wait_ge(product_done[p], use + 1)
                    for m in range(2):
                        last = nc.scalar.activation(dst[:, 4 * i + 2 * u + m, :], banks[2 * p + m][:], ACT.Copy)
                    last.then_inc(bank_free[p], 1)
                return take

            def out_of_job(name, j, parts):
                p, use = one(name, j)
                act.wait_ge(product_done[p], use + 1)
                for dst, m, r, w in parts:
                    last = nc.scalar.activation(dst, banks[2 * p + m][0:r, 0:w], ACT.Copy)
                last.then_inc(bank_free[p], 1)

            def memory_k(name):
                out_of_job(name, 0, [(k_mem[:, m, :], m, P, MEM) for m in range(2)])

            def memory_v(name):
                out_of_job(name, 1, [(v_mem[:, m, :], m, P, MEM) for m in range(2)])

            def attend(k):
                g0, groups = GROUPS_BEFORE[k], ATTENTION[k]

                def exps(g):
                    n = g0 + g
                    act.wait_ge(S["at_neg_max"], n + 1)
                    heads = groups[g]["heads"]
                    with_sink = 0 if groups[g].get("sink") is None else 1
                    for e, (lo, w) in enumerate(heads):
                        part = probs[:, n % RING, lo:lo + w + with_sink]
                        last = nc.scalar.activation(part, part, ACT.Exp, bias=stat(n, 2 + e), accum_out=stat(n, 4 + e))
                    last.then_inc(S["at_exp"], 1)

                def copies(g):
                    n = g0 + g
                    act.wait_ge(S["at_turned"], n + 1)
                    if n >= 3:
                        act.wait_ge(S["at_sums"], n - 2)
                    w = groups[g]["n"]
                    nc.scalar.activation(probs_turned[:, n % 3, 0:w], banks[6 + n % 2][:, 0:w], ACT.Copy).then_inc(S["at_copied"], 1)

                def outputs(g):
                    n = g0 + g
                    act.wait_ge(S["at_sums"], n + 1)
                    nc.scalar.activation(groups[g]["out"][0], banks[n // TB % 2][:], ACT.Copy).then_inc(S["at_out"], 1)

                for g in range(len(groups) + SUM_LAG):
                    if g < len(groups):
                        exps(g)
                    if LAG <= g < len(groups) + LAG:
                        copies(g - LAG)
                    if g >= SUM_LAG and (g - SUM_LAG) % TB == TB - 1:
                        outputs(g - SUM_LAG)

            norm_act(act, "a_mix", xT, TILES_BEFORE["final0"])
            memory_k("a_mem")
            norm_split(act, "a_mix", None, 0, 5)
            memory_v("a_mem")
            norm_split(act, "a_mix", None, 5, DT)
            split_ahead("a_idx", take_tiles(idx_tiles))
            split_after("a_keys", 0, lambda: out_of_job("a_keys", 0, [(tile(8)[0:48, :], 0, 48, T), (tile(17), 1, P, T)]))
            split_after("a_kv", 0, lambda: out_of_job("a_kv", 0, [(kv_low[:, m, :], m, P, T) for m in range(2)]))
            act.wait_ge(S["w_idx_turned"], 1)
            nc.scalar.activation(small[:, 0:TB * IDX_HEADS], banks[6][:, 0:TB * IDX_HEADS], ACT.Copy,
                                 scale=(IDX_HEADS * 64) ** -0.5).then_inc(S["w_idx_ready"], 1)
            split_after("a_qmem", 0, lambda: out_of_job("a_qmem", 0, [(q_mem[:, m, :], m, P, T) for m in range(2)]))
            n = 0
            for b in range(1, TB):
                for hd in range(IDX_HEADS):
                    act.wait_ge(S["idx_dots"], n + 1)
                    if n >= 3:
                        act.wait_ge(S["relu_used"], n - 2)
                    w = (b + 1) * P
                    nc.scalar.activation(relu_idx[:, n % 3, 0:w], banks[4 + n % 4][:, 0:w], ACT.Relu).then_inc(S["relu_ready"], 1)
                    n += 1
            split_ahead("a_q", take_tiles(q_tiles))
            norm_act(act, "kv", kv_low)
            p, use = one("a_uk", 0)
            for hd in range(A_HEADS):
                if hd < A_HEADS - 1:
                    act.wait_ge(S["k_made"], hd + 1)
                else:
                    act.wait_ge(product_done[p], use + 1)
                nc.scalar.activation(k_heads[:, hd, :], banks[(2 * p, 2 * p + 1, 6, 7)[hd % 4]][:],
                                     ACT.Copy).then_inc(S["k_taken"] if hd < A_HEADS - 1 else bank_free[p], 1)
            p, use = one("a_uv", 0)
            for n in range(2 * TB):
                b, half = divmod(n, 2)
                if n < 2 * TB - 1:
                    act.wait_ge(S["v_made"], n + 1)
                else:
                    act.wait_ge(product_done[p], use + 1)
                nc.scalar.activation(v_heads[:, b, half * T:(half + 1) * T], banks[2 * p + n % 2][:],
                                     ACT.Copy).then_inc(S["v_taken"] if n < 2 * TB - 1 else bank_free[p], 1)
            attend(0)
            split_first("a_out", 0)
            split_first("a_out", 1)
            attend(1)
            split_ahead("a_out", squares("ffn1"), True)
            norm_root(act, "ffn1")
            norm_split(act, "ffn1")
            ffn(1)
            norm_split(act, "b_mix", None, 0, 2)
            memory_k("b_mem")
            norm_split(act, "b_mix", None, 2, 6)
            memory_v("b_mem")
            norm_split(act, "b_mix", None, 6, DT)
            split_ahead("b_q", take_tiles(q_tiles))
            split_after("b_k", 0, lambda: out_of_job("b_k", 0, [(tile(KEYS[m]), m, P, T) for m in range(2)]))
            p, use = one("b_v", 0)
            act.wait_ge(product_done[p], use + 1)
            for m in range(2):
                last = nc.scalar.activation(v_groups[:, 2 * m:2 * m + 2, :], banks[2 * p + m][:].rearrange("p (b n) -> p b n", b=2), ACT.Copy)
            last.then_inc(bank_free[p], 1)
            out_of_job("b_qmem", 0, [(q_mem[:, m, :], m, P, T) for m in range(2)])
            for kv in range(4):
                act.wait_ge(S["dup_made"], kv + 1)
                nc.scalar.activation(kw_heads[:, kv, :], banks[6 + kv % 2][:], ACT.Copy).then_inc(S["dup_ready"], 1)
            attend(2)
            split_first("b_out", 0)
            split_first("b_out", 1)
            attend(3)
            split_ahead("b_out", squares("ffn2"), True)
            norm_root(act, "ffn2")
            norm_split(act, "ffn2")
            ffn(2)

        @block.vector
        def _(dve):
            steps = Steps(dve, dve_steps)
            dve.wait_ge(S["cons_in"], 16)

            dve.wait_ge(S["pos_in"], 16)
            pos, ang, turns = trig_tmp[:, 0, :], trig_tmp[:, 1, :], trig_tmp[:, 2, :]
            steps.did(nc.vector.tensor_copy(pos, pos_int))
            steps.settle()
            for k in range(4):
                out, quarter = trig[:, k, :], 0.25 if k % 2 == 0 else 0.0
                steps.did(nc.vector.tensor_scalar(ang, pos, con("inv32" if k < 2 else "inv64", 1), None, ALU.mult))
                steps.settle()
                steps.did(nc.vector.tensor_scalar(turns, ang, 1 / (2 * np.pi), quarter, ALU.mult, ALU.add))
                steps.settle()
                steps.did(nc.vector.tensor_scalar(turns, turns, ROUND, ROUND, ALU.add, ALU.subtract))
                for part in (TWO_PI_HI, TWO_PI_MID, TWO_PI_LO):
                    steps.settle()
                    steps.did(nc.vector.scalar_tensor_tensor(out=ang, in0=turns, scalar=-part, in1=ang, op0=ALU.mult, op1=ALU.add))
                steps.settle()
                if k % 2 == 0:
                    steps.did(nc.vector.tensor_scalar(ang, ang, np.pi / 2, None, ALU.add))
                    steps.settle()
                nc.vector.tensor_scalar(out, ang, PI_IN, -PI_IN, ALU.min, ALU.max).then_inc(S["angle_ready"], 1)
                dve.wait_ge(S["angle_ready"], k + 1)


            def gains(k, g):
                at = (3 * k + 1) * DT
                nc.vector.scalar_tensor_tensor(out=modg[:, k, :], in0=mod[:, at:at + DT], scalar=1.0,
                                               in1=cols[:, COL[g]:COL[g] + DT], op0=ALU.add, op1=ALU.mult).then_inc(S["modg_ready"], 1)
                dve.wait_ge(S["modg_ready"], k + 1)

            def ada_product(out, w, c):
                if c == 0:
                    return nc.vector.tensor_scalar(out, w[:, c, :], silu_c[:, c:c + 1], None, ALU.mult)
                return nc.vector.scalar_tensor_tensor(out=out, in0=w[:, c, :], scalar=silu_c[:, c:c + 1], in1=out, op0=ALU.mult, op1=ALU.add)

            dve.wait_ge(S["cols_in"], 16)
            dve.wait_ge(S["silu_c_ready"], 1)
            for k in range(3):
                dve.wait_ge(ada_first_in[k], 16)
                for c in range(DT):
                    steps.settle()
                    ins = ada_product(ada_first_sums[:, k, :], ada_first[k], c)
                    if c < DT - 1:
                        steps.did(ins)
                    else:
                        ins.then_inc(S["ada_first_summed"], 1)
                if k == 0:
                    inverse_root(dve, steps, "mix")
            dve.wait_ge(S["ada_first_done"], 1)
            steps.did(nc.vector.tensor_tensor(mod[:, 0:2 * DT], banks[5][:, 0:2 * DT], cols[:, COL["b_ada"]:COL["b_ada"] + 2 * DT], ALU.add))
            steps.settle()
            gains(0, "norm_mix_g")
            norm_dve_split(dve, steps, "mix", xT, lambda c: modg[:, 0, c:c + 1], lambda c: mod[:, c:c + 1])
            def ada_sum(stage, i, u, p):
                dve.wait_ge(ada_in[p], (i + 4 * stage + 1) * 16)
                dve.wait_ge(ada_used[p], i + 4 * stage + 1)
                for c in range(DT):
                    if c:
                        steps.settle()
                    ins = ada_product(ada_sums[:, p, :], ada_rest[p], c)
                    if c < DT - 1:
                        steps.did(ins)
                    else:
                        ins.then_inc(ada_summed[p], 1)

            dve.wait_ge(S["pads_zero"], 2)
            for i, u, p, use in pairs(dve, "glu"):
                if u == 0:
                    steps.loop(i, 2 * (DT - 1))
                ada_sum(0, i, u, p)
                dve.wait_ge(S["sig_ready"], 2 * i + u + 1)
                nc.vector.scalar_tensor_tensor(out=a_pad[:, 2 * i + u, KW - 1:], in0=banks[2 * p][:], scalar=col_at("b_glu", 16, 2 * i + u),
                                               in1=sig[:, p, :], op0=ALU.add, op1=ALU.mult).then_inc(bank_free[p], 1)
            steps.end_loop(4)
            qk_w = cols[:, COL["qk_w"]:COL["qk_w"] + 16 * QW].rearrange("p (a b) -> p a b", b=QW)
            for i, u, p, use in pairs(dve, "qk"):
                if u == 0:
                    steps.loop(i, 4 * (QW - 1) + 2 * (DT - 1))
                ada_sum(1, i, u, p)
                dve.wait_ge(bank_free[p], use + 2)
                for k in range(QW):
                    for m in range(2):
                        t = 4 * i + 2 * u + m
                        if k == 0:
                            dve.wait_ge(S["conv_acc_free"], t + 1)
                            steps.did(nc.vector.tensor_scalar(conv_acc[:, m, :], qk[:, t, 0:T], qk_w[:, t, 0:1], None, ALU.mult))
                            continue
                        steps.settle(0 if (k, m) == (QW - 1, 1) else 1)
                        ins = nc.vector.scalar_tensor_tensor(out=conv_acc[:, m, :], in0=qk[:, t, k:k + T], scalar=qk_w[:, t, k:k + 1],
                                                             in1=conv_acc[:, m, :], op0=ALU.mult, op1=ALU.add)
                        if k < QW - 1:
                            steps.did(ins)
                        else:
                            ins.then_inc(S["conv_acc_ready"], 1)
            steps.end_loop(4)
            for p in range(2):
                dve.wait_ge(ada_used[p], 1 + 8)
            steps.did(nc.vector.tensor_tensor(mod[:, 2 * DT:], banks[6][:, 0:4 * DT], cols[:, COL["b_ada"] + 2 * DT:COL["b_ada"] + 6 * DT], ALU.add))
            steps.settle()
            gains(1, "norm_ffn_g")
            (pi, use_i), (pf, use_f) = one("gates", 0), one("gates", 1)
            dve.wait_ge(product_done[pi], use_i + 1)
            dve.wait_ge(product_done[pf], use_f + 1)
            steps.did(nc.vector.memset(ones_row, 1.0))
            dve.wait_ge(S["softplus_ready"], 1)
            steps.did(nc.vector.tensor_scalar(logf, banks[5][0:HEADS, :], cols[0:HEADS, COL["b_f"]:COL["b_f"] + 1], 0.0,
                                              ALU.add, ALU.min))
            steps.settle()
            steps.did(nc.vector.tensor_tensor(logf, logf, soft, ALU.subtract))
            steps.settle()
            nc.vector.tensor_tensor_scan(cum_f, ones_row, logf, 0.0, ALU.mult, ALU.add).then_inc(S["gate_cum"], 1)
            dve.wait_ge(S["gate_cum"], 1)
            nc.vector.scalar_tensor_tensor(out=g_row, in0=banks[4][0:HEADS, :], scalar=cols[0:HEADS, COL["b_i"]:COL["b_i"] + 1],
                                           in1=cum_f, op0=ALU.add, op1=ALU.subtract).then_inc(S["gate_ready"], 1)
            dve.wait_ge(S["gate_ready"], 1)
            steps.did(nc.vector.tensor_tensor_scan(neg_m, g_row, g_row, 0.0, ALU.max, ALU.max))
            steps.settle()
            steps.did(nc.vector.scalar_tensor_tensor(out=em_row, in0=cum_f, scalar=-1.0, in1=neg_m, op0=ALU.mult, op1=ALU.subtract))
            steps.settle()
            nc.vector.tensor_scalar(em_row, em_row, LARGEST_LOG, None, ALU.min).then_inc(S["nm_ready"], 1)
            nc.vector.tensor_scalar(neg_m, neg_m, -1.0, None, ALU.mult).then_inc(S["nm_ready"], 1)
            dw_w = cols[:, COL["dw_w"]:COL["dw_w"] + DT * KW].rearrange("p (a b) -> p a b", b=KW)
            wait_emptied(dve, "glu")
            dve.wait_ge(S["h_whole"], DT)
            with dve.Fori(0, DT // 2) as i:
                steps.loop(i, 2 * (KW - 1))
                for k in range(KW):
                    for m in range(2):
                        c = 2 * i + m
                        if k == 0:
                            steps.did(nc.vector.tensor_scalar(conv[:, c, :], a_pad[:, c, 0:T], dw_w[:, c, 0:1], col_at("dw_b", DT, c),
                                                              ALU.mult, ALU.add))
                            continue
                        steps.settle(0 if (k, m) == (KW - 1, 1) else 1)
                        ins = nc.vector.scalar_tensor_tensor(out=conv[:, c, :], in0=a_pad[:, c, k:k + T], scalar=dw_w[:, c, k:k + 1],
                                                             in1=conv[:, c, :], op0=ALU.mult, op1=ALU.add)
                        if k < KW - 1:
                            steps.did(ins)
                        else:
                            ins.then_inc(S["conv_ready"], 1)
            steps.end_loop(DT // 2)

            dve.wait_ge(S["ln_mean"], 1)
            for c in range(DT):
                nc.vector.tensor_tensor(conv[:, c, :], conv[:, c, :], banks[4][:], ALU.subtract).then_inc(S["ln_dev"], 1)
            dve.wait_ge(S["ln_root"], 1)
            steps.did(nc.vector.reciprocal(rstd[:], rstd[:]))
            steps.settle()
            dve.wait_ge(S["ln_dev"], DT)
            for c in range(DT):
                nc.vector.scalar_tensor_tensor(out=conv[:, c, :], in0=conv[:, c, :], scalar=col("ln_g", c), in1=rstd[:],
                                               op0=ALU.mult, op1=ALU.mult).then_inc(S["ln_scaled"], 1)

            dve.wait_ge(S["merge_used"], 4 + 2)
            dve.wait_ge(S["g_cols_ready"], 1)

            def logits(hd, j):
                nc.vector.tensor_scalar(decay[:, j % 2, 0:T - j * P], banks[4][:, j * P:T], small[:, j * HEADS + hd:j * HEADS + hd + 1],
                                        0.0, ALU.add, ALU.min).then_inc(S["logit_ready"], 1)

            def head_weights(hd, j):
                n = TB * hd + j
                if hd and j == 0:
                    dve.wait_ge(S["num_ready"], hd)
                dve.wait_ge(S["score_ready"], n + 1)
                dve.wait_ge(S["decay_ready"], n + 1)
                steps.did(nc.vector.scalar_tensor_tensor(out=probs_t[:, j, j * P:T], in0=banks[6 + j % 2][:, 0:T - j * P],
                                                         scalar=(2 * P) ** -0.5, in1=decay[:, j % 2, 0:T - j * P],
                                                         op0=ALU.mult, op1=ALU.mult))
                steps.settle()
                diagonal = probs_t[:, j, j * P:(j + 1) * P]
                nc.vector.tensor_tensor(diagonal, diagonal, con("causal_t"), ALU.mult).then_inc(S["weight_ready"], 1)

            def denominator(hd):
                dve.wait_ge(S["num_taken"], 3 * hd + 3)
                dve.wait_ge(S["em_copied"], hd + 1)
                d = den[:, hd % 2, :]
                nc.vector.tensor_tensor(d, d, n_squared, ALU.max).then_inc(S["den_ready"], 1)

            def square_of_root(hd):
                dve.wait_ge(S["var_ready"], hd + 1)
                dve.wait_ge(S["den_ready"], hd + 1)
                if hd:
                    dve.wait_ge(S["hm_ready"], 2 * hd)
                else:
                    dve.wait_ge(S["ln_scaled"], DT)
                nc.vector.scalar_tensor_tensor(out=rstd[:], in0=den[:, hd % 2, :], scalar=con("eps", 1), in1=banks[3][:],
                                               op0=ALU.mult, op1=ALU.add).then_inc(S["var_used"], 1)

            def normalise(hd):
                dve.wait_ge(S["head_root"], hd + 1)
                steps.did(nc.vector.reciprocal(rstd[:], rstd[:]))
                steps.settle()
                for e in range(2):
                    out = qk[:, 2 * hd + e, QW - 1:]
                    nc.vector.scalar_tensor_tensor(out=out, in0=out, scalar=col("mlstm_g", 2 * hd + e), in1=rstd[:],
                                                   op0=ALU.mult, op1=ALU.mult).then_inc(S["hm_ready"], 1)

            for hd in range(HEADS):
                dve.wait_ge(S["spread_ready"], 2 * hd + 1)
                logits(hd, 0)
                if hd:
                    denominator(hd - 1)
                logits(hd, 1)
                head_weights(hd, 0)
                if hd:
                    square_of_root(hd - 1)
                logits(hd, 2)
                head_weights(hd, 1)
                if hd:
                    normalise(hd - 1)
                logits(hd, 3)
                head_weights(hd, 2)
                head_weights(hd, 3)
            denominator(HEADS - 1)
            square_of_root(HEADS - 1)
            normalise(HEADS - 1)
            for j in range(4):
                p, use = one("conv_pw", j)
                dve.wait_ge(product_done[p], use + 1)
                for m in range(2):
                    t = conv_gate[:, 2 * j + m, :]
                    last = nc.vector.scalar_tensor_tensor(out=t, in0=banks[2 * p + m][:], scalar=col("b_pw", 2 * j + m), in1=t,
                                                          op0=ALU.add, op1=ALU.mult)
                last.then_inc(bank_free[p], 1)

            def residual(name, tiles, gate=None, norm=None):
                def turn(i, u, p, use):
                    dve.wait_ge(product_done[p], use + 1)
                    for m in range(tiles):
                        t = tiles * (2 * i + u) + m
                        if gate is None:
                            last = nc.vector.tensor_tensor(xT[:, t, :], xT[:, t, :], banks[2 * p + m][:], ALU.add)
                        else:
                            g = mod[:, gate * DT:(gate + 1) * DT].rearrange("p (a b) -> p a b", b=1)[:, t, :]
                            last = nc.vector.scalar_tensor_tensor(out=xT[:, t, :], in0=banks[2 * p + m][:], scalar=g, in1=xT[:, t, :],
                                                                  op0=ALU.mult, op1=ALU.add)
                    last.then_inc(bank_free[p], 1)

                if norm is None:
                    for i, u, p, use in pairs(dve, name):
                        turn(i, u, p, use)
                    return

                def add(i, odd):
                    for m in range(tiles):
                        c = odd * tiles + m
                        n = i * (2 * tiles) + (TILES_BEFORE[norm] + c)
                        dve.wait_ge(S["square_ready"], n + 1)
                        dve.wait_ge(S["square_used"], n)
                        if isinstance(i, int) and i == 0 and c == 0:
                            dve.wait_ge(S["norm_ready"], TILES_BEFORE[norm])
                            ins = nc.vector.tensor_copy(rstd[:], square[:, 0, :])
                        else:
                            ins = nc.vector.tensor_tensor(rstd[:], rstd[:], square[:, c % 2, :], ALU.add)
                        ins.then_inc(S["square_used"], 1)

                for i, u, p, use in turn_of(name, 0):
                    turn(i, u, p, use)
                    if u == 1:
                        add(0, 0)
                for i, u, p, use in pairs(dve, name, 1):
                    turn(i, u, p, use)
                    add(i + (u - 1), (u + 1) % 2)

            norm_dve(dve, steps, "mem", memT, memT, lambda c: col("g_mem", c))
            residual("mix_out", 2, 2, "ffn0")
            wait_emptied(dve, "mix_out")
            norm_dve_split(dve, steps, "ffn0", xT, lambda c: modg[:, 1, c:c + 1], lambda c: mod[:, 3 * DT + c:3 * DT + c + 1])

            def hidden(n, t, tiles, p, use):
                dve.wait_ge(S["act_gate"], n + 1)
                dve.wait_ge(S["hid_ready"], n + 1)
                nc.vector.tensor_tensor(hid_raw[:, p, :], up_gate[:, p, :], banks[2 * p + 1][:], ALU.mult).then_inc(bank_free[p], 1)
                dve.wait_ge(S["hid_hi_ready"], n + 1)
                nc.vector.tensor_tensor(hid[1][:, 0:tiles, :][:, t, :], hid_raw[:, p, :], hid[0][:, 0:tiles, :][:, t, :].bitcast(F32),
                                        ALU.subtract).then_inc(S["hid_ready"], 1)

            for half, (t0, tiles) in enumerate(HALVES):
                for i, u, p, use in pairs(dve, f"ffn0_up{half}"):
                    hidden(t0 + 2 * i + u, 2 * i + u, tiles, p, use)
                residual(f"ffn0_down{half}", 1, 5, AFTER_FFN[0] if half else None)
            wait_emptied(dve, "ffn0_down1")
            norm_dve(dve, steps, "final0", xT, xT, lambda c: col("final_g", c))
            dve.wait_ge(S["norm_ready"], TILES_BEFORE["a_mix"])
            norm_dve_split(dve, steps, "a_mix", xT, lambda c: col("g_mix", c))

            def rope(tiles, table, rows, done):
                for k, t in enumerate(tiles):
                    n = done + k
                    dve.wait_ge(S["rot_ready"], n + 1)
                    nc.vector.tensor_tensor(rot_sin[0:rows, n % 2, :], banks[4 + n % 2][0:rows, :], trig[0:rows, table + 1, :],
                                            ALU.mult).then_inc(S["rot_sin_ready"], 1)
                    dve.wait_ge(S["rot_sin_ready"], n + 1)
                    dve.wait_ge(S["rot_cos_ready"], n + 1)
                    nc.vector.tensor_tensor(tile(t)[0:rows, :], rot_cos[0:rows, n % 2, :], rot_sin[0:rows, n % 2, :],
                                            ALU.add).then_inc(S["rope_ready"], 1)

            def attend(k):
                g0, groups = GROUPS_BEFORE[k], ATTENTION[k]

                def logits(g):
                    n, grp = g0 + g, groups[g]
                    w, ne = grp["n"], len(grp["heads"])
                    dve.wait_ge(S["at_scores"], n + 1)
                    if n >= RING:
                        dve.wait_ge(S["at_turned"], n - RING + 1)
                    sink = grp.get("sink")
                    if sink is not None:
                        columns = probs[:, n % RING, 0:w + 2].rearrange("p (e k) -> p e k", e=2)[:, :, w // 2:]
                        nc.vector.tensor_copy(columns, cols[:, COL["sinks"] + sink:COL["sinks"] + sink + 2].rearrange("p (e k) -> p e k", k=1))
                    for e, (lo, keys) in enumerate(grp["heads"]):
                        src, out = score_bank(n, e)[:, 0:keys], probs[:, n % RING, lo:lo + keys]
                        mask, op = (grp["mask"], ALU.add) if grp["mask"] is not None else (con("one", 1).to_broadcast([P, keys]), ALU.mult)
                        ins = nc.vector.tensor_tensor_reduce(out=out, in0=src, in1=mask, scale=grp["scale"], scalar=NEG, op0=op, op1=ALU.max,
                                                             accum_out=stat(n, e))
                    ins.then_inc(S["at_logits"], 1)

                def negate(g):
                    n, grp = g0 + g, groups[g]
                    ne, sink = len(grp["heads"]), grp.get("sink")
                    dve.wait_ge(S["at_logits"], n + 1)
                    if sink is None:
                        ins = nc.vector.tensor_scalar(stat(n, 2, ne), stat(n, 0, ne), -1.0, None, ALU.mult)
                    else:
                        for e in range(ne):
                            ins = nc.vector.tensor_scalar(stat(n, 2 + e), stat(n, e), col("sinks", sink + e), -1.0, ALU.max, ALU.mult)
                    ins.then_inc(S["at_neg_max"], 1)

                def inverses(g):
                    n, grp = g0 + g, groups[g]
                    ne = len(grp["heads"])
                    dve.wait_ge(S["at_exp"], n + 1)
                    steps.did(nc.vector.reciprocal(stat(n, 0, ne), stat(n, 4, ne)))

                def weights(g):
                    n = g0 + g
                    steps.settle()
                    for e, (lo, w) in enumerate(groups[g]["heads"]):
                        part = probs[:, n % RING, lo:lo + w]
                        last = nc.vector.tensor_scalar(part, part, stat(n, e), None, ALU.mult)
                    last.then_inc(S["at_probs"], 1)

                def lower(g):
                    n = g0 + g
                    dve.wait_ge(S["at_out"], n // TB + 1)
                    upper, out = groups[g]["out"]
                    nc.vector.tensor_tensor(out, banks[n // TB % 2][:], upper.bitcast(F32), ALU.subtract).then_inc(S["at_low"], 1)

                for g in range(len(groups) + SUM_LAG + 1):
                    if g < len(groups):
                        logits(g)
                    if 1 <= g <= len(groups):
                        inverses(g - 1)
                    if g < len(groups):
                        negate(g)
                    if 1 <= g <= len(groups):
                        weights(g - 1)
                    if g > SUM_LAG and (g - SUM_LAG) % TB == 0:
                        lower(g - SUM_LAG - 1)

            def ffn(k):
                steps.did(nc.vector.memset(up_pad[:, :, 0:2], 0.0))
                steps.settle()
                for half, (t0, tiles) in enumerate(HALVES):
                    at = COL["fconv_w"] + ((k - 1) * FT + t0) * 3
                    w3 = cols[:, at:at + 3 * tiles].rearrange("p (a b) -> p a b", b=3)
                    at = COL["fconv_b"] + (k - 1) * FT + t0
                    b3 = cols[:, at:at + tiles].rearrange("p (a b) -> p a b", b=1)
                    for i, u, p, use in pairs(dve, f"ffn{k}_up{half}"):
                        if u == 0:
                            steps.loop(i, 4)
                        t = 2 * i + u
                        n = FT * k + t0 + t
                        dve.wait_ge(S["conv3_in"], n - FT + 1)
                        acc = up_acc[:, p, :]
                        steps.did(nc.vector.tensor_scalar(acc, up_pad[:, p, 0:T], w3[:, t, 0:1], b3[:, t, :], ALU.mult, ALU.add))
                        steps.settle()
                        steps.did(nc.vector.scalar_tensor_tensor(out=acc, in0=up_pad[:, p, 1:T + 1], scalar=w3[:, t, 1:2], in1=acc,
                                                                 op0=ALU.mult, op1=ALU.add))
                        steps.settle()
                        nc.vector.scalar_tensor_tensor(out=acc, in0=up_pad[:, p, 2:T + 2], scalar=w3[:, t, 2:3], in1=acc,
                                                       op0=ALU.mult, op1=ALU.add).then_inc(S["conv3_ready"], 1)
                        hidden(n, t, tiles, p, use)
                    steps.end_loop(tiles // 2)
                    residual(f"ffn{k}_down{half}", 1, None, AFTER_FFN[k] if half else None)

            rope(range(9, 17), 2, 80, 0)
            rope([8], 0, 32, 8)
            rope([17], 2, 80, 9)
            dve.wait_ge(S["w_idx_ready"], 1)
            n = 0
            for b in range(1, TB):
                w = (b + 1) * P
                left = chosen_at(b)
                for hd in range(IDX_HEADS):
                    dve.wait_ge(S["relu_ready"], n + 1)
                    wcol = small[:, b * IDX_HEADS + hd:b * IDX_HEADS + hd + 1]
                    if hd == 0:
                        ins = nc.vector.tensor_scalar(left, relu_idx[:, n % 3, 0:w], wcol, None, ALU.mult)
                    else:
                        ins = nc.vector.scalar_tensor_tensor(out=left, in0=relu_idx[:, n % 3, 0:w], scalar=wcol, in1=left,
                                                             op0=ALU.mult, op1=ALU.add)
                    ins.then_inc(S["relu_used"], 1)
                    n += 1
                    dve.wait_ge(S["relu_used"], n)
            for b in range(1, TB):
                if b == TB - 1:
                    norm_dve(dve, steps, "kv", kv_low, kv_low, lambda c: col("kv_g", c))
                    rope(range(8), 0, 32, 10)
                left = chosen_at(b)
                diagonal = left[:, b * P:]
                steps.did(nc.vector.tensor_tensor(diagonal, diagonal, con("causal"), ALU.mult))
                steps.settle()
                steps.did(nc.vector.tensor_tensor(diagonal, diagonal, con("after_fill"), ALU.add))
                for _ in range(TOPK // 8):
                    steps.settle()
                    steps.did(nc.vector.max(small[:, 96:104], left))
                    steps.settle()
                    steps.did(nc.vector.match_replace(left, small[:, 96:104], left, CHOSEN))
                steps.settle()
                steps.did(nc.vector.tensor_scalar(left, left, CHOSEN, None, ALU.is_equal))
                steps.settle()
                steps.did(nc.vector.tensor_scalar(left, left, -1.0, -NEG, ALU.add, ALU.mult))
            steps.settle()
            attend(0)
            attend(1)
            residual("a_out", 1, None, "ffn1")
            wait_emptied(dve, "a_out")
            norm_dve_split(dve, steps, "ffn1", xT, lambda c: col("g_ffn", c))
            ffn(1)
            wait_emptied(dve, "ffn1_down1")
            norm_dve_split(dve, steps, "b_mix", xT, lambda c: col("g_mix", DT + c))
            rope(range(8), 2, 80, 18)
            rope(KEYS, 2, 80, 26)
            attend(2)
            attend(3)
            residual("b_out", 1, None, "ffn2")
            wait_emptied(dve, "b_out")
            norm_dve_split(dve, steps, "ffn2", xT, lambda c: col("g_ffn", DT + c))
            ffn(2)
            wait_emptied(dve, "ffn2_down1")
            norm_dve(dve, steps, "last", xT, xT, lambda c: col("g_last", c))

        @block.gpsimd
        def _(pool):
            steps = Steps(pool, pool_steps)
            for c in range(1, DT):
                pool.wait_ge(S["ada_scaled"], c + 1)
                if c > 1:
                    pool.wait_ge(S["ada_last_summed"], c - 1)
                first = ada_first[3][:, 0, :] if c == 1 else ada_first_sums[:, 3, :]
                nc.gpsimd.tensor_tensor(ada_first_sums[:, 3, :], first, ada_first[3][:, c, :], ALU.add).then_inc(S["ada_last_summed"], 1)

            def split_weights(*names, first=0):
                for name in names:
                    size = SIZE[name]

                    def lower(p, before):
                        pool.wait_ge(hi_ready[p], before + 1)
                        part = split_of(name, p)
                        nc.gpsimd.tensor_tensor(part[:, 1, 0:size], slot(p, 1, size)[:, 0, :], part[:, 0, 0:size].bitcast(F32),
                                                ALU.subtract).then_inc(lo_ready[p], 1)

                    if first == "turn":
                        for i, u, p, use in turn_of(name, 0):
                            lower(p, SPLITS_BEFORE[FIRST[name] + u])
                    elif JOBS[name] > 2:
                        for i, u, p, use in pairs(pool, name, first):
                            lower(p, SPLITS_BEFORE[FIRST[name] + u] + i)
                    else:
                        for n in range(FIRST[name], FIRST[name] + JOBS[name]):
                            lower(n % 2, SPLITS_BEFORE[n])

            def ffn(k):
                split_weights(*(name for name, _ in ffn_stages(k)))

            split_weights("glu", first="turn")
            pool.wait_ge(S["ada_first_done"], 1)
            nc.gpsimd.memset(a_pad[:, :, 0:KW - 1], 0.0).then_inc(S["pads_zero"], 1)
            nc.gpsimd.memset(qk[:, :, 0:QW - 1], 0.0).then_inc(S["pads_zero"], 1)
            split_weights("glu", first=1)
            split_weights("qk")
            for m in (FIRST["gates"] - 2, FIRST["gates"] - 1):
                pool.wait_ge(product_done[m % 2], m // 2 + 1)
            for c in range(DT):
                nc.gpsimd.tensor_tensor(hT[:, c, :], h_split[0][:, c, :].bitcast(F32), h_split[1][:, c, :].bitcast(F32),
                                        ALU.add).then_inc(S["h_whole"], 1)
            wait_emptied(pool, "v")
            v_means = small[:, 64:64 + TB * HEADS]
            steps.did(nc.gpsimd.tensor_scalar(v_means, v_means, -1.0 / (2 * P), None, ALU.mult))
            steps.settle()
            for hd in range(HEADS):
                for b in range(TB):
                    v = v_tok[:, b, hd * 2 * P:(hd + 1) * 2 * P]
                    nc.gpsimd.tensor_scalar(v, v, v_means[:, hd * TB + b:hd * TB + b + 1], None, ALU.add).then_inc(S["v_centred"], 1)
            for j in range(4):
                p, use = one("merge_mlstm", j)
                pool.wait_ge(bank_free[p], use + 2)
                for m in range(2):
                    t = o_gate[:, 2 * j + m, :]
                    last = nc.gpsimd.tensor_tensor(t, t, merge_gate[:, 2 * (j % 2) + m, :], ALU.mult)
                last.then_inc(S["merge_used"], 1)
            pool.wait_ge(S["merge_used"], 4 + 2)
            for t in range(2 * HEADS):
                pool.wait_ge(S["hm_ready"], t + 1)
                steps.did(nc.gpsimd.tensor_tensor(qk[:, t, QW - 1:], qk[:, t, QW - 1:], o_gate[:, t, :], ALU.mult))
            steps.settle()
            for j in range(4):
                p, use = one("conv_pw", j)
                pool.wait_ge(bank_free[p], use + 2)
                for t in (2 * j, 2 * j + 1):
                    nc.gpsimd.tensor_tensor(y_conv[:, t, :], y_conv[:, t, :], qk[:, t, QW - 1:], ALU.add).then_inc(S["mixed_ready"], 1)
            ffn(0)
            split_weights("a_idx", "a_keys", "a_kv")
            def rope(tiles, table, rows, done):
                for k, t in enumerate(tiles):
                    n = done + k
                    if n >= 2:
                        pool.wait_ge(S["rope_ready"], n - 1)
                    nc.gpsimd.tensor_tensor(rot_cos[0:rows, n % 2, :], tile(t)[0:rows, :], trig[0:rows, table, :],
                                            ALU.mult).then_inc(S["rot_cos_ready"], 1)

            wait_emptied(pool, "a_idx")
            rope(range(9, 17), 2, 80, 0)
            split_weights("a_qmem")
            wait_emptied(pool, "a_keys")
            rope([8], 0, 32, 8)
            rope([17], 2, 80, 9)
            split_weights("a_q")
            p, use = one("a_uk", 0)
            pool.wait_ge(lo_ready[p], SPLITS_BEFORE[FIRST["a_uk"]])
            nc.gpsimd.memset(slot(p, 2, D).rearrange("p c (h n) -> p c h n", n=P)[:, :, :, 0:32], 0.0).then_inc(S["uk_pad_zero"], 1)
            wait_emptied(pool, "a_q")
            pool.wait_ge(S["relu_used"], (TB - 1) * IDX_HEADS)
            rope(range(8), 0, 32, 10)
            split_weights("a_out")
            ffn(1)
            split_weights("b_q", "b_k", "b_v")
            wait_emptied(pool, "b_q")
            rope(range(8), 2, 80, 18)
            split_weights("b_qmem")
            wait_emptied(pool, "b_k")
            rope(KEYS, 2, 80, 26)
            split_weights("b_out")
            ffn(2)




def kernel(**inputs):
    import concourse.bacc as bacc
    from concourse.bass_utils import run_bass_kernel_spmd

    a = {k: np.ascontiguousarray(v) for k, v in inputs.items()}
    tiles = lambda v: v.reshape(-1, P).T

    b_in = a["b_in"][0]
    gates0 = 6 * D
    merge0 = gates0 + 2 * HEADS
    four = lambda v: np.pad(v.reshape(HEADS, 1), ((0, P - HEADS), (0, 0)))
    by_tap = lambda w: w.reshape(w.shape[0], -1, P).transpose(2, 1, 0).reshape(P, -1)
    parts = {
        "b_ada": tiles(a["b_ada"]), "c": tiles(a["c"]), "norm_mix_g": tiles(a["norm_mix_g"]), "b_glu": tiles(b_in[:2 * D]),
        "b_qk": tiles(b_in[2 * D:4 * D]), "b_o": tiles(b_in[5 * D:6 * D]), "b_merge": tiles(b_in[merge0:]),
        "dw_w": by_tap(a["conv_dw_w"][0]), "dw_b": tiles(a["conv_dw_b"]), "ln_g": tiles(a["conv_ln_g"]), "ln_b": tiles(a["conv_ln_b"]),
        "b_pw": tiles(a["b_conv_pw"]), "qk_w": by_tap(a["qk_conv_w"][0]), "qk_b": tiles(a["qk_conv_b"]),
        "mlstm_g": tiles(a["mlstm_norm_g"]), "norm_ffn_g": tiles(a["norm_ffn_g"]), "final_g": tiles(a["final_norm_g"]),
        "g_mix": tiles(a["g_mix_2"]), "g_ffn": tiles(a["g_ffn_2"]), "g_mem": tiles(a["g_mem_2"]), "g_last": tiles(a["g_final_2"]),
        "kv_g": tiles(a["a_kv_norm_2"]),
        "fconv_w": np.concatenate([by_tap(w) for w in a["f_conv_w_2"]], axis=1), "fconv_b": tiles(a["f_conv_b_2"]),
        "sinks": np.broadcast_to(a["b_sinks_2"][0], (P, B_HEADS)),
        "b_i": four(b_in[gates0:gates0 + HEADS]), "b_f": four(b_in[gates0 + HEADS:merge0]),
    }
    columns = np.concatenate([parts[name] for name, _ in COLUMNS], axis=1)
    assert columns.shape == (P, NCOL)

    feeds = {
        "columns": columns, "constants": constants(), "x": a["x"][0].T, "v_bias": b_in[None, 4 * D:5 * D],
        "mem": a["mem_2"][0].T, "positions": np.broadcast_to(a["positions_2"], (P, T)),
    }
    for name in ("w_ada", "w_in", "w_conv_pw", "w_out", "w_ffn_up", "w_ffn_down", "w_mem_kv_2", "a_w_in_2", "a_w_uk_2", "a_w_uv_2",
                 "a_w_out_2", "b_w_in_2", "b_w_out_2", "f_w_up_2", "f_w_down_2"):
        feeds[name] = a[name]
    feeds = {k: np.ascontiguousarray(v) for k, v in feeds.items()}

    nc = bacc.Bacc("TRN2", target_bir_lowering=False, num_devices=1)
    io = {k: nc.dram_tensor(f"in_{k}", v.shape, mybir.dt.from_np(v.dtype), kind="ExternalInput").ap() for k, v in feeds.items()}
    io["out"] = nc.dram_tensor("out", (D, T), F32, kind="ExternalOutput").ap()
    build(nc, io)
    r = run_bass_kernel_spmd(nc, [{f"in_{k}": v for k, v in feeds.items()}], core_ids=[0])
    return np.ascontiguousarray(r.results[0]["out"].T)[None]
```
